# Optimizing a Trainium2 kernel written in Bass

```python
import math
import jax, jax.numpy as jnp
from jax import lax
import numpy as np

D_MODEL = 1024
BATCH = 1
SEQ = 2048
DEPTH = 1

N_MIXERS = 2
NORM_EPS = 1e-6

GLA_HEADS = 4
GLA_DK = D_MODEL // 2
GLA_DV = D_MODEL
GLA_DK_HEAD = GLA_DK // GLA_HEADS
GLA_DV_HEAD = GLA_DV // GLA_HEADS
GLA_RANK = 16
GLA_TAU = 16.0
GLA_CHUNK = 64
GLA_IN = 2 * GLA_DK + GLA_DV + GLA_RANK + GLA_DV

DSW_HEADS = 16
DSW_HEAD_DIM = D_MODEL // DSW_HEADS
DSW_WIDTH = DSW_HEADS * DSW_HEAD_DIM
DSW_GROUPS = ((128, 1), (512, 4), (2048, 16))
N_GROUPS = len(DSW_GROUPS)
DSW_IN = N_GROUPS * 3 * DSW_WIDTH + DSW_WIDTH

REL_BUCKETS = 32
REL_MAX_DIST = 2048


def rmsnorm(x, g):
    x32 = x.astype(jnp.float32)
    y = x32 * lax.rsqrt(jnp.mean(x32 * x32, axis=-1, keepdims=True) + NORM_EPS)
    return y.astype(x.dtype) * g

def t5_causal_bucket(n):
    max_exact = REL_BUCKETS // 2
    nf = np.maximum(n, 1).astype(np.float32)
    large = max_exact + (np.log(nf / max_exact) / math.log(REL_MAX_DIST / max_exact)
                         * (REL_BUCKETS - max_exact)).astype(np.int32)
    large = np.minimum(large, REL_BUCKETS - 1)
    return np.where(n < max_exact, n, large).astype(np.int32)

def gla_mixer(h, w_in, w_alpha, b_alpha, norm_g, w_out):
    B, S, _ = h.shape
    H, dk, dv, C = GLA_HEADS, GLA_DK_HEAD, GLA_DV_HEAD, GLA_CHUNK
    nc = S // C
    proj = h @ w_in
    q, k, v, g_lr, r = jnp.split(
        proj, [GLA_DK, 2 * GLA_DK, 2 * GLA_DK + GLA_DV, 2 * GLA_DK + GLA_DV + GLA_RANK], axis=-1)
    log_a = jax.nn.log_sigmoid((g_lr @ w_alpha + b_alpha).astype(jnp.float32)) / GLA_TAU

    def chunks(t, d):
        return t.astype(jnp.float32).reshape(B, nc, C, H, d).transpose(0, 3, 1, 2, 4)

    q = chunks(q, dk) * (dk ** -0.5)
    k = chunks(k, dk)
    v = chunks(v, dv)
    b = jnp.cumsum(chunks(log_a, dk), axis=3)

    mid = b[:, :, :, C // 2:C // 2 + 1]
    a_intra = jnp.einsum('bhnid,bhnjd->bhnij', q * jnp.exp(b - mid), k * jnp.exp(mid - b))
    causal = jnp.tril(jnp.ones((C, C), dtype=bool))
    a_intra = jnp.where(causal, a_intra, 0.0)
    o = jnp.einsum('bhnij,bhnje->bhnie', a_intra, v)

    b_last = b[:, :, :, -1:]
    kv = jnp.einsum('bhnjd,bhnje->bhnde', k * jnp.exp(b_last - b), v)
    decay = jnp.exp(b_last[:, :, :, 0])

    def step(state, inp):
        dec, kv_n = inp
        return dec[..., None] * state + kv_n, state

    _, states = lax.scan(step, jnp.zeros((B, H, dk, dv), jnp.float32),
                         (decay.transpose(2, 0, 1, 3), kv.transpose(2, 0, 1, 3, 4)))
    o = o + jnp.einsum('bhnid,nbhde->bhnie', q * jnp.exp(b), states)

    o = o.transpose(0, 2, 3, 1, 4).reshape(B, S, H, dv)
    o = rmsnorm(o, norm_g)
    o = o.reshape(B, S, GLA_DV).astype(h.dtype) * jax.nn.silu(r)
    return o @ w_out

def dilated_group_attn(q, k, v, rel_bias, window, dil):
    B, S, H, Dh = q.shape
    span = window // dil
    L = S // dil
    nb = -(-L // span)
    Lp = nb * span

    def to_sub(t):
        t = t.reshape(B, L, dil, H, Dh).transpose(0, 2, 3, 1, 4)
        return jnp.pad(t, ((0, 0), (0, 0), (0, 0), (0, Lp - L), (0, 0)))

    def banded(t):
        tp = jnp.pad(to_sub(t), ((0, 0), (0, 0), (0, 0), (span, 0), (0, 0)))
        prev = tp[:, :, :, :Lp].reshape(B, dil, H, nb, span, Dh)
        cur = tp[:, :, :, span:].reshape(B, dil, H, nb, span, Dh)
        return jnp.concatenate([prev, cur], axis=-2)

    qs = to_sub(q).reshape(B, dil, H, nb, span, Dh)
    kb, vb = banded(k), banded(v)

    qi = np.arange(span)[:, None]
    kj = np.arange(2 * span)[None, :]
    steps = qi + span - kj
    in_window = (steps >= 0) & (steps <= span)
    bucket = t5_causal_bucket(np.clip(steps, 0, span) * dil)
    bias = rel_bias[bucket].transpose(2, 0, 1).astype(jnp.float32)
    first_block = (np.arange(nb) == 0)[:, None, None]
    mask = in_window[None] & (~first_block | (kj >= span)[None])

    logits = jnp.einsum('bdhnqe,bdhnke->bdhnqk', qs, kb).astype(jnp.float32) * (Dh ** -0.5)
    logits = jnp.where(mask, logits + bias[:, None], -jnp.inf)
    lse = jax.nn.logsumexp(logits, axis=-1)
    p = jnp.exp(logits - lse[..., None])
    o = jnp.einsum('bdhnqk,bdhnke->bdhnqe', p.astype(vb.dtype), vb)

    o = o.reshape(B, dil, H, Lp, Dh)[:, :, :, :L].transpose(0, 3, 1, 2, 4).reshape(B, S, H, Dh)
    lse = lse.reshape(B, dil, H, Lp)[:, :, :, :L].transpose(0, 3, 1, 2).reshape(B, S, H)
    return o, lse

def dilated_mixer(h, w_in, w_out, rel_bias):
    B, S, _ = h.shape
    proj = h @ w_in
    qkv = proj[..., :N_GROUPS * 3 * DSW_WIDTH].reshape(B, S, N_GROUPS, 3, DSW_HEADS, DSW_HEAD_DIM)
    gate = proj[..., N_GROUPS * 3 * DSW_WIDTH:]
    outs, lses = [], []
    for g, (window, dil) in enumerate(DSW_GROUPS):
        o, lse = dilated_group_attn(qkv[:, :, g, 0], qkv[:, :, g, 1], qkv[:, :, g, 2],
                                    rel_bias, window, dil)
        outs.append(o)
        lses.append(lse)
    w = jax.nn.softmax(jnp.stack(lses, axis=0), axis=0)
    o = jnp.sum(w[..., None] * jnp.stack(outs, axis=0).astype(jnp.float32), axis=0)
    o = o.reshape(B, S, DSW_WIDTH).astype(h.dtype) * jax.nn.silu(gate)
    return o @ w_out

def first_inputs(seed: int = 0) -> dict:
    key = jax.random.key(seed)
    ks = jax.random.split(key, 16)
    n_gla = (DEPTH + N_MIXERS - 1) // N_MIXERS
    n_dsw = DEPTH // N_MIXERS
    nrm = jax.random.normal
    f32 = jnp.float32
    return {
        "x": nrm(ks[0], (BATCH, SEQ, D_MODEL), f32),
        "c": nrm(ks[1], (BATCH, D_MODEL), f32),
        "ada_w": nrm(ks[2], (DEPTH, D_MODEL, 3 * D_MODEL), f32) * D_MODEL ** -0.5,
        "ada_b": nrm(ks[3], (DEPTH, 3 * D_MODEL), f32) * 0.02,
        "norm_g": 1.0 + 0.05 * nrm(ks[4], (DEPTH, D_MODEL), f32),
        "gla_w_in": nrm(ks[5], (n_gla, D_MODEL, GLA_IN), f32) * D_MODEL ** -0.5,
        "gla_w_alpha": nrm(ks[6], (n_gla, GLA_RANK, GLA_DK), f32) * GLA_RANK ** -0.5,
        "gla_b_alpha": nrm(ks[7], (n_gla, GLA_DK), f32) * 0.1,
        "gla_norm_g": 1.0 + 0.05 * nrm(ks[8], (n_gla, GLA_DV_HEAD), f32),
        "gla_w_out": nrm(ks[9], (n_gla, GLA_DV, D_MODEL), f32) * GLA_DV ** -0.5,
        "dsw_w_in": nrm(ks[10], (n_dsw, D_MODEL, DSW_IN), f32) * D_MODEL ** -0.5,
        "dsw_w_out": nrm(ks[11], (n_dsw, DSW_WIDTH, D_MODEL), f32) * DSW_WIDTH ** -0.5,
        "rel_bias": nrm(ks[12], (REL_BUCKETS, DSW_HEADS), f32) * 0.5,
        "final_g": 1.0 + 0.05 * nrm(ks[13], (D_MODEL,), f32),
    }

def first_block(x, c, ada_w, ada_b, norm_g, gla_w_in, gla_w_alpha, gla_b_alpha, gla_norm_g,
              gla_w_out, dsw_w_in, dsw_w_out, rel_bias, final_g):
    c_act = jax.nn.silu(c)
    for i in range(DEPTH):
        mod = c_act @ ada_w[i] + ada_b[i]
        shift, scale, gate = jnp.split(mod, 3, axis=-1)
        h = rmsnorm(x, norm_g[i]) * (1.0 + scale[:, None]) + shift[:, None]
        j = i // N_MIXERS
        if i % N_MIXERS == 0:
            y = gla_mixer(h, gla_w_in[j], gla_w_alpha[j], gla_b_alpha[j], gla_norm_g[j], gla_w_out[j])
        else:
            y = dilated_mixer(h, dsw_w_in[j], dsw_w_out[j], rel_bias)
        x = x + gate[:, None] * y
    return rmsnorm(x, final_g)


D_MIX = D_MODEL
M_HEADS = 4
M_DH = 96
M_W = M_HEADS * M_DH
M_CHUNK = 64
M_CONV = 4
A_HEADS = 6
A_KV = 2
A_DH = 64
A_W = A_HEADS * A_DH
A_KVW = A_KV * A_DH
WINDOW = 128
S_HEADS = 4
S_DH = 64
S_W = S_HEADS * S_DH
S_BLOCK = 128
EPS = 1e-6

SPLITS = (M_W, M_W, M_HEADS, M_HEADS, M_W,
          A_W, A_KVW, A_KVW, A_W,
          S_W, S_W, S_W, S_W)
N_IN = int(sum(SPLITS))
OFFSETS = tuple(int(o) for o in np.cumsum(SPLITS)[:-1])


def rmsnorm_2(x, g):
    xf = x.astype(jnp.float32)
    y = xf * lax.rsqrt(jnp.mean(xf * xf, axis=-1, keepdims=True) + EPS)
    return (y * g.astype(jnp.float32)).astype(x.dtype)

def alibi_slopes():
    return jnp.asarray(2.0 ** (-8.0 * np.arange(1, A_HEADS + 1) / A_HEADS), dtype=jnp.float32)

def causal_conv(u, w, b):
    C = u.shape[-1]
    out = lax.conv_general_dilated(u, w.reshape(M_CONV, 1, C).astype(u.dtype), window_strides=(1,),
                                   padding=[(M_CONV - 1, 0)], dimension_numbers=('NWC', 'WIO', 'NWC'),
                                   feature_group_count=C)
    return out + b

def mlstm_branch(u, v, i_pre, f_pre, conv_w, conv_b, wq, wk, b_i, b_f, hn_g, skip):
    B, S, _ = u.shape
    f32 = jnp.float32
    cu = jax.nn.silu(causal_conv(u, conv_w, conv_b))
    ch = cu.reshape(B, S, M_HEADS, M_DH)
    q = jnp.einsum('bshd,hde->bhse', ch, wq).astype(f32) * (M_DH ** -0.5)
    k = jnp.einsum('bshd,hde->bhse', ch, wk).astype(f32)
    vh = v.reshape(B, S, M_HEADS, M_DH).transpose(0, 2, 1, 3).astype(f32)
    log_i = (i_pre + b_i).astype(f32).transpose(0, 2, 1)
    log_f = jax.nn.log_sigmoid((f_pre + b_f).astype(f32)).transpose(0, 2, 1)
    nc = S // M_CHUNK

    def chunks(t):
        return jnp.moveaxis(t.reshape(B, M_HEADS, nc, M_CHUNK, *t.shape[3:]), 2, 0)

    causal = jnp.tril(jnp.ones((M_CHUNK, M_CHUNK), dtype=bool))

    def step(carry, inp):
        C, n, m = carry
        qb, kb, vb, li, lf = inp
        b = jnp.cumsum(lf, axis=-1)
        g = b[..., -1]
        dmat = jnp.where(causal, b[..., :, None] - b[..., None, :] + li[..., None, :], -jnp.inf)
        inter = b + m[..., None]
        m_t = jnp.maximum(inter, jnp.max(dmat, axis=-1))
        w_inter = jnp.exp(inter - m_t)
        s = jnp.einsum('bhtd,bhsd->bhts', qb, kb) * jnp.exp(dmat - m_t[..., None])
        num = w_inter[..., None] * jnp.einsum('bhed,bhtd->bhte', C, qb) + jnp.einsum('bhts,bhse->bhte', s, vb)
        den = w_inter * jnp.einsum('bhd,bhtd->bht', n, qb) + jnp.sum(s, axis=-1)
        h = num / jnp.maximum(jnp.abs(den), jnp.exp(-m_t))[..., None]
        decay_s = g[..., None] - b + li
        m_next = jnp.maximum(g + m, jnp.max(decay_s, axis=-1))
        ws = jnp.exp(decay_s - m_next[..., None])
        carry_scale = jnp.exp(g + m - m_next)
        C_next = carry_scale[..., None, None] * C + jnp.einsum('bhs,bhse,bhsd->bhed', ws, vb, kb)
        n_next = carry_scale[..., None] * n + jnp.einsum('bhs,bhsd->bhd', ws, kb)
        return (C_next, n_next, m_next), h

    init = (jnp.zeros((B, M_HEADS, M_DH, M_DH), f32), jnp.zeros((B, M_HEADS, M_DH), f32),
            jnp.zeros((B, M_HEADS), f32))
    _, hs = lax.scan(step, init, (chunks(q), chunks(k), chunks(vh), chunks(log_i), chunks(log_f)))
    h = jnp.moveaxis(hs, 0, 2).reshape(B, M_HEADS, S, M_DH).transpose(0, 2, 1, 3)
    h = h * lax.rsqrt(jnp.mean(h * h, axis=-1, keepdims=True) + EPS)
    h = h.reshape(B, S, M_W) * hn_g.astype(f32)
    return (h + skip.astype(f32) * cu.astype(f32)).astype(u.dtype)

def swa_branch(q, k, v, sinks):
    B, S, _ = q.shape
    nb = S // WINDOW
    G = A_HEADS // A_KV
    qb = q.reshape(B, nb, WINDOW, A_KV, G, A_DH)
    kh = k.reshape(B, nb, WINDOW, A_KV, A_DH)
    vh = v.reshape(B, nb, WINDOW, A_KV, A_DH)
    pad = jnp.zeros_like(kh[:, :1])
    kk = jnp.concatenate([jnp.concatenate([pad, kh[:, :-1]], 1), kh], 2)
    vv = jnp.concatenate([jnp.concatenate([pad, vh[:, :-1]], 1), vh], 2)
    scores = jnp.einsum('bnqkgd,bnskd->bnkgqs', qb, kk).astype(jnp.float32) * (A_DH ** -0.5)
    qi = jnp.arange(WINDOW)[:, None]
    si = jnp.arange(2 * WINDOW)[None, :]
    rel = WINDOW + qi - si
    band = (rel >= 0) & (rel < WINDOW)
    valid = band[None] & ((jnp.arange(nb)[:, None, None] - 1) * WINDOW + si[None] >= 0)
    alibi = -alibi_slopes().reshape(A_KV, G)[:, :, None, None] * rel.astype(jnp.float32)
    scores = jnp.where(valid[None, :, None, None], scores + alibi[None, None], -jnp.inf)
    sink = jnp.broadcast_to(sinks.astype(jnp.float32).reshape(A_KV, G)[None, None, :, :, None, None],
                            scores.shape[:-1] + (1,))
    probs = jax.nn.softmax(jnp.concatenate([scores, sink], axis=-1), axis=-1)[..., :-1]
    out = jnp.einsum('bnkgqs,bnskd->bnqkgd', probs.astype(v.dtype), vv)
    return out.reshape(B, S, A_W)

def stickbreak_branch(q, k, v):
    B, S, _ = q.shape
    nb = S // S_BLOCK
    qh = q.reshape(B, nb, S_BLOCK, S_HEADS, S_DH).transpose(1, 0, 3, 2, 4)
    kh = k.reshape(B, S, S_HEADS, S_DH).transpose(0, 2, 1, 3)
    vh = v.reshape(B, S, S_HEADS, S_DH).transpose(0, 2, 1, 3)
    kpos = jnp.arange(S)

    def block(args):
        qb, n = args
        z = jnp.einsum('bhqd,bhsd->bhqs', qb, kh).astype(jnp.float32) * (S_DH ** -0.5)
        tpos = n * S_BLOCK + jnp.arange(S_BLOCK)
        strict = kpos[None, :] < tpos[:, None]
        log_keep = jnp.where(strict, jax.nn.log_sigmoid(-z), 0.0)
        suffix = lax.cumsum(log_keep, axis=log_keep.ndim - 1, reverse=True) - log_keep
        a = jnp.where(strict, jnp.exp(jax.nn.log_sigmoid(z) + suffix), 0.0)
        return jnp.einsum('bhqs,bhsd->bhqd', a.astype(vh.dtype), vh)

    out = lax.map(block, (qh, jnp.arange(nb)))
    return out.transpose(1, 0, 3, 2, 4).reshape(B, S, S_W)

def hybrid_layer(x, c_act, w_mod, b_mod, g_pre, g_post, w_in, m_conv_w, m_conv_b, m_wq, m_wk,
                 m_b_i, m_b_f, m_norm_g, m_skip, a_sinks, w_out):
    mod = c_act @ w_mod + b_mod
    shift, scale, gate = jnp.split(mod, 3, axis=-1)
    h = rmsnorm_2(x, g_pre) * (1.0 + scale[:, None]) + shift[:, None]
    proj = h @ w_in
    (mu, mv, mi, mf, mz, aq, ak, av, az, sq, sk, sv, sz) = jnp.split(proj, OFFSETS, axis=-1)
    y_m = mlstm_branch(mu, mv, mi, mf, m_conv_w, m_conv_b, m_wq, m_wk, m_b_i, m_b_f, m_norm_g, m_skip) * jax.nn.silu(mz)
    y_a = swa_branch(aq, ak, av, a_sinks) * jax.nn.silu(az)
    y_s = stickbreak_branch(sq, sk, sv) * jax.nn.silu(sz)
    y = jnp.concatenate([y_m, y_a, y_s], axis=-1) @ w_out
    return x + gate[:, None] * rmsnorm_2(y, g_post)

def second_inputs(seed: int = 0) -> dict:
    key = jax.random.key(seed)
    ks = jax.random.split(key, 20)
    nrm = jax.random.normal
    f32 = jnp.float32
    d = D_MODEL
    return {
        "x": nrm(ks[0], (BATCH, SEQ, d), f32),
        "c": nrm(ks[1], (BATCH, d), f32),
        "w_mod": nrm(ks[2], (DEPTH, d, 3 * d), f32) * (0.5 * d ** -0.5),
        "b_mod": nrm(ks[3], (DEPTH, 3 * d), f32) * 0.02,
        "g_pre": 1.0 + 0.05 * nrm(ks[4], (DEPTH, d), f32),
        "g_post": 1.0 + 0.05 * nrm(ks[5], (DEPTH, d), f32),
        "w_in": nrm(ks[6], (DEPTH, d, N_IN), f32) * d ** -0.5,
        "m_conv_w": nrm(ks[7], (DEPTH, M_CONV, M_W), f32) * M_CONV ** -0.5,
        "m_conv_b": nrm(ks[8], (DEPTH, M_W), f32) * 0.02,
        "m_wq": nrm(ks[9], (DEPTH, M_HEADS, M_DH, M_DH), f32) * M_DH ** -0.5,
        "m_wk": nrm(ks[10], (DEPTH, M_HEADS, M_DH, M_DH), f32) * M_DH ** -0.5,
        "m_b_i": nrm(ks[11], (DEPTH, M_HEADS), f32) * 0.1,
        "m_b_f": 3.0 + 0.5 * nrm(ks[12], (DEPTH, M_HEADS), f32),
        "m_norm_g": 1.0 + 0.05 * nrm(ks[13], (DEPTH, M_W), f32),
        "m_skip": 1.0 + 0.05 * nrm(ks[14], (DEPTH, M_W), f32),
        "a_sinks": nrm(ks[15], (DEPTH, A_HEADS), f32) * 0.5,
        "w_out": nrm(ks[16], (DEPTH, D_MIX, d), f32) * D_MIX ** -0.5,
    }

def second_block(x, c, w_mod, b_mod, g_pre, g_post, w_in, m_conv_w, m_conv_b, m_wq, m_wk,
              m_b_i, m_b_f, m_norm_g, m_skip, a_sinks, w_out):
    c_act = jax.nn.silu(c)
    for l in range(DEPTH):
        x = hybrid_layer(x, c_act, w_mod[l], b_mod[l], g_pre[l], g_post[l], w_in[l], m_conv_w[l], m_conv_b[l],
                         m_wq[l], m_wk[l], m_b_i[l], m_b_f[l], m_norm_g[l], m_skip[l], a_sinks[l], w_out[l])
    return x


def setup_inputs(seed=0):
    out = dict(first_inputs(seed))
    for name, value in second_inputs(seed + 1).items():
        if name != "x":
            out[name + "_2"] = value
    return out


def reference(
    x, c, ada_w, ada_b, norm_g, gla_w_in, gla_w_alpha, gla_b_alpha, gla_norm_g, gla_w_out,
    dsw_w_in, dsw_w_out, rel_bias, final_g, c_2, w_mod_2, b_mod_2, g_pre_2, g_post_2, w_in_2,
    m_conv_w_2, m_conv_b_2, m_wq_2, m_wk_2, m_b_i_2, m_b_f_2, m_norm_g_2, m_skip_2, a_sinks_2,
    w_out_2,
):
    x = first_block(
        x, c, ada_w, ada_b, norm_g, gla_w_in, gla_w_alpha, gla_b_alpha, gla_norm_g, gla_w_out,
        dsw_w_in, dsw_w_out, rel_bias, final_g,
    )
    return second_block(
        x, c_2, w_mod_2, b_mod_2, g_pre_2, g_post_2, w_in_2, m_conv_w_2, m_conv_b_2, m_wq_2,
        m_wk_2, m_b_i_2, m_b_f_2, m_norm_g_2, m_skip_2, a_sinks_2, w_out_2,
    )


_drawn_inputs = setup_inputs


def setup_inputs(seed=0):
    import zlib

    import numpy as np

    out = dict(_drawn_inputs(seed))
    spreads = {}
    factors = {'g_post_2': 4.102,
     'm_conv_b_2': 6.072,
     'm_b_i_2': 64.0,
     'm_b_f_2': 24.224,
     'm_norm_g_2': 5.266,
     'm_skip_2': 8.0,
     'a_sinks_2': 25.303}
    for name, (base, spread) in spreads.items():
        noise = np.random.default_rng([zlib.crc32(name.encode()), seed]).standard_normal(out[name].shape)
        drawn = base * np.exp(spread * noise) if base else spread * noise
        out[name] = __import__('jax').numpy.asarray(drawn.astype(out[name].dtype))
    for name, factor in factors.items():
        out[name] = (out[name] * factor).astype(out[name].dtype)
    return out
```

```python
from contextlib import ExitStack

import concourse.bass as bass
from concourse import mybir

ALU = mybir.AluOpType
ACT = mybir.ActivationFunctionType
AX = mybir.AxisListType
F32 = mybir.dt.float32
BF16 = mybir.dt.bfloat16
U32 = mybir.dt.uint32

P = 128
S = 2048
D = 1024
T = 128
NT = S // T
KB = D // P
EPS = 1e-6

GH = 4
GDK = 128
GDV = 256
GR = 16
CH = 64
NC = T // CH
TAU = 16.0
Q0, K0, V0, A0, R0 = 0, GH * GDK, 2 * GH * GDK, 2 * GH * GDK + GH * GDV, 2 * GH * GDK + GH * GDV + GR
GIN = R0 + GH * GDV


class Link:

    def __init__(self, eng, sem, base):
        self.eng, self.sem, self.base, self.n = eng, sem, base, 0

    def done(self, ins):
        self.n += 1
        ins.then_inc(self.sem, 1)
        self.eng.wait_ge(self.sem, self.base + self.n)


def phase_semaphores(nc, ctx, prefix):
    held = []

    def sem(name):
        held.append(nc.alloc_semaphore(prefix + name))
        return held[-1]

    def give_back():
        nc.clear_and_free_semaphores(held)
        nc.all_engine_barrier()

    ctx.callback(give_back)
    return sem


def gla_phase(nc, x, c, ada_w, ada_b, ada_b_cols, norm_g, w_in, w_alpha, b_alpha, norm_h, w_out, final_g, x1):
    with ExitStack() as ctx:
        def sb(name, shape, dt=F32):
            return ctx.enter_context(nc.sbuf_tensor("g_" + name, shape, dt))

        sem = phase_semaphores(nc, ctx, "g_")

        wi_hi, wi_lo = sb("wi_hi", [P, KB, GIN], BF16), sb("wi_lo", [P, KB, GIN], BF16)
        wo_hl = sb("wo_hl", [P, 2, KB, D], BF16)
        wo_hi, wo_lo = wo_hl[:, 0], wo_hl[:, 1]
        acc = wo_hl[:].rearrange("p a k d -> p (a k d)").bitcast(F32)[:, 0:3 * D]
        NS = 4
        stage = sb("stage", [P, NS, GIN])
        arena = stage[:].rearrange("p s n -> p (s n)")
        used = [0]

        def carve(n):
            at = used[0]
            used[0] += n
            assert used[0] <= NS * GIN
            return arena[:, at:at + n]

        def carve3(a, b):
            return carve(a * b).rearrange("p (a b) -> p a b", a=a)

        qT, kT = carve(512), carve(512)
        v_sb = carve(D)
        r_sb, sg = carve(D), carve(D)
        lg, tmp = carve(512), carve(512)
        e_q, e_k, e_l, e_b = carve(512), carve(512), carve(512), carve(512)
        am = carve(512)
        st = [carve3(GH, GDV) for _ in range(NC)]
        og_hi = carve(512).bitcast(BF16)
        klT = carve(512)
        og_lo = klT.bitcast(BF16)
        xo = carve(D)
        xs = sb("xs", [P, 2, D])
        xn = sb("xn", [P, D])
        h_hi, h_lo = sb("h_hi", [P, KB, T], BF16), sb("h_lo", [P, KB, T], BF16)
        gate_row, fin_row, nh_row = sb("gate_row", [P, D]), sb("fin_row", [P, D]), sb("nh_row", [P, GDV])
        ident = sb("ident", [P, P])
        ones = sb("ones", [P, P])
        scan_keep = sb("scan_keep", [P, 512], BF16)
        causal = sb("causal", [P, 512], mybir.dt.uint8)
        causal_f = sb("causal_f", [P, 128])
        wal = sb("wal", [GR, 512])
        glr = sb("glr", [GR, T])
        cols = sb("cols", [P, 96])
        c_col, c_t, c_act = cols[:, 0:8], cols[:, 8:16], cols[:, 16:24]
        ng_col, ab_col, h_scale, h_shift = cols[:, 24:32], cols[:, 32:48], cols[:, 48:56], cols[:, 56:64]
        bal_col, eps_col, one_col = cols[:, 64:68], cols[:, 68:69], cols[:, 69:70]
        ssx, lnx, rsx = cols[:, 70:71], cols[:, 71:72], cols[:, 72:73]
        ssy, lny, rsy = cols[:, 73:74], cols[:, 74:75], cols[:, 75:76]
        sso, lno, rso = cols[:, 76:80], cols[:, 80:84], cols[:, 84:88]
        dec = sb("dec", [P, GH * NC])

        banks = [ctx.enter_context(nc.psum_tensor(f"g_bank{b}", [P, 512], F32)) for b in range(8)]
        G0, G1, TR, A, O0, O1, KV0, KV1 = banks
        O, KV = [O0, O1], [KV0, KV1]

        names = ("consts_in  mod_summed mod_out rows_in consts_ready c_silu w_hi w_lo mod_acc "
                 "x_stat xn_done xT_done hf_done h_hi_done h_lo_done glr_done glr_copied q_done q_copied k_done k_copied "
                 "alpha_done gate_in gate_act lg_done exp_q_done exp_k_done exp_l_done exp_b_done scores_in "
                 "v_done v_copied a_done am_done kl_turned klT_copied r_done r_used kv_done state_done o_done "
                 "o_stat og_done ogT_done og_hi_done og_lo_done y_done y_used x2_done y_stat x1_done x1_out "
                 "silu_ln silu_arg silu_exp r_gained act_link dve_link act_pre dve_pre pool_pre").split()
        s = {n: sem(n) for n in names}
        slot_in = [sem(f"slot_in{n}") for n in range(NS)]
        x_in = [sem(f"x_in{n}") for n in range(2)]
        block = ctx.enter_context(nc.Block())

        NW = 24

        @block.sync
        def _(sp):
            def wait(name, v):
                if not (isinstance(v, int) and v <= 0):
                    sp.wait_ge(s[name], v)

            small = [(c_col, c), (ng_col, norm_g), (ab_col, ada_b_cols), (bal_col, b_alpha),
                     (wal[:], w_alpha[0]), (gate_row[:], ada_b[0, 2 * D:3 * D].partition_broadcast(P)),
                     (fin_row[:], final_g.partition_broadcast(P)), (nh_row[:], norm_h[0].partition_broadcast(P))]
            for dst, src in small:
                sp.dma_start(dst, src).then_inc(s["consts_in"], 16)
            assert len(small) == 8
            for n in range(NW):
                w = (ada_w[0], w_in[0], w_out[0])[n // KB]
                width = w.shape[1]
                kb = n % KB
                if n >= NS:
                    m = n - NS
                    if m < KB:
                        sp.wait_ge(s["mod_acc"], m + 1)
                    else:
                        sp.wait_ge(s["w_lo"], m - KB + 1)
                sp.dma_start(stage[:, n % NS, 0:width], w[kb * P:(kb + 1) * P, :]).then_inc(slot_in[n % NS], 16)
                if n == KB:
                    sp.dma_start(xs[:, 0, :], x[0, 0:T, :]).then_inc(x_in[0], 16)

            def tile(i, par, more=True):
                if more:
                    wait("x2_done", 2 * i)
                    sp.dma_start(xs[:, 1 - par, :], x[0, bass.ds((i + 1) * T, T), :]).then_inc(x_in[1 - par], 16)
                store(i)

            def store(i):
                if isinstance(i, int) and i == 0:
                    return
                wait("x1_done", i)
                sp.dma_start(x1[bass.ds((i - 1) * T, T), :], xo).then_inc(s["x1_out"], 16)

            tile(0, 0)
            with sp.Fori(0, (NT - 2) // 2) as j:
                tile(2 * j + 1, 1)
                tile(2 * j + 2, 0)
            tile(NT - 1, 1, more=False)
            store(NT)
            sp.wait_ge(s["x1_out"], 16 * NT)

        @block.gpsimd
        def _(pool):
            pool.memset(ones[:], 1.0).then_inc(s["pool_pre"], 1)
            pool.memset(ident[:], 0.0).then_inc(s["pool_pre"], 1)
            pool.memset(scan_keep[:], 1.0).then_inc(s["pool_pre"], 1)
            pool.memset(causal_f[:], 1.0).then_inc(s["pool_pre"], 1)
            pool.memset(eps_col, EPS).then_inc(s["pool_pre"], 1)
            pool.memset(one_col, 1.0).then_inc(s["pool_pre"], 1)
            pool.wait_ge(s["pool_pre"], 6)
            pool.affine_select(out=ident[:], in_=ident[:], compare_op=ALU.not_equal, fill=1.0, base=0,
                               pattern=[[-1, P]], channel_multiplier=1).then_inc(s["pool_pre"], 1)
            pool.memset(scan_keep[:].rearrange("p (c t) -> p c t", t=CH)[:, :, 0:1], 0.0).then_inc(s["pool_pre"], 1)
            pool.affine_select(out=causal_f[:], in_=causal_f[:], compare_op=ALU.is_ge, fill=0.0, base=0,
                               pattern=[[1, T]], channel_multiplier=-1).then_inc(s["pool_pre"], 1)
            pool.wait_ge(s["pool_pre"], 9)
            pool.memset(causal_f[0:CH, CH:T], 0.0).then_inc(s["pool_pre"], 1)
            pool.wait_ge(s["pool_pre"], 10)
            for h in range(GH):
                ins = pool.tensor_copy(causal[:, h * T:(h + 1) * T], causal_f[:])
            ins.then_inc(s["consts_ready"], 1)

            def tile(i):
                pool.wait_ge(s["silu_arg"], i + 1)
                pool.tensor_tensor(r_sb.rearrange("p (h e) -> p h e", h=GH), r_sb.rearrange("p (h e) -> p h e", h=GH),
                                   nh_row[:].unsqueeze(1).broadcast_to([P, GH, GDV]), ALU.mult).then_inc(s["r_gained"], 1)

            tile(0)
            with pool.Fori(1, NT) as i:
                tile(i)

        @block.scalar
        def _(act):
            def wait(name, v):
                if not (isinstance(v, int) and v <= 0):
                    act.wait_ge(s[name], v)

            pre = Link(act, s["act_pre"], 0)
            act.preload_act_table_set("natural_log_exp_and_others")
            act.wait_ge(s["consts_ready"], 1)
            act.wait_ge(s["consts_in"], 16 * 8)
            act.activation(c_t, c_col, ACT.Exp, scale=-1.0).then_inc(s["c_silu"], 1)
            for n in range(KB, NW):
                act.wait_ge(slot_in[n % NS], 16 * (n // NS + 1))
                kb = n % KB
                if n == 2 * KB:
                    act.wait_ge(s["mod_out"], 1)
                dst = wi_hi[:, kb, :] if n < 2 * KB else wo_hi[:, kb, :]
                act.activation(dst, stage[:, n % NS, 0:dst.shape[1]], ACT.Copy).then_inc(s["w_hi"], 1)

            def x_stats(i, par, half, link):
                act.wait_ge(x_in[par], 16 * (half + 1))
                link.done(act.activation(r_sb, xs[:, par, :], ACT.Square, accum_out=ssx))
                link.done(act.activation(lnx, ssx, ACT.Ln, scale=1.0 / D, bias=eps_col))
                wait("xn_done", i)
                act.activation(rsx, lnx, ACT.Exp, scale=-0.5).then_inc(s["x_stat"], 1)

            def h_high(i):
                act.wait_ge(s["hf_done"], 2 * (i + 1))
                wait("r_done", 2 * i)
                act.activation(h_hi[:].rearrange("p k t -> p (k t)"), xn[:], ACT.Copy).then_inc(s["h_hi_done"], 1)

            def y_tail(i, link):
                act.wait_ge(s["x2_done"], 2 * (i + 1))
                link.done(act.activation(r_sb, xo, ACT.Square, accum_out=ssy))
                link.done(act.activation(lny, ssy, ACT.Ln, scale=1.0 / D, bias=eps_col))
                wait("x1_done", i)
                act.activation(rsy, lny, ACT.Exp, scale=-0.5).then_inc(s["y_stat"], 1)

            def og_high(i):
                for n, bank in enumerate((TR, G1)):
                    act.wait_ge(s["ogT_done"], 2 * i + n + 1)
                    wait("y_done", 2 * i)
                    act.activation(og_hi[:, n * 512:(n + 1) * 512], bank[:], ACT.Copy).then_inc(s["og_hi_done"], 1)

            ACT_LINKS = 9

            def tile(i, par, half, first=False, last=False):
                link = Link(act, s["act_link"], 0 if first else ACT_LINKS * i - 2)
                act.wait_ge(s["glr_done"], i + 1)
                wait("alpha_done", i)
                act.activation(glr[:], A[0:GR, 0:T], ACT.Copy).then_inc(s["glr_copied"], 1)
                act.wait_ge(s["q_done"], i + 1)
                wait("scores_in", 4 * i)
                act.activation(qT, G0[:], ACT.Copy).then_inc(s["q_copied"], 1)
                act.wait_ge(s["gate_in"], i + 1)
                link.done(act.activation(tmp, lg, ACT.Abs))
                link.done(act.activation(tmp, tmp, ACT.Exp, scale=-1.0))
                act.activation(tmp, tmp, ACT.Ln, bias=one_col).then_inc(s["gate_act"], 1)
                act.wait_ge(s["k_done"], i + 1)
                act.activation(kT, G0[:], ACT.Copy).then_inc(s["k_copied"], 1)
                if not first:
                    og_high(i - 1)
                act.wait_ge(s["lg_done"], i + 1)
                wait("a_done", i)
                act.activation(e_q, tmp, ACT.Exp, scale=1.0 / TAU).then_inc(s["exp_q_done"], 1)
                act.activation(e_k, tmp, ACT.Exp, scale=-1.0 / TAU).then_inc(s["exp_k_done"], 1)
                act.activation(e_l, e_l, ACT.Exp, scale=1.0 / TAU).then_inc(s["exp_l_done"], 1)
                wait("o_done", i)
                act.activation(e_b, lg, ACT.Exp, scale=1.0 / TAU).then_inc(s["exp_b_done"], 1)
                for n, bank in enumerate((G0, G1)):
                    act.wait_ge(s["v_done"], 2 * i + n + 1)
                    act.activation(v_sb[:, n * 512:(n + 1) * 512], bank[:], ACT.Copy).then_inc(s["v_copied"], 1)
                if not first:
                    y_tail(i - 1, link)
                if not last:
                    x_stats(i + 1, 1 - par, half + par, link)
                act.wait_ge(s["kl_turned"], i + 1)
                act.activation(klT, TR[:], ACT.Copy).then_inc(s["klT_copied"], 1)
                for n, bank in enumerate((G0, G1)):
                    act.wait_ge(s["r_done"], 2 * i + n + 1)
                    wait("ogT_done", 2 * i)
                    cs = slice(n * 512, (n + 1) * 512)
                    act.activation(r_sb[:, cs], bank[:], ACT.Copy)
                    act.activation(sg[:, cs], bank[:], ACT.Abs).then_inc(s["r_used"], 1)
                if not last:
                    h_high(i + 1)
                act.wait_ge(s["r_used"], 2 * (i + 1))
                link.done(act.activation(sg, sg, ACT.Exp, scale=-1.0))
                act.activation(sg, sg, ACT.Ln, bias=one_col).then_inc(s["silu_ln"], 1)
                act.wait_ge(s["o_done"], i + 1)
                for h in range(GH):
                    o_h = O[h // 2][:, (h % 2) * GDV:(h % 2 + 1) * GDV]
                    ins = act.activation((qT, kT)[h // 2][:, (h % 2) * GDV:(h % 2 + 1) * GDV], o_h, ACT.Square, accum_out=sso[:, h:h + 1])
                link.done(ins)
                link.done(act.activation(lno, sso, ACT.Ln, scale=1.0 / GDV, bias=eps_col))
                act.activation(rso, lno, ACT.Exp, scale=-0.5).then_inc(s["o_stat"], 1)
                act.wait_ge(s["silu_arg"], i + 1)
                act.activation(sg, sg, ACT.Exp).then_inc(s["silu_exp"], 1)

            act.wait_ge(s["w_lo"], 2 * KB)
            x_stats(0, 0, 0, pre)
            h_high(0)
            tile(0, 0, 0, first=True)
            with act.Fori(0, (NT - 2) // 2) as j:
                tile(2 * j + 1, 1, j)
                tile(2 * j + 2, 0, j + 1)
            tile(NT - 1, 1, NT // 2 - 1, last=True)
            og_high(NT - 1)
            y_tail(NT - 1, Link(act, s["act_link"], ACT_LINKS * NT - 4))

        @block.vector
        def _(dve):
            def wait(name, v):
                if not (isinstance(v, int) and v <= 0):
                    dve.wait_ge(s[name], v)

            pre = Link(dve, s["dve_pre"], 0)
            dve.wait_ge(s["consts_ready"], 1)
            dve.wait_ge(s["consts_in"], 16 * 8)
            dve.wait_ge(s["c_silu"], 1)
            pre.done(dve.tensor_scalar(c_t, c_t, 1.0, None, ALU.add))
            pre.done(dve.reciprocal(c_t, c_t))
            pre.done(dve.tensor_tensor(c_act, c_t, c_col, ALU.mult))
            for kb in range(KB):
                dve.wait_ge(slot_in[kb % NS], 16 * (kb // NS + 1))
                w = stage[:, kb % NS, 0:3 * D]
                if kb == 0:
                    ins = dve.tensor_scalar(acc, w, c_act[:, 0:1], None, ALU.mult)
                else:
                    dve.wait_ge(s["mod_acc"], kb)
                    ins = dve.scalar_tensor_tensor(acc, w, c_act[:, kb:kb + 1], acc, ALU.mult, ALU.add)
                ins.then_inc(s["mod_acc"], 1)

            def low(n):
                kb = n % KB
                hi, lo = (wi_hi, wi_lo) if n < 2 * KB else (wo_hi, wo_lo)
                dve.wait_ge(s["w_hi"], n - KB + 1)
                dve.tensor_tensor(lo[:, kb, :], stage[:, n % NS, 0:hi.shape[-1]], hi[:, kb, :],
                                  ALU.subtract).then_inc(s["w_lo"], 1)

            for n in range(KB, 2 * KB):
                low(n)
            dve.wait_ge(s["mod_summed"], 1)
            pre.done(dve.tensor_tensor(ab_col, ab_col, G0[:, 0:16], ALU.add))
            pre.done(dve.scalar_tensor_tensor(h_scale, ab_col[:, 8:16], 1.0, ng_col, ALU.add, ALU.mult))
            pre.done(dve.tensor_copy(h_shift, ab_col[:, 0:8]))
            for n, bank in enumerate((KV0, KV1)):
                half = slice(n * 512, (n + 1) * 512)
                pre.done(dve.tensor_tensor(gate_row[:, half], gate_row[:, half], bank[:], ALU.add))
            dve.memset(c_t, 0.0).then_inc(s["mod_out"], 1)
            for n in range(2 * KB, NW):
                low(n)
            dve.wait_ge(s["w_lo"], 2 * KB)
            pre.done(dve.memset(am, 0.0))
            pre.done(dve.memset(st[0], 0.0))

            def x_norm(i, par):
                dve.wait_ge(s["x_stat"], i + 1)
                wait("h_lo_done", i)
                wait("h_hi_done", i)
                dve.tensor_scalar(xn[:], xs[:, par, :], rsx, None, ALU.mult).then_inc(s["xn_done"], 1)

            def h_make(i):
                for n, bank in enumerate((TR, G0)):
                    dve.wait_ge(s["xT_done"], 2 * i + n + 1)
                    for m in range(4):
                        kb = 4 * n + m
                        ins = dve.tensor_scalar(xn[:, kb * T:(kb + 1) * T], bank[:, m * T:(m + 1) * T],
                                                h_scale[:, kb:kb + 1], h_shift[:, kb:kb + 1], ALU.mult, ALU.add)
                    ins.then_inc(s["hf_done"], 1)
                dve.wait_ge(s["h_hi_done"], i + 1)
                dve.wait_ge(s["hf_done"], 2 * (i + 1))
                dve.tensor_tensor(h_lo[:].rearrange("p k t -> p (k t)"), xn[:],
                                  h_hi[:].rearrange("p k t -> p (k t)"), ALU.subtract).then_inc(s["h_lo_done"], 1)

            def og_low(i):
                for n, bank in enumerate((TR, G1)):
                    half = slice(n * 512, (n + 1) * 512)
                    dve.wait_ge(s["og_hi_done"], 2 * i + n + 1)
                    dve.tensor_tensor(og_lo[:, half], bank[:], og_hi[:, half], ALU.subtract)\
                       .then_inc(s["og_lo_done"], 1)

            def y_add(i, par, link):
                wait("x1_out", 16 * i)
                for n, bank in enumerate((G1, TR)):
                    half = slice(n * 512, (n + 1) * 512)
                    dve.wait_ge(s["y_done"], 2 * i + n + 1)
                    dve.tensor_tensor(xo[:, half], bank[:], gate_row[:, half], ALU.mult).then_inc(s["y_used"], 1)
                    dve.wait_ge(s["y_used"], 2 * i + n + 1)
                    dve.tensor_tensor(xo[:, half], xo[:, half], xs[:, par, half], ALU.add).then_inc(s["x2_done"], 1)

            def y_norm(i):
                dve.wait_ge(s["y_stat"], i + 1)
                dve.scalar_tensor_tensor(xo, xo, rsy, fin_row[:], ALU.mult, ALU.mult).then_inc(s["x1_done"], 1)

            DVE_LINKS = 4

            def tile(i, par, first=False, last=False):
                link = Link(dve, s["dve_link"], DVE_LINKS * i)
                dve.wait_ge(s["alpha_done"], i + 1)
                wait("exp_b_done", i)
                dve.tensor_tensor(lg.rearrange("p (h t) -> p h t", h=GH), A[:].rearrange("p (h t) -> p h t", h=GH),
                                  bal_col.unsqueeze(2).broadcast_to([P, GH, T]), ALU.add).then_inc(s["gate_in"], 1)
                dve.wait_ge(s["gate_act"], i + 1)
                link.done(dve.scalar_tensor_tensor(tmp, lg, 0.0, tmp, ALU.min, ALU.subtract))
                link.done(dve.tensor_tensor_scan(lg, scan_keep[:], tmp, 0.0, ALU.mult, ALU.add))
                b3 = lg.rearrange("p (c t) -> p c t", t=CH)
                mid = b3[:, :, CH // 2:CH // 2 + 1].broadcast_to([P, GH * NC, CH])
                end = b3[:, :, CH - 1:CH].broadcast_to([P, GH * NC, CH])
                wait("kl_turned", i)
                dve.tensor_tensor(tmp.rearrange("p (c t) -> p c t", t=CH), b3, mid, ALU.subtract)
                dve.tensor_tensor(e_l.rearrange("p (c t) -> p c t", t=CH), end, b3, ALU.subtract)\
                   .then_inc(s["lg_done"], 1)
                if not first:
                    og_low(i - 1)
                qs = GDK ** -0.5
                dve.wait_ge(s["q_copied"], i + 1)
                dve.wait_ge(s["exp_q_done"], i + 1)
                dve.scalar_tensor_tensor(e_q, qT, qs, e_q, ALU.mult, ALU.mult).then_inc(s["scores_in"], 1)
                dve.wait_ge(s["k_copied"], i + 1)
                dve.wait_ge(s["exp_k_done"], i + 1)
                dve.tensor_tensor(e_k, kT, e_k, ALU.mult).then_inc(s["scores_in"], 1)
                dve.wait_ge(s["exp_l_done"], i + 1)
                dve.tensor_tensor(e_l, kT, e_l, ALU.mult).then_inc(s["scores_in"], 1)
                dve.wait_ge(s["exp_b_done"], i + 1)
                link.done(dve.tensor_copy(dec[:].unsqueeze(2), e_b.rearrange("p (c t) -> p c t", t=CH)[:, :, CH - 1:CH]))
                dve.scalar_tensor_tensor(e_b, qT, qs, e_b, ALU.mult, ALU.mult).then_inc(s["scores_in"], 1)
                if not first:
                    y_add(i - 1, 1 - par, link)
                if not last:
                    x_norm(i + 1, 1 - par)
                dve.wait_ge(s["a_done"], i + 1)
                dve.memset(c_t[:, 0:1], 0.0)
                dve.copy_predicated(am, causal[:], A[:]).then_inc(s["am_done"], 1)
                for ch in range(NC):
                    if ch == 1 and not last:
                        h_make(i + 1)
                    dve.wait_ge(s["kv_done"], NC * i + ch + 1)
                    old, new = st[ch], st[(ch + 1) % NC]
                    for h in range(GH):
                        ins = dve.scalar_tensor_tensor(new[:, h, :], old[:, h, :], dec[:, NC * h + ch:NC * h + ch + 1],
                                                       KV[h // 2][:, (h % 2) * GDV:(h % 2 + 1) * GDV],
                                                       ALU.mult, ALU.add)
                    ins.then_inc(s["state_done"], 1)
                    dve.wait_ge(s["state_done"], NC * i + ch + 1)
                dve.wait_ge(s["silu_ln"], i + 1)
                dve.scalar_tensor_tensor(sg, r_sb, 0.0, sg, ALU.min, ALU.subtract).then_inc(s["silu_arg"], 1)
                if not first:
                    y_norm(i - 1)
                dve.wait_ge(s["silu_exp"], i + 1)
                dve.wait_ge(s["r_gained"], i + 1)
                link.done(dve.tensor_tensor(sg, sg, r_sb, ALU.mult))
                dve.wait_ge(s["o_stat"], i + 1)
                for h in range(GH):
                    part = sg[:, h * GDV:(h + 1) * GDV]
                    ins = dve.scalar_tensor_tensor(part, O[h // 2][:, (h % 2) * GDV:(h % 2 + 1) * GDV],
                                                   rso[:, h:h + 1], part, ALU.mult, ALU.mult)
                ins.then_inc(s["og_done"], 1)
                assert link.n == DVE_LINKS, link.n

            x_norm(0, 0)
            h_make(0)
            tile(0, 0, first=True)
            with dve.Fori(0, (NT - 2) // 2) as j:
                tile(2 * j + 1, 1)
                tile(2 * j + 2, 0)
            tile(NT - 1, 1, last=True)
            og_low(NT - 1)
            y_add(NT - 1, 1, None)
            y_norm(NT - 1)

        @block.tensor
        def _(pe):
            def wait(name, v):
                if not (isinstance(v, int) and v <= 0):
                    pe.wait_ge(s[name], v)

            def mm3(out, parts, name):
                n = len(parts)
                for k, (l_hi, l_lo, r_hi, r_lo) in enumerate(parts):
                    pe.matmul(out, l_hi, r_hi, start=(k == 0), stop=False)
                    pe.matmul(out, l_hi, r_lo, start=False, stop=False)
                    ins = pe.matmul(out, l_lo, r_hi, start=False, stop=(k == n - 1))
                if name:
                    ins.then_inc(s[name], 1)

            def by_feature(out, c0, width, name):
                cs = slice(c0, c0 + width)
                mm3(out, [(wi_hi[:, kb, cs], wi_lo[:, kb, cs], h_hi[:, kb, :], h_lo[:, kb, :]) for kb in range(KB)], name)

            def by_token(out, c0, name):
                cs = slice(c0, c0 + 512)
                mm3(out, [(h_hi[:, kb, :], h_lo[:, kb, :], wi_hi[:, kb, cs], wi_lo[:, kb, cs]) for kb in range(KB)], name)

            pe.wait_ge(s["consts_ready"], 1)
            pe.wait_ge(s["mod_acc"], KB)
            for m in range(16):
                pe.matmul(G0[:, m:m + 1], acc[:, m * P:(m + 1) * P], ones[:, 0:1], start=(m == 0), stop=(m == 15),
                          skip_group_check=True)
            for n, bank in enumerate((KV0, KV1)):
                ins = pe.matmul(bank[:], ones[:], acc[:, 2 * D + n * 512:2 * D + (n + 1) * 512], start=True, stop=True)
            ins.then_inc(s["mod_summed"], 1)

            def turn_x(i):
                pe.wait_ge(s["xn_done"], i + 1)
                for n, bank in enumerate((TR, G0)):
                    if n == 0:
                        wait("klT_copied", i)
                    else:
                        wait("r_used", 2 * i - 1)
                    for m in range(4):
                        kb = 4 * n + m
                        ins = pe.transpose(bank[:, m * T:(m + 1) * T], xn[:, kb * P:(kb + 1) * P], ident[:])
                    ins.then_inc(s["xT_done"], 1)

            def turn_og(i):
                pe.wait_ge(s["og_done"], i + 1)
                for n, bank in enumerate((TR, G1)):
                    if n == 1:
                        pe.wait_ge(s["r_used"], 2 * (i + 1))
                    for m in range(4):
                        kb = 4 * n + m
                        ins = pe.transpose(bank[:, m * T:(m + 1) * T], sg[:, kb * P:(kb + 1) * P], ident[:])
                    ins.then_inc(s["ogT_done"], 1)

            def y_products(i):
                for n, bank in enumerate((G1, TR)):
                    pe.wait_ge(s["og_lo_done"], 2 * (i + 1))
                    cs = slice(n * 512, (n + 1) * 512)
                    mm3(bank[:], [(og_hi[:, kb * P:(kb + 1) * P], og_lo[:, kb * P:(kb + 1) * P],
                                   wo_hi[:, kb, cs], wo_lo[:, kb, cs]) for kb in range(KB)], "y_done")

            def tile(i, par, first=False, last=False):
                pe.wait_ge(s["h_lo_done"], i + 1)
                wait("am_done", i)
                by_feature(A[0:GR, 0:T], A0, GR, "glr_done")
                pe.wait_ge(s["hf_done"], 2 * (i + 1))
                for h in range(GH):
                    by_feature(G0[:, h * T:(h + 1) * T], Q0 + h * GDK, GDK, "q_done" if h == GH - 1 else None)
                pe.wait_ge(s["glr_copied"], i + 1)
                for h in range(GH):
                    ins = pe.matmul(A[:, h * T:(h + 1) * T], wal[:, h * GDK:(h + 1) * GDK], glr[:], start=True, stop=True)
                ins.then_inc(s["alpha_done"], 1)
                pe.wait_ge(s["q_copied"], i + 1)
                for h in range(GH):
                    by_feature(G0[:, h * T:(h + 1) * T], K0 + h * GDK, GDK, "k_done" if h == GH - 1 else None)
                if not first:
                    turn_og(i - 1)
                pe.wait_ge(s["k_copied"], i + 1)
                by_token(G0[:], V0, "v_done")
                if not first:
                    y_products(i - 1)
                wait("y_used", 2 * i - 1)
                by_token(G1[:], V0 + 512, "v_done")
                pe.wait_ge(s["scores_in"], 4 * (i + 1))
                pe.wait_ge(s["gate_in"], i + 1)
                for h in range(GH):
                    hs = slice(h * T, (h + 1) * T)
                    ins = pe.matmul(A[:, hs], e_k[:, hs], e_q[:, hs], start=True, stop=True)
                ins.then_inc(s["a_done"], 1)
                wait("y_used", 2 * i)
                for h in range(GH):
                    ins = pe.transpose(TR[:, h * T:(h + 1) * T], e_l[:, h * T:(h + 1) * T], ident[:])
                ins.then_inc(s["kl_turned"], 1)
                pe.wait_ge(s["v_copied"], 2 * i + 1)
                by_token(G0[:], R0, "r_done")

                def kv(ch):
                    pe.wait_ge(s["klT_copied"], i + 1)
                    pe.wait_ge(s["v_copied"], 2 * (i + 1))
                    wait("state_done", NC * i + ch)
                    ts = slice(ch * CH, (ch + 1) * CH)
                    for h in range(GH):
                        ins = pe.matmul(KV[h // 2][:, (h % 2) * GDV:(h % 2 + 1) * GDV], klT[ts, h * GDK:(h + 1) * GDK],
                                        v_sb[ts, h * GDV:(h + 1) * GDV], start=True, stop=True)
                    ins.then_inc(s["kv_done"], 1)

                def o_state(ch):
                    if ch == 0:
                        wait("og_done", i)
                    for h in range(GH):
                        ins = pe.matmul(O[h // 2][ch * CH:(ch + 1) * CH, (h % 2) * GDV:(h % 2 + 1) * GDV],
                                        e_b[:, h * T + ch * CH:h * T + (ch + 1) * CH], st[ch][:, h, :],
                                        start=(h % 2 == 0), stop=False, skip_group_check=True)
                kv(0)
                by_token(G1[:], R0 + 512, "r_done")
                if not last:
                    turn_x(i + 1)
                o_state(0)
                kv(1)
                pe.wait_ge(s["state_done"], NC * i + 1)
                o_state(1)
                pe.wait_ge(s["am_done"], i + 1)
                for h in range(GH):
                    ins = pe.matmul(O[h // 2][:, (h % 2) * GDV:(h % 2 + 1) * GDV], am[:, h * T:(h + 1) * T],
                                    v_sb[:, h * GDV:(h + 1) * GDV], start=False, stop=True, skip_group_check=True)
                ins.then_inc(s["o_done"], 1)

            turn_x(0)
            pe.wait_ge(s["w_lo"], KB)
            tile(0, 0, first=True)
            with pe.Fori(0, (NT - 2) // 2) as j:
                tile(2 * j + 1, 1)
                tile(2 * j + 2, 0)
            tile(NT - 1, 1, last=True)
            turn_og(NT - 1)
            y_products(NT - 1)


MH, MD = 4, 96
MW = MH * MD
TAPS = 4
AH, AKV, AD = 6, 2, 64
AG = AH // AKV
AW = AH * AD
WINDOW = 128
SH, SD = 4, 64
SW = SH * SD
PARTS = [("i", MH), ("f", MH), ("u", MW), ("mz", MW), ("mv", MW), ("av", AKV * AD), ("sv", SW), ("aq", AW),
         ("ak", AKV * AD), ("az", AW), ("sq", SW), ("sk", SW), ("sz", SW)]
C0 = {n: sum(w for _, w in PARTS[:k]) for k, (n, _) in enumerate(PARTS)}
NIN = sum(w for _, w in PARTS)
MASKED = -1e30
SLOPES = [2.0 ** (-8.0 * (h + 1) / AH) for h in range(AH)]


def mix_phase(nc, x1, c, w_mod, b_mod_cols, g_pre, w_in, conv_w, conv_b, wq, wk, b_i, b_f, norm_h, skip, sinks,
              ym_d, ya_d, sqk_d, sv_d, sz_d):
    with ExitStack() as ctx:
        def sb(name, shape, dt=F32):
            return ctx.enter_context(nc.sbuf_tensor("m_" + name, shape, dt))

        w_hi, w_lo = sb("w_hi", [P, KB, NIN], BF16), sb("w_lo", [P, KB, NIN], BF16)
        NS = 3
        SIZE = 24096
        arena = sb("arena", [P, SIZE])
        stage = arena[:, 0:NS * NIN].rearrange("p (s n) -> p s n", s=NS)
        acc = arena[:, NS * NIN:NS * NIN + 2 * D]
        used = [0]

        def carve(n, dt=F32):
            at = used[0]
            used[0] += n if dt == F32 else n // 2
            assert used[0] <= SIZE, used[0]
            v = arena[:, at:used[0]]
            return v if dt == F32 else v.bitcast(dt)

        def carve3(a, b, dt=F32):
            return carve(a * b, dt).rearrange("p (a b) -> p a b", a=a)

        z_sb, e_sb = [carve(1152) for _ in range(2)], carve(1152)
        u_sb = carve3(MH, T + TAPS - 1)
        cv, ec, cu, skc = (carve3(MH, T) for _ in range(4))
        ct = ec
        va, vw = carve3(MH, MD + 1), carve3(MH, MD + 1)
        qT, kT, k_tok = carve3(MH, T), carve3(MH, T), carve3(MH, MD)
        dx = carve3(MH, T)
        C_st = [carve3(MH, MD + 1) for _ in range(NC)]
        nb, hh = carve3(MH, MD + 1), carve3(MH, MD)
        ym = carve3(MH, T)
        ym_hl = carve(2 * MH * T, BF16).rearrange("p (s h t) -> p s h t", s=2, h=MH)
        aq = carve3(AG, T)
        ak, av = carve3(2, T), carve3(2, AKV * AD)
        sc, pt = carve3(AH, 2 * T), carve3(AH, 2 * T)
        oa, ya = carve3(AH, AD), carve(AG * T)
        ya_hl = carve(2 * AG * T, BF16).rearrange("p (s n) -> p s n", s=2)
        sqk, sv = carve(2 * SW), carve(SW)
        rows = carve(10 * T)[0:MH, :].rearrange("p (n t) -> p n t", n=10)
        li, fr, ft, b_r, g_r, m_r, wi_r, ws_r, nm_r, nM_r = (rows[:, n, :] for n in range(10))
        used[0] = max(used[0], NS * NIN + 2 * D)
        xs = carve3(2, D)
        xn = carve(D)
        h_hi, h_lo = carve3(KB, T, BF16), carve3(KB, T, BF16)
        bias = carve3(AH, 2 * T)
        maskneg = sb("maskneg", [P, T])
        ident, ones = sb("ident", [P, P]), sb("ones", [P, 1])
        keep = sb("keep", [MH, T])
        sel = sb("sel", [MH, MH, P])
        wq_sb, wk_sb = sb("wq", [MD, MH, MD]), sb("wk", [MD, MH, MD])
        cols = sb("cols", [P, 176])
        at = [0]

        def col(n):
            at[0] += n
            assert at[0] <= 176
            return cols[:, at[0] - n:at[0]]

        c_col, c_t, c_act, gp_col, b_col, h_scale = col(8), col(8), col(8), col(8), col(16), col(8)
        eps_col, one_col, ssx, lnx, rsx = col(1), col(1), col(1), col(1), col(1)
        cw_col, cb_col, hn_col, sk_col = col(TAPS * MH), col(MH), col(MH), col(MH)
        bi_col, bf_col, m_0, m_1 = col(1), col(1), col(1), col(1)
        g_col, x_col, carry = col(MH), col(3 * MH), col(2 * MH)
        w_col, s_col, n_col = x_col[:, 0:MH], x_col[:, MH:2 * MH], x_col[:, 2 * MH:3 * MH]
        dn, rd, ssh, lnh, rsh = col(MH), col(MH), col(MH), col(MH), col(MH)
        snk, mx, ngm, es, sm, rs_a = (col(AH) for _ in range(6))

        banks = [ctx.enter_context(nc.psum_tensor(f"m_bank{b}", [P, 512], F32)) for b in range(8)]
        G0, G1, TR, B3, B4, B5, B6, B7 = banks

        names = ("consts_in pool_pre consts_ready c_silu w_hi w_lo mod_acc mod_summed mod_out tiles_free "
                 "x_stat xn_done xT_done hf_done h_hi_done h_lo_done "
                 "gates_done gates_read gate_abs u_done u_copied mz_done mz_read aqk_done aqk_copied tv_done tv_copied "
                 "cols_done neg_max_done cols_exp az_done az_read qk_done qk_copied ktok_copied sqk_done sqk_copied "
                 "qk_scores dx_arg dx_exp dx_done kv_done state_done sz_done sz_read inter_done intra_done "
                 "sv_done sv_copied conv_done conv_link conv_exp cu_done skc_done vw_done num_done h_sq h_done hT_done ym_mid ym_done ym_split "
                 "scores_done hh_done max_done p_done pT_done pT_copied av_done oa_done oT_done ya_done ya_split "
                 "rows_done silu_one silu_rec silu_done ym_out ya_out sqk_out sv_out sz_out dve_pre act_pre dve_link act_link "
                 "head_2_scored").split()
        sem = phase_semaphores(nc, ctx, "m_")
        s = {n: sem(n) for n in names}
        slot_in = [sem(f"slot_in{n}") for n in range(NS)]
        x_in = [sem(f"x_in{n}") for n in range(2)]
        block = ctx.enter_context(nc.Block())

        def by_head(bank):
            return bank[0:MD, :].rearrange("p (h t) -> p h t", h=MH)

        def waiter(eng):
            def wait(name, v):
                if not (isinstance(v, int) and v <= 0):
                    eng.wait_ge(s[name], v)
            return wait

        def all_tiles(eng, tile):
            tile(0, 0, 0, True, False)
            with eng.Fori(0, (NT - 2) // 2) as j:
                tile(2 * j + 1, 1, j, False, False)
                tile(2 * j + 2, 0, j + 1, False, False)
            tile(NT - 1, 1, NT // 2 - 1, False, True)

        @block.sync
        def _(sp):
            wait = waiter(sp)
            small = [(c_col, c), (gp_col, g_pre), (b_col, b_mod_cols), (cw_col[0:MD], conv_w), (cb_col[0:MD], conv_b),
                     (hn_col[0:MD], norm_h), (sk_col[0:MD], skip), (bi_col[0:MH], b_i), (bf_col[0:MH], b_f),
                     (wq_sb[:], wq), (wk_sb[:], wk), (snk, sinks.partition_broadcast(P))]
            for dst, src in small:
                sp.dma_start(dst, src).then_inc(s["consts_in"], 16)
            assert len(small) == 12
            for n in range(2 * KB):
                kb = n % KB
                src = w_mod[0, kb * P:(kb + 1) * P, 0:2 * D] if n < KB else w_in[kb * P:(kb + 1) * P, :]
                if n >= NS:
                    m = n - NS
                    if m < KB:
                        sp.wait_ge(s["mod_acc"], m + 1)
                    else:
                        sp.wait_ge(s["w_lo"], m - KB + 1)
                sp.dma_start(stage[:, n % NS, 0:src.shape[1]], src).then_inc(slot_in[n % NS], 16)
                if n == KB:
                    sp.dma_start(xs[:, 0, :], x1[0:T, :]).then_inc(x_in[0], 16)

            def store_y(i):
                wait("ym_split", 2 * (i + 1))
                sp.dma_start(ym_d[bass.ds(i * MD, MD), :], ym_hl[0:MD].rearrange("p s h t -> p (s h t)"))\
                  .then_inc(s["ym_out"], 16)
                wait("ya_split", 2 * (i + 1))
                sp.dma_start(ya_d[bass.ds(i * P, P), :], ya_hl.rearrange("p s n -> p (s n)")).then_inc(s["ya_out"], 16)

            def tile(i, par, half, first, last):
                if not last:
                    wait("xn_done", i + 1)
                    sp.dma_start(xs[:, 1 - par, :], x1[bass.ds((i + 1) * T, T), :]).then_inc(x_in[1 - par], 16)
                if not first:
                    store_y(i - 1)
                wait("sqk_copied", 2 * (i + 1))
                sp.dma_start(sqk_d[bass.ds(i * P, P), :], sqk).then_inc(s["sqk_out"], 16)
                wait("sv_copied", i + 1)
                sp.dma_start(sv_d[bass.ds(i * P, P), :], sv).then_inc(s["sv_out"], 16)
                wait("silu_done", i + 1)
                sp.dma_start(sz_d[bass.ds(i * P, P), :], z_sb[par][:, 896:1152]).then_inc(s["sz_out"], 16)

            all_tiles(sp, tile)
            store_y(NT - 1)
            for n in ("ym_out", "ya_out", "sqk_out", "sv_out", "sz_out"):
                sp.wait_ge(s[n], 16 * NT)

        @block.gpsimd
        def _(pool):
            wait = waiter(pool)
            n_pre = [0]

            def pre(ins):
                n_pre[0] += 1
                ins.then_inc(s["pool_pre"], 1)
                pool.wait_ge(s["pool_pre"], n_pre[0])

            pre(pool.memset(ones[:], 1.0))
            pre(pool.memset(eps_col, EPS))
            pre(pool.memset(one_col, 1.0))
            pre(pool.memset(ident[:], 0.0))
            pre(pool.affine_select(out=ident[:], in_=ident[:], compare_op=ALU.not_equal, fill=1.0, base=0,
                                   pattern=[[-1, P]], channel_multiplier=1))
            pre(pool.memset(keep[:], 1.0))
            pre(pool.memset(keep[:].rearrange("p (c t) -> p c t", t=CH)[:, :, 0:1], 0.0))
            pre(pool.memset(sel[:], 0.0))
            pre(pool.affine_select(out=sel[:], in_=sel[:], compare_op=ALU.not_equal, fill=1.0, base=0,
                                   pattern=[[-1, MH], [0, P]], channel_multiplier=1))
            pre(pool.memset(maskneg[:], 0.0))
            pre(pool.affine_select(out=maskneg[:], in_=maskneg[:], compare_op=ALU.is_ge, fill=MASKED, base=0,
                                   pattern=[[1, T]], channel_multiplier=-1))
            pre(pool.memset(maskneg[0:CH, CH:T], MASKED))
            pre(pool.iota(bias[:, 0, :], pattern=[[-1, 2 * T]], base=WINDOW, channel_multiplier=1,
                          allow_small_or_imprecise_dtypes=True))
            for n in reversed(range(AH)):
                pre(pool.tensor_scalar(bias[:, n, :], bias[:, 0, :], -SLOPES[n], None, ALU.mult))
            pre(pool.affine_select(out=bias, in_=bias, compare_op=ALU.is_ge, fill=MASKED, base=WINDOW,
                                   pattern=[[0, AH], [-1, 2 * T]], channel_multiplier=1))
            pre(pool.affine_select(out=bias, in_=bias, compare_op=ALU.is_ge, fill=MASKED, base=-1,
                                   pattern=[[0, AH], [1, 2 * T]], channel_multiplier=-1))
            pool.memset(m_0, 0.0).then_inc(s["consts_ready"], 1)
            pool.wait_ge(s["w_lo"], KB)
            pool.wait_ge(s["mod_out"], 1)
            for v in (u_sb, C_st[0], e_sb, z_sb[0], z_sb[1]):
                pool.memset(v, 0.0)
            pool.memset(va[:, :, MD:MD + 1], 1.0).then_inc(s["tiles_free"], 1)
            pool.wait_ge(s["tiles_free"], 1)

            CONV_LINKS = 8

            def tap(n):
                return cw_col[0:MD, n * MH:(n + 1) * MH].unsqueeze(2).broadcast_to([MD, MH, T])

            def wide(v):
                return v[0:MD].unsqueeze(2).broadcast_to([MD, MH, T])

            def wide1(n):
                return ones[0:MD].unsqueeze(2).broadcast_to([MD, MH, n])

            def split_y(i):
                pool.wait_ge(s["ym_done"], i + 1)
                wait("ym_out", 16 * i)
                pool.tensor_tensor(ym_hl[0:MD, 0], ym[0:MD], wide1(T), ALU.mult).then_inc(s["ym_split"], 1)
                pool.wait_ge(s["ym_split"], 2 * i + 1)
                pool.tensor_tensor(ym_hl[0:MD, 1], ym[0:MD], ym_hl[0:MD, 0], ALU.subtract).then_inc(s["ym_split"], 1)
                pool.wait_ge(s["ya_done"], i + 1)
                wait("ya_out", 16 * i)
                pool.tensor_tensor(ya_hl[:, 0], ya, ones[:].broadcast_to([P, AG * T]), ALU.mult).then_inc(s["ya_split"], 1)
                pool.wait_ge(s["ya_split"], 2 * i + 1)
                pool.tensor_tensor(ya_hl[:, 1], ya, ya_hl[:, 0], ALU.subtract).then_inc(s["ya_split"], 1)

            def tile(i, par, half, first, last):
                n = [CONV_LINKS * i]

                def link(ins):
                    n[0] = n[0] + 1
                    ins.then_inc(s["conv_link"], 1)
                    pool.wait_ge(s["conv_link"], n[0])

                pool.wait_ge(s["u_copied"], i + 1)
                link(pool.tensor_tensor(cv[0:MD], u_sb[0:MD, :, 0:T], tap(0), ALU.mult))
                for k in range(1, TAPS):
                    link(pool.tensor_tensor(ct[0:MD], u_sb[0:MD, :, k:k + T], tap(k), ALU.mult))
                    link(pool.tensor_tensor(cv[0:MD], cv[0:MD], ct[0:MD], ALU.add))
                link(pool.tensor_tensor(u_sb[0:MD, :, 0:TAPS - 1], u_sb[0:MD, :, T:T + TAPS - 1],
                                        wide1(TAPS - 1), ALU.mult))
                pool.tensor_tensor(cv[0:MD], cv[0:MD], wide(cb_col), ALU.add).then_inc(s["conv_done"], 1)
                if not first:
                    split_y(i - 1)
                pool.wait_ge(s["cu_done"], i + 1)
                pool.tensor_tensor(skc[0:MD], cu[0:MD], wide(sk_col), ALU.mult).then_inc(s["skc_done"], 1)
                pool.wait_ge(s["sz_read"], i + 1)
                pool.tensor_tensor(e_sb, e_sb, ones[:].broadcast_to([P, 1152]), ALU.add).then_inc(s["silu_one"], 1)
                pool.wait_ge(s["silu_rec"], i + 1)
                pool.tensor_tensor(z_sb[par], z_sb[par], e_sb, ALU.mult).then_inc(s["silu_done"], 1)

            all_tiles(pool, tile)
            split_y(NT - 1)

        @block.scalar
        def _(act):
            wait = waiter(act)
            pre = Link(act, s["act_pre"], 0)
            act.preload_act_table_set("natural_log_exp_and_others")
            act.wait_ge(s["consts_ready"], 1)
            act.wait_ge(s["consts_in"], 16 * 12)
            act.activation(c_t, c_col, ACT.Exp, scale=-1.0).then_inc(s["c_silu"], 1)
            for n in range(KB, 2 * KB):
                act.wait_ge(slot_in[n % NS], 16 * (n // NS + 1))
                act.activation(w_hi[:, n - KB, :], stage[:, n % NS, :], ACT.Copy).then_inc(s["w_hi"], 1)

            def x_stats(i, par, half, link):
                act.wait_ge(x_in[par], 16 * (half + 1))
                wait("h_lo_done", i)
                wait("h_hi_done", i)
                link.done(act.activation(xn, xs[:, par, :], ACT.Square, accum_out=ssx))
                link.done(act.activation(lnx, ssx, ACT.Ln, scale=1.0 / D, bias=eps_col))
                act.activation(rsx, lnx, ACT.Exp, scale=-0.5).then_inc(s["x_stat"], 1)

            def h_high(i):
                act.wait_ge(s["hf_done"], 2 * (i + 1))
                wait("sv_done", i)
                act.activation(h_hi.rearrange("p k t -> p (k t)"), xn, ACT.Copy).then_inc(s["h_hi_done"], 1)

            def gate_out(name, bank, n, at, i, par):
                act.wait_ge(s[name + "_done"], i + 1)
                act.activation(z_sb[par][0:n, at[0]:at[1]], bank[0:n, 0:at[1] - at[0]], ACT.Copy)
                act.activation(e_sb[0:n, at[0]:at[1]], bank[0:n, 0:at[1] - at[0]], ACT.Exp, scale=-1.0)\
                   .then_inc(s[name + "_read"], 1)

            ACT_LINKS = 6

            def late(i, par):
                for n, bank in enumerate((B3, B4, B5)):
                    act.wait_ge(s["pT_done"], 3 * i + n + 1)
                    act.activation(pt[:, 2 * n:2 * n + 2, :].rearrange("p h s -> p (h s)"), bank[:], ACT.Copy)\
                       .then_inc(s["pT_copied"], 1)

            def late_first(i, par):
                for n, bank in enumerate((B3, B4, B5)):
                    act.wait_ge(s["pT_done"], n + 1)
                    act.activation(pt[:, 2 * n:2 * n + 2, T:2 * T],
                                   bank[:].rearrange("p (h s) -> p h s", h=2)[:, :, T:2 * T], ACT.Copy)\
                       .then_inc(s["pT_copied"], 1)

            def tile(i, par, half, first, last):
                link = Link(act, s["act_link"], ACT_LINKS * i)
                act.wait_ge(s["gates_read"], i + 1)
                link.done(act.activation(ft, fr, ACT.Abs))
                link.done(act.activation(ft, ft, ACT.Exp, scale=-1.0))
                act.activation(ft, ft, ACT.Ln, bias=one_col[0:MH]).then_inc(s["gate_abs"], 1)
                act.wait_ge(s["u_done"], i + 1)
                wait("conv_done", i)
                act.activation(u_sb[0:MD, :, TAPS - 1:], by_head(G0), ACT.Copy).then_inc(s["u_copied"], 1)
                wait("silu_done", i)
                wait("sz_out", 16 * (i - 1) if not first else 0)
                gate_out("mz", G1, MD, (0, 512), i, par)
                if not first:
                    (late_first if isinstance(i, int) and i == 1 else late)(i - 1, 1 - par)
                act.wait_ge(s["aqk_done"], i + 1)
                wait("scores_done", i)
                act.activation(aq.rearrange("p j t -> p (j t)"), G0[:, 0:AG * T], ACT.Copy, scale=AD ** -0.5)
                act.activation(ak[:, par, :], G0[:, AG * T:AG * T + T], ACT.Copy).then_inc(s["aqk_copied"], 1)
                act.wait_ge(s["conv_done"], i + 1)
                wait("cu_done", i)
                act.activation(ec[0:MD], cv[0:MD], ACT.Exp, scale=-1.0).then_inc(s["conv_exp"], 1)
                act.wait_ge(s["tv_done"], i + 1)
                wait("av_done", i)
                act.activation(va[:, :, 0:MD], G1[:, 0:MW].rearrange("p (h e) -> p h e", h=MH), ACT.Copy)
                act.activation(av[:, par, :], G1[:, MW:MW + AKV * AD], ACT.Copy).then_inc(s["tv_copied"], 1)
                act.wait_ge(s["cols_done"], i + 1)
                wait("num_done", i)
                act.activation(g_col, TR[:, 0:MH], ACT.Copy)
                act.activation(x_col, TR[:, MH:4 * MH], ACT.Exp)
                act.activation(carry[0:MD], TR[0:MD, 4 * MH:6 * MH], ACT.Exp).then_inc(s["cols_exp"], 1)
                act.wait_ge(s["dx_arg"], i + 1)
                act.activation(dx, dx, ACT.Exp).then_inc(s["dx_exp"], 1)
                gate_out("az", G0, P, (512, 896), i, par)
                act.wait_ge(s["qk_done"], i + 1)
                act.activation(qT[0:MD], by_head(B3), ACT.Copy, scale=MD ** -0.5)
                act.activation(kT[0:MD], by_head(B4), ACT.Copy).then_inc(s["qk_copied"], 1)
                act.wait_ge(s["sqk_done"], i + 1)
                wait("sqk_out", 16 * i)
                act.activation(sqk[:, 0:SW], G1[:, 0:SW], ACT.Copy, scale=SD ** -0.5).then_inc(s["sqk_copied"], 1)
                act.activation(sqk[:, SW:2 * SW], G1[:, SW:2 * SW], ACT.Copy).then_inc(s["sqk_copied"], 1)
                if not last:
                    x_stats(i + 1, 1 - par, half + par, link)
                gate_out("sz", G0, P, (896, 1152), i, par)
                act.wait_ge(s["sv_done"], i + 1)
                wait("sv_out", 16 * i)
                act.activation(sv, G1[:, 0:SW], ACT.Copy).then_inc(s["sv_copied"], 1)
                if not last:
                    h_high(i + 1)
                act.wait_ge(s["h_sq"], i + 1)
                for h in range(MH):
                    ins = act.activation(dx[:, h, 0:MD], hh[:, h, :], ACT.Square, accum_out=ssh[:, h:h + 1])
                link.done(ins)
                link.done(act.activation(lnh, ssh, ACT.Ln, scale=1.0 / MD, bias=eps_col))
                act.activation(rsh, lnh, ACT.Exp, scale=-0.5).then_inc(s["h_done"], 1)
                act.wait_ge(s["max_done"], i + 1)
                act.activation(es, es, ACT.Exp)
                for n in range(AH):
                    at = sc[:, n, T if first else 0:2 * T]
                    ins = act.activation(at, at, ACT.Exp, bias=ngm[:, n:n + 1], accum_out=sm[:, n:n + 1])
                ins.then_inc(s["p_done"], 1)

            act.wait_ge(s["tiles_free"], 1)
            x_stats(0, 0, 0, pre)
            h_high(0)
            tile(0, 0, 0, True, False)
            tile(1, 1, 0, False, False)
            with act.Fori(1, (NT - 2) // 2) as j:
                tile(2 * j, 0, j, False, False)
                tile(2 * j + 1, 1, j, False, False)
            tile(NT - 2, 0, NT // 2 - 1, False, False)
            tile(NT - 1, 1, NT // 2 - 1, False, True)
            late(NT - 1, 1)

        @block.vector
        def _(dve):
            wait = waiter(dve)
            pre = Link(dve, s["dve_pre"], 0)
            dve.wait_ge(s["consts_ready"], 1)
            dve.wait_ge(s["consts_in"], 16 * 12)
            dve.wait_ge(s["c_silu"], 1)
            pre.done(dve.tensor_scalar(c_t, c_t, 1.0, None, ALU.add))
            pre.done(dve.reciprocal(c_t, c_t))
            pre.done(dve.tensor_tensor(c_act, c_t, c_col, ALU.mult))
            for kb in range(KB):
                dve.wait_ge(slot_in[kb % NS], 16 * (kb // NS + 1))
                w = stage[:, kb % NS, 0:2 * D]
                if kb == 0:
                    ins = dve.tensor_scalar(acc, w, c_act[:, 0:1], None, ALU.mult)
                else:
                    dve.wait_ge(s["mod_acc"], kb)
                    ins = dve.scalar_tensor_tensor(acc, w, c_act[:, kb:kb + 1], acc, ALU.mult, ALU.add)
                ins.then_inc(s["mod_acc"], 1)
            for kb in range(KB):
                dve.wait_ge(s["w_hi"], kb + 1)
                dve.tensor_tensor(w_lo[:, kb, :], stage[:, (KB + kb) % NS, :], w_hi[:, kb, :], ALU.subtract)\
                   .then_inc(s["w_lo"], 1)
            dve.wait_ge(s["mod_summed"], 1)
            pre.done(dve.tensor_tensor(b_col, b_col, G0[:, 0:16], ALU.add))
            dve.scalar_tensor_tensor(h_scale, b_col[:, 8:16], 1.0, gp_col, ALU.add, ALU.mult).then_inc(s["mod_out"], 1)
            dve.wait_ge(s["mod_out"], 1)
            h_shift = b_col[:, 0:8]

            def x_norm(i, par):
                dve.wait_ge(s["x_stat"], i + 1)
                dve.tensor_scalar(xn, xs[:, par, :], rsx, None, ALU.mult).then_inc(s["xn_done"], 1)

            def h_make(i):
                for n, bank in enumerate((TR, G0)):
                    dve.wait_ge(s["xT_done"], 2 * i + n + 1)
                    for m in range(4):
                        kb = 4 * n + m
                        ins = dve.tensor_scalar(xn[:, kb * T:(kb + 1) * T], bank[:, m * T:(m + 1) * T],
                                                h_scale[:, kb:kb + 1], h_shift[:, kb:kb + 1], ALU.mult, ALU.add)
                    ins.then_inc(s["hf_done"], 1)

            def h_low(i):
                dve.wait_ge(s["h_hi_done"], i + 1)
                dve.wait_ge(s["hf_done"], 2 * (i + 1))
                dve.tensor_tensor(h_lo.rearrange("p k t -> p (k t)"), xn, h_hi.rearrange("p k t -> p (k t)"),
                                  ALU.subtract).then_inc(s["h_lo_done"], 1)

            DVE_LINKS = 24

            def heads_out(i, par):
                dve.wait_ge(s["hT_done"], i + 1)
                wait("ym_split", 2 * i)
                for h in range(MH):
                    ins = dve.scalar_tensor_tensor(ym[0:MD, h, :], B7[0:MD, h * T:(h + 1) * T], hn_col[0:MD, h:h + 1],
                                                   skc[0:MD, h, :], ALU.mult, ALU.add)
                ins.then_inc(s["ym_mid"], 1)
                dve.wait_ge(s["ym_mid"], i + 1)
                dve.wait_ge(s["silu_done"], i + 1)
                dve.tensor_tensor(ym[0:MD], ym[0:MD], z_sb[par][0:MD, 0:512].rearrange("p (h t) -> p h t", h=MH),
                                  ALU.mult).then_inc(s["ym_done"], 1)

            def window_norm(i):
                dve.wait_ge(s["av_done"], i + 1)
                dve.tensor_tensor(oa, B6[:, 0:AW].rearrange("p (h e) -> p h e", h=AH),
                                  rs_a.unsqueeze(2).broadcast_to([P, AH, AD]), ALU.mult).then_inc(s["oa_done"], 1)

            def window_out(i, par):
                dve.wait_ge(s["oT_done"], i + 1)
                wait("ya_split", 2 * i)
                dve.tensor_tensor(ya, TR[:, 0:AG * T], z_sb[par][:, 512:896], ALU.mult).then_inc(s["ya_done"], 1)

            def tile(i, par, half, first, last):
                link = Link(dve, s["dve_link"], DVE_LINKS * i)
                dve.wait_ge(s["gates_done"], i + 1)
                dve.tensor_scalar(li, TR[0:MH, 0:T], bi_col[0:MH], None, ALU.add)
                dve.tensor_scalar(fr, TR[0:MH, T:2 * T], bf_col[0:MH], None, ALU.add).then_inc(s["gates_read"], 1)
                dve.wait_ge(s["gate_abs"], i + 1)
                wait("cols_done", i)
                wait("neg_max_done", i)
                link.done(dve.scalar_tensor_tensor(fr, fr, 0.0, ft, ALU.min, ALU.subtract))
                link.done(dve.tensor_tensor_scan(b_r, keep[:], fr, 0.0, ALU.mult, ALU.add))
                link.done(dve.tensor_tensor(g_r, li, b_r, ALU.subtract))
                for ch in range(NC):
                    ts = slice(ch * CH, (ch + 1) * CH)
                    last_t = slice((ch + 1) * CH - 1, (ch + 1) * CH)
                    m_old, m_new = (m_0, m_1) if ch == 0 else (m_1, m_0)
                    link.done(dve.tensor_tensor_scan(m_r[:, ts], g_r[:, ts], g_r[:, ts], m_old[0:MH], ALU.max, ALU.max))
                    link.done(dve.tensor_scalar(wi_r[:, ts], m_r[:, ts], -1.0, m_old[0:MH], ALU.mult, ALU.add))
                    link.done(dve.tensor_scalar(ws_r[:, ts], g_r[:, ts], m_r[:, last_t], None, ALU.subtract))
                    link.done(dve.tensor_tensor(m_new[0:MH], b_r[:, last_t], m_r[:, last_t], ALU.add))
                link.done(dve.scalar_tensor_tensor(nm_r, b_r, -1.0, m_r, ALU.mult, ALU.subtract))
                dve.tensor_scalar(nM_r, m_r, -1.0, None, ALU.mult).then_inc(s["rows_done"], 1)
                if not first:
                    heads_out(i - 1, 1 - par)
                    window_norm(i - 1)
                dve.wait_ge(s["conv_exp"], i + 1)
                wait("skc_done", i)
                wait("qk_done", i)
                link.done(dve.tensor_scalar(ec[0:MD], ec[0:MD], 1.0, None, ALU.add))
                link.done(dve.reciprocal(ec[0:MD], ec[0:MD]))
                dve.tensor_tensor(cu[0:MD], cv[0:MD], ec[0:MD], ALU.mult).then_inc(s["cu_done"], 1)
                dve.wait_ge(s["cols_exp"], i + 1)
                dve.wait_ge(s["neg_max_done"], i + 1)
                wait("h_done", i)
                for h in range(MH):
                    ins = dve.scalar_tensor_tensor(dx[:, h, :], B7[:, h * T:(h + 1) * T], g_col[:, h:h + 1],
                                                   maskneg[:], ALU.add, ALU.min)
                ins.then_inc(s["dx_arg"], 1)
                if not first:
                    window_out(i - 1, 1 - par)
                dve.wait_ge(s["tv_copied"], i + 1)
                wait("kv_done", NC * i)
                dve.tensor_tensor(vw, va, s_col.unsqueeze(2).broadcast_to([P, MH, MD + 1]), ALU.mult)\
                   .then_inc(s["vw_done"], 1)
                dve.wait_ge(s["qk_done"], i + 1)
                dve.tensor_copy(k_tok, B5[:, 0:MW].rearrange("p (h e) -> p h e", h=MH)).then_inc(s["ktok_copied"], 1)
                dve.wait_ge(s["dx_exp"], i + 1)
                dve.wait_ge(s["qk_scores"], i + 1)
                dve.tensor_tensor(dx, B6[:].rearrange("p (h t) -> p h t", h=MH), dx, ALU.mult)\
                   .then_inc(s["dx_done"], 1)
                for ch, bank in enumerate((B3, B5)):
                    dve.wait_ge(s["kv_done"], NC * i + ch + 1)
                    old, new = C_st[ch], C_st[(ch + 1) % NC]
                    for h in range(MH):
                        ins = dve.scalar_tensor_tensor(new[0:MD, h, :], old[0:MD, h, :],
                                                       carry[0:MD, NC * h + ch:NC * h + ch + 1],
                                                       bank[0:MD, h * (MD + 1):(h + 1) * (MD + 1)], ALU.mult, ALU.add)
                    ins.then_inc(s["state_done"], 1)
                    dve.wait_ge(s["state_done"], NC * i + ch + 1)
                    if ch == 0 and not last:
                        x_norm(i + 1, 1 - par)
                if not last:
                    h_make(i + 1)
                dve.wait_ge(s["inter_done"], i + 1)
                wait("hT_done", i)
                link.done(dve.tensor_tensor(nb, B4[:, 0:MH * (MD + 1)].rearrange("p (h e) -> p h e", h=MH),
                                            w_col.unsqueeze(2).broadcast_to([P, MH, MD + 1]), ALU.mult))
                dve.wait_ge(s["intra_done"], i + 1)
                link.done(dve.tensor_tensor(nb, nb, B7[:, 0:MH * (MD + 1)].rearrange("p (h e) -> p h e", h=MH), ALU.add))
                den = nb[:, :, MD:MD + 1].rearrange("p h o -> p (h o)")
                link.done(dve.scalar_tensor_tensor(dn, den, -1.0, den, ALU.mult, ALU.max))
                dve.tensor_tensor(dn, dn, n_col, ALU.max).then_inc(s["num_done"], 1)
                dve.wait_ge(s["num_done"], i + 1)
                link.done(dve.reciprocal(rd, dn))
                dve.tensor_tensor(hh, nb[:, :, 0:MD], rd.unsqueeze(2).broadcast_to([P, MH, MD]), ALU.mult)\
                   .then_inc(s["h_sq"], 1)
                if not last:
                    h_low(i + 1)
                wait("pT_done", 3 * i)
                k0 = T if first else 0
                for n, bank in enumerate((B3, B5, B6)):
                    dve.wait_ge(s["scores_done"], i + 1)
                    ins = dve.tensor_tensor(sc[:, 2 * n:2 * n + 2, k0:2 * T],
                                            bank[:].rearrange("p (h s) -> p h s", h=2)[:, :, k0:2 * T],
                                            bias[:, 2 * n:2 * n + 2, k0:2 * T], ALU.add)
                link.done(ins)
                link.done(dve.tensor_reduce(mx, sc[:, :, k0:2 * T], AX.X, ALU.max))
                link.done(dve.tensor_tensor(mx, mx, snk, ALU.max))
                link.done(dve.tensor_tensor(es, snk, mx, ALU.subtract))
                dve.tensor_scalar(ngm, mx, -1.0, None, ALU.mult).then_inc(s["max_done"], 1)
                dve.wait_ge(s["h_done"], i + 1)
                dve.tensor_tensor(hh, hh, rsh.unsqueeze(2).broadcast_to([P, MH, MD]), ALU.mult)\
                   .then_inc(s["hh_done"], 1)
                dve.wait_ge(s["sz_read"], i + 1)
                dve.wait_ge(s["silu_one"], i + 1)
                dve.reciprocal(e_sb, e_sb).then_inc(s["silu_rec"], 1)
                dve.wait_ge(s["p_done"], i + 1)
                link.done(dve.tensor_tensor(sm, sm, es, ALU.add))
                link.done(dve.reciprocal(rs_a, sm))
                assert link.n == DVE_LINKS, link.n

            x_norm(0, 0)
            h_make(0)
            h_low(0)
            all_tiles(dve, tile)
            heads_out(NT - 1, 1)
            window_norm(NT - 1)
            window_out(NT - 1, 1)

        @block.tensor
        def _(pe):
            wait = waiter(pe)

            def mm3(out, parts, name):
                n = len(parts)
                for k, (l_hi, l_lo, r_hi, r_lo) in enumerate(parts):
                    pe.matmul(out, l_hi, r_hi, start=(k == 0), stop=False)
                    pe.matmul(out, l_hi, r_lo, start=False, stop=False)
                    ins = pe.matmul(out, l_lo, r_hi, start=False, stop=(k == n - 1))
                if name:
                    ins.then_inc(s[name], 1)

            def by_feature(bank, blocks, name):
                for n, (c0, width) in enumerate(blocks):
                    cs = slice(c0, c0 + width)
                    mm3(bank[0:width, n * T:(n + 1) * T],
                        [(w_hi[:, kb, cs], w_lo[:, kb, cs], h_hi[:, kb, :], h_lo[:, kb, :]) for kb in range(KB)],
                        name if n == len(blocks) - 1 else None)

            def by_token(bank, c0, width, name):
                cs = slice(c0, c0 + width)
                mm3(bank[:, 0:width], [(h_hi[:, kb, :], h_lo[:, kb, :], w_hi[:, kb, cs], w_lo[:, kb, cs])
                                       for kb in range(KB)], name)

            pe.wait_ge(s["consts_ready"], 1)
            pe.wait_ge(s["mod_acc"], KB)
            for m in range(16):
                ins = pe.matmul(G0[:, m:m + 1], acc[:, m * P:(m + 1) * P], ones[:, 0:1], start=(m == 0), stop=(m == 15),
                                skip_group_check=True)
            ins.then_inc(s["mod_summed"], 1)
            pe.wait_ge(s["mod_out"], 1)

            def turn_x(i):
                pe.wait_ge(s["xn_done"], i + 1)
                for n, bank in enumerate((TR, G0)):
                    if n == 0:
                        wait("ya_done", i - 1)
                        wait("cols_exp", i)
                    else:
                        wait("sz_read", i)
                    for m in range(4):
                        kb = 4 * n + m
                        ins = pe.transpose(bank[:, m * T:(m + 1) * T], xn[:, kb * P:(kb + 1) * P], ident[:])
                    ins.then_inc(s["xT_done"], 1)

            def turn_p(i, first):
                pe.wait_ge(s["p_done"], i + 1)
                for n, bank in enumerate((B3, B4, B5)):
                    for k in range(4):
                        head, half = 2 * n + k // 2, k % 2
                        if first and half == 0:
                            continue
                        ins = pe.transpose(bank[:, k * T:(k + 1) * T], sc[:, head, half * T:(half + 1) * T], ident[:])
                    ins.then_inc(s["pT_done"], 1)

            def p_times_v(i, par, first):
                pe.wait_ge(s["pT_copied"], 3 * (i + 1))
                for n in range(AH):
                    g = n // AG
                    for half in range(1 if first else 0, 2):
                        slot = par if half else 1 - par
                        ins = pe.matmul(B6[:, n * AD:(n + 1) * AD], pt[:, n, half * T:(half + 1) * T],
                                        av[:, slot, g * AD:(g + 1) * AD], start=(first or half == 0), stop=(half == 1))
                ins.then_inc(s["av_done"], 1)

            def turn_h(i):
                pe.wait_ge(s["hh_done"], i + 1)
                for h in range(MH):
                    ins = pe.transpose(B7[0:MD, h * T:(h + 1) * T], hh[:, h, :], ident[:])
                ins.then_inc(s["hT_done"], 1)

            def turn_o(i):
                pe.wait_ge(s["oa_done"], i + 1)
                flat = oa.rearrange("p h e -> p (h e)")
                for j in range(AG):
                    ins = pe.transpose(TR[:, j * T:(j + 1) * T], flat[:, j * P:(j + 1) * P], ident[:])
                ins.then_inc(s["oT_done"], 1)

            def tile(i, par, half, first, last, second=False):
                pe.wait_ge(s["h_lo_done"], i + 1)
                for n, name in enumerate(("i", "f")):
                    cs = slice(C0[name], C0[name] + MH)
                    mm3(TR[0:MH, n * T:(n + 1) * T], [(w_hi[:, kb, cs], w_lo[:, kb, cs], h_hi[:, kb, :], h_lo[:, kb, :])
                                                      for kb in range(KB)], "gates_done" if n else None)
                pe.wait_ge(s["hf_done"], 2 * (i + 1))
                by_feature(G0, [(C0["u"] + h * MD, MD) for h in range(MH)], "u_done")
                wait("sv_copied", i)
                by_feature(G1, [(C0["mz"] + h * MD, MD) for h in range(MH)], "mz_done")
                if not first:
                    turn_p(i - 1, second)
                pe.wait_ge(s["u_copied"], i + 1)
                by_feature(G0, [(C0["aq"] + n * P, P) for n in range(AG + 1)], "aqk_done")
                if not first:
                    p_times_v(i - 1, 1 - par, second)
                    turn_h(i - 1)
                pe.wait_ge(s["mz_read"], i + 1)
                by_token(G1, C0["mv"], MW + AKV * AD, "tv_done")
                pe.wait_ge(s["rows_done"], i + 1)
                for h in range(MH):
                    pe.matmul(TR[0:MD, 4 * MH + NC * h:4 * MH + NC * (h + 1)], sel[:, h, 0:MD],
                              wi_r[:, CH - 1:T:CH], start=True, stop=True)
                for n, row in enumerate((g_r, wi_r, ws_r, nm_r)):
                    ins = pe.transpose(TR[:, n * MH:(n + 1) * MH], row, ident[0:MH, 0:MH])
                ins.then_inc(s["cols_done"], 1)
                wait("ym_mid", i)
                for h in range(MH):
                    ins = pe.matmul(B7[:, h * T:(h + 1) * T], sel[:, h, :], nM_r, start=True, stop=True)
                ins.then_inc(s["neg_max_done"], 1)
                pe.wait_ge(s["aqk_copied"], i + 1)
                by_feature(G0, [(C0["az"] + n * P, P) for n in range(AG)], "az_done")
                if not first:
                    pe.wait_ge(s["cols_exp"], i + 1)
                    turn_o(i - 1)
                pe.wait_ge(s["cu_done"], i + 1)
                for h in range(MH):
                    hs = slice(h * T, (h + 1) * T)
                    pe.matmul(B3[0:MD, hs], wq_sb[:, h, :], cu[0:MD, h, :], start=True, stop=True)
                    pe.matmul(B4[0:MD, hs], wk_sb[:, h, :], cu[0:MD, h, :], start=True, stop=True)
                    ins = pe.matmul(B5[:, h * MD:(h + 1) * MD], cu[0:MD, h, :], wk_sb[:, h, :], start=True, stop=True)
                ins.then_inc(s["qk_done"], 1)
                pe.wait_ge(s["tv_copied"], i + 1)
                by_feature(G1, [(C0["sq"] + n * P, P) for n in range(4)], "sqk_done")
                pe.wait_ge(s["qk_copied"], i + 1)
                wait("oa_done", i)
                for h in range(MH):
                    ins = pe.matmul(B6[:, h * T:(h + 1) * T], kT[0:MD, h, :], qT[0:MD, h, :], start=True, stop=True)
                ins.then_inc(s["qk_scores"], 1)

                def kv(ch, bank):
                    pe.wait_ge(s["ktok_copied"], i + 1)
                    pe.wait_ge(s["vw_done"], i + 1)
                    ts = slice(ch * CH, (ch + 1) * CH)
                    for h in range(MH):
                        ins = pe.matmul(bank[0:MD, h * (MD + 1):(h + 1) * (MD + 1)], k_tok[ts, h, :], vw[ts, h, :],
                                        start=True, stop=True)
                    ins.then_inc(s["kv_done"], 1)

                def inter(ch):
                    for h in range(MH):
                        ins = pe.matmul(B4[ch * CH:(ch + 1) * CH, h * (MD + 1):(h + 1) * (MD + 1)],
                                        qT[0:MD, h, ch * CH:(ch + 1) * CH], C_st[ch][0:MD, h, :], start=True, stop=True)
                    return ins

                kv(0, B3)
                pe.wait_ge(s["az_read"], i + 1)
                by_feature(G0, [(C0["sz"] + n * P, P) for n in range(2)], "sz_done")
                inter(0)
                kv(1, B5)
                pe.wait_ge(s["sqk_copied"], 2 * (i + 1))
                by_token(G1, C0["sv"], SW, "sv_done")
                if not last:
                    turn_x(i + 1)
                pe.wait_ge(s["state_done"], NC * i + 1)
                inter(1).then_inc(s["inter_done"], 1)
                pe.wait_ge(s["dx_done"], i + 1)
                for h in range(MH):
                    ins = pe.matmul(B7[:, h * (MD + 1):(h + 1) * (MD + 1)], dx[:, h, :], va[:, h, :],
                                    start=True, stop=True)
                ins.then_inc(s["intra_done"], 1)
                pe.wait_ge(s["state_done"], NC * (i + 1))
                for head in (0, 1, 2, 4, 5, 3):
                    if head == 3:
                        pe.wait_ge(s["head_2_scored"], i + 1)
                    for half in range(1 if first else 0, 2):
                        slot = par if half else 1 - par
                        g, j = head // AG, head % AG
                        ps = slice(g * AD, (g + 1) * AD)
                        at = (head % 2) * 2 * T + half * T
                        ins = pe.matmul((B3, B5, B6)[head // 2][:, at:at + T], aq[ps, j, :], ak[ps, slot, :],
                                        start=True, stop=True)
                    if head == 2:
                        ins.then_inc(s["head_2_scored"], 1)
                ins.then_inc(s["scores_done"], 1)

            turn_x(0)
            pe.wait_ge(s["w_lo"], KB)
            tile(0, 0, 0, True, False)
            tile(1, 1, 0, False, False, True)
            with pe.Fori(1, (NT - 2) // 2) as j:
                tile(2 * j, 0, j, False, False)
                tile(2 * j + 1, 1, j, False, False)
            tile(NT - 2, 0, NT // 2 - 1, False, False)
            tile(NT - 1, 1, NT // 2 - 1, False, True)
            turn_p(NT - 1, False)
            p_times_v(NT - 1, 1, False)
            turn_h(NT - 1)
            turn_o(NT - 1)


Y_BLOCKS = [MD] * MH + [P] * (AW // P) + [P] * (SW // P)
NY = len(Y_BLOCKS)
T2 = 2 * T
NP2 = S // T2
UNITS = 4


def stick_phase(nc, x1, c, w_mod, b_mod, g_post, w_out, ym_d, ya_d, sqk_d, sv_d, sz_d, out):
    with ExitStack() as ctx:
        def sb(name, shape, dt=F32):
            return ctx.enter_context(nc.sbuf_tensor("s_" + name, shape, dt))

        wo_hi, wo_lo = sb("wo_hi", [P, NY, D], BF16), sb("wo_lo", [P, NY, D], BF16)
        NS = 6
        stage = sb("stage", [P, NS, D])
        acc = sb("acc", [P, D])
        kv_c = sb("kv_c", [P, NT, 2 * SW])
        flat = stage[:].rearrange("p s n -> p (s n)")
        k_st = [flat[:, n * SW:(n + 1) * SW].rearrange("p (b t) -> p b t", b=2) for n in range(2)]
        v_st = [flat[:, (2 + n) * SW:(3 + n) * SW] for n in range(2)]
        lo_at = 4 * SW
        ab = [flat[:, lo_at + n * 512:lo_at + (n + 1) * 512] for n in range(UNITS)]
        lo_at += UNITS * 512
        sp_ = [flat[:, lo_at + n * 512:lo_at + (n + 1) * 512] for n in range(UNITS)]
        lo_at += UNITS * 512
        assert lo_at <= NS * D
        zs = [sb(f"zs{n}", [P, 512]) for n in range(UNITS)]
        hi = [sb(f"hi{n}", [P, 512], BF16) for n in range(UNITS)]
        lo = [sb(f"lo{n}", [P, 512], BF16) for n in range(UNITS)]
        q_sb = [sb(f"q{n}", [P, 2, T2]) for n in range(2)]
        sz_sb = [sb(f"sz{n}", [P, 2, T2]) for n in range(2)]
        ym_sb = [sb(f"ym{n}", [P, 2, 2, MH, T], BF16) for n in range(2)]
        ya_sb = [sb(f"ya{n}", [P, 2, 2, AW // P, T], BF16) for n in range(2)]
        ys, ys_hi, ys_lo = acc[:, 0:512], sb("ys_hi", [P, 2, T2], BF16), sb("ys_lo", [P, 2, T2], BF16)
        xr = sb("xr", [P, 2, D])
        y_sb = sb("y_sb", [P, UNITS, 512])
        junk = [sb(f"junk{n}", [P, 512], BF16) for n in range(UNITS)]
        zero = sb("zero", [P, P], BF16)
        gp_row, g_row = sb("gp_row", [P, D]), sb("g_row", [P, D])
        ones = sb("ones", [P, P])
        tri, unt = sb("tri", [P, P], BF16), sb("unt", [P, P], BF16)
        keep = sb("keep", [P, 2, T2])
        cap = sb("cap", [P, 2, T2])
        cols = sb("cols", [P, 64])
        c_col, c_t, c_act = cols[:, 0:8], cols[:, 8:16], cols[:, 16:24]
        eps_col, one_col = cols[:, 24:25], cols[:, 25:26]
        ssy, sst, lny, rsy = cols[:, 26:30], cols[:, 30:32], cols[:, 32:34], cols[:, 34:36]

        banks = [ctx.enter_context(nc.psum_tensor(f"s_bank{b}", [P, 512], F32)) for b in range(8)]
        Z, C, O, M = banks[0:4], banks[4:6], banks[6], banks[7]

        names = ("consts_in pool_pre consts_ready c_silu w_hi w_lo mod_acc mod_summed row_done kv_in x_in "
                 "k_staged v_staged z_done z_read abs_done ln_done sp_done hi_done lo_done cs_done arg_done a_done av_done "
                 "ys_done ys_hi_done ys_lo_done y_done y_sq y_stat y_used x_out act_pre dve_pre act_link dve_link "
                 "carried masked y_scaled y_read").split()
        sem = phase_semaphores(nc, ctx, "s_")
        s = {n: sem(n) for n in names}
        slot_in = [sem(f"slot_in{n}") for n in range(NS)]
        q_in = [sem(f"q_in{side}") for side in range(2)]
        block = ctx.enter_context(nc.Block())
        NW = KB + NY

        def waiter(eng):
            def wait(name, v):
                if not (isinstance(v, int) and v <= 0):
                    eng.wait_ge(s[name], v)
            return wait

        def all_passes(eng, one_pass):
            def round_(m):
                last = m * -1 + NP2
                one_pass(m, 2 * m, (NP2 + 1) * m, 0, m, (NP2 + 2) * m + 1, last)
                late = m * -1 + (NP2 - 1)
                one_pass(late, 2 * m + 1, (NP2 + 2) * m + 1, 1, late, (NP2 + 1) * m + NP2 + 1, m)
            round_(0)
            with eng.Fori(1, NP2 // 2) as m:
                round_(m)

        def is0(v):
            return isinstance(v, int) and v == 0

        def run_units(eng, stages, nb, inner, beside=None):
            def body(nb, diagonal):
                for k in range(UNITS):
                    for stage_, lag in stages:
                        if k >= lag:
                            stage_(nb, k - lag, diagonal)
                        elif not diagonal:
                            stage_(nb - 1, k - lag + UNITS, False)
                    if diagonal and beside:
                        beside(k)

            body(nb, True)
            if not is0(inner):
                with eng.Fori(0, inner) as r:
                    body(nb + 1 + r, False)

        def drain_units(stages, end):
            for k in range(UNITS, UNITS + max(lag for _, lag in stages)):
                for stage_, lag in stages:
                    if k - lag < UNITS:
                        stage_(end - 1, k - lag, False)

        @block.sync
        def _(sp):
            wait = waiter(sp)
            small = [(c_col, c), (g_row[:], b_mod[0, 2 * D:3 * D].partition_broadcast(P)),
                     (gp_row[:], g_post[0].partition_broadcast(P))]
            for dst, src in small:
                sp.dma_start(dst, src).then_inc(s["consts_in"], 16)
            row = 0
            for n in range(NW):
                if n < KB:
                    src = w_mod[0, n * P:(n + 1) * P, 2 * D:3 * D]
                else:
                    src = w_out[row:row + Y_BLOCKS[n - KB], :]
                    row += Y_BLOCKS[n - KB]
                if n >= NS:
                    m = n - NS
                    if m < KB:
                        sp.wait_ge(s["mod_acc"], m + 1)
                    else:
                        sp.wait_ge(s["w_lo"], m - KB + 1)
                sp.dma_start(stage[0:src.shape[0], n % NS, :], src).then_inc(slot_in[n % NS], 16)
            sp.dma_start(kv_c[:, :, 0:SW], sqk_d.rearrange("(n p) f -> p n f", p=P)[:, :, SW:2 * SW])\
              .then_inc(s["kv_in"], 16)
            sp.dma_start(kv_c[:, :, SW:2 * SW], sv_d.rearrange("(n p) f -> p n f", p=P)).then_inc(s["kv_in"], 16)

            def one_pass(I, n, nb, side, inner, end, last):
                wait("y_used", 4 * (n - 1))
                for tt in range(2):
                    ts = slice(tt * T, (tt + 1) * T)
                    rows = bass.ds((2 * I + tt) * P, P)
                    sp.dma_start(q_sb[side][:, :, ts], sqk_d[rows, 0:SW].rearrange("p (b t) -> p b t", b=2))\
                      .then_inc(q_in[side], 16)
                    sp.dma_start(sz_sb[side][:, :, ts], sz_d[rows, :].rearrange("p (b t) -> p b t", b=2))\
                      .then_inc(q_in[side], 16)
                    sp.dma_start(ym_sb[side][0:MD, tt].rearrange("p s h t -> p (s h t)"),
                                 ym_d[bass.ds((2 * I + tt) * MD, MD), :]).then_inc(q_in[side], 16)
                    sp.dma_start(ya_sb[side][:, tt].rearrange("p s h t -> p (s h t)"), ya_d[rows, :])\
                      .then_inc(q_in[side], 16)
                if not is0(n):
                    store(last, n - 1)
                for tt in range(2):
                    sp.dma_start(xr[:, tt, :], x1[bass.ds((2 * I + tt) * T, T), :]).then_inc(s["x_in"], 16)

            def store(I, n):
                for tt in range(2):
                    sp.wait_ge(s["y_used"], 4 * n + 2 * (tt + 1))
                    sp.dma_start(out[bass.ds((2 * I + tt) * T, T), :], xr[:, tt, :]).then_inc(s["x_out"], 16)
                sp.wait_ge(s["x_out"], 32 * (n + 1))

            all_passes(sp, one_pass)
            store(NP2 // 2, NP2 - 1)
            sp.wait_ge(s["x_out"], 32 * NP2)

        @block.gpsimd
        def _(pool):
            wait = waiter(pool)
            n_pre = [0]

            def pre(ins):
                n_pre[0] += 1
                ins.then_inc(s["pool_pre"], 1)
                pool.wait_ge(s["pool_pre"], n_pre[0])

            pre(pool.memset(ones[:], 1.0))
            pre(pool.memset(eps_col, EPS))
            pre(pool.memset(one_col, 1.0))
            for m, op, b in ((tri, ALU.is_ge, 0), (unt, ALU.is_gt, 0)):
                pre(pool.memset(m[:], 1.0))
                sign = 1 if m is tri else -1
                pre(pool.affine_select(out=m[:], in_=m[:], compare_op=op, fill=0.0, base=b, pattern=[[-sign, P]],
                                       channel_multiplier=sign))
            pre(pool.memset(zero[:], 0.0))
            pre(pool.memset(hi[0][:], 0.0))
            for n in range(2):
                pre(pool.memset(keep[:, n], 1.0))
                pre(pool.affine_select(out=keep[:, n], in_=keep[:, n], compare_op=ALU.is_gt, fill=0.0,
                                       base=-T * (1 - n), pattern=[[1, T2]], channel_multiplier=-1))
                pre(pool.tensor_scalar(cap[:, n], keep[:, n], 0.5, -2.0 * MASKED, ALU.subtract, ALU.mult))
            pool.memset(cols[:, 42:43], 0.0).then_inc(s["consts_ready"], 1)
            pool.wait_ge(s["w_lo"], NY)
            pool.wait_ge(s["kv_in"], 32)

            def carry_wait(n):
                wait("carried", n)
                pool.tensor_tensor(cols[:, 40:41], one_col, one_col, ALU.mult).then_inc(s["carried"], 1)

            def stage_block(kv, nb, slot, j, order):
                if kv == 0:
                    wait("z_done", UNITS * nb - 2 + 2 * slot if not is0(nb) else 0)
                    src, dst, name = kv_c[:, bass.ds(j, 1), 0:SW], k_st[slot].rearrange("p b t -> p (b t)"), "k_staged"
                else:
                    wait("av_done", UNITS * nb - 2 + 2 * slot if not is0(nb) else 0)
                    src, dst, name = kv_c[:, bass.ds(j, 1), SW:2 * SW], v_st[slot], "v_staged"
                carry_wait(4 * nb + order)
                pool.tensor_copy(dst, src.rearrange("p o f -> p (o f)")).then_inc(s[name], 1)

            def high(nb, k):
                pool.wait_ge(s["sp_done"], UNITS * nb + k + 1)
                wait("cs_done", UNITS * nb + k - 1 if not is0(nb) else 0)
                pool.tensor_tensor(hi[k][:], sp_[k], one_col.broadcast_to([P, 512]), ALU.mult).then_inc(s["hi_done"], 1)

            def before(j):
                return nc.s_assert_within(j - 1, 0, NT - 2, skip_runtime_bounds_check_because="a key block before the queries")

            def pair(nb, j_odd):
                stage_block(0, nb, 0, j_odd, 0)
                stage_block(0, nb, 1, before(j_odd), 1)
                high(nb, 0)
                stage_block(1, nb, 0, j_odd, 2)
                high(nb, 1)
                high(nb, 2)
                stage_block(1, nb, 1, before(j_odd), 3)
                high(nb, 3)

            def one_pass(I, n, nb, side, inner, end, last):
                pair(nb, 2 * I + 1)
                if not is0(inner):
                    with pool.Fori(0, inner) as r:
                        pair(nb + 1 + r, nc.s_assert_within(2 * (I - 1 - r) + 1, 1, NT - 3, skip_runtime_bounds_check_because="a key block before the queries"))
                pool.wait_ge(s["ys_done"], n + 1)
                wait("y_done", 4 * n)
                pool.tensor_tensor(ys_hi[:].rearrange("p b t -> p (b t)"), ys, one_col.broadcast_to([P, 512]), ALU.mult).then_inc(s["ys_hi_done"], 1)

            all_passes(pool, one_pass)

        @block.scalar
        def _(act):
            wait = waiter(act)
            act.preload_act_table_set("natural_log_exp_and_others")
            act.wait_ge(s["consts_ready"], 1)
            act.wait_ge(s["consts_in"], 48)
            act.activation(c_t, c_col, ACT.Exp, scale=-1.0).then_inc(s["c_silu"], 1)
            for n in range(KB, NW):
                act.wait_ge(slot_in[n % NS], 16 * (n // NS + 1))
                r = Y_BLOCKS[n - KB]
                act.activation(wo_hi[0:r, n - KB, :], stage[0:r, n % NS, :], ACT.Copy).then_inc(s["w_hi"], 1)

            def z_abs(nb, k, diagonal):
                act.wait_ge(s["z_done"], UNITS * nb + k + 1)
                wait("sp_done", UNITS * (nb - 1) + k + 1 if not is0(nb) else 0)
                act.activation(ab[k], Z[k][:], ACT.Abs).then_inc(s["abs_done"], 1)

            def exp_ln(nb, k, diagonal):
                act.wait_ge(s["abs_done"], UNITS * nb + k + 1)
                act.activation(ab[k], ab[k], ACT.Exp, scale=-1.0).then_inc(s["act_link"], 1)
                act.wait_ge(s["act_link"], UNITS * nb + k + 1)
                act.activation(ab[k], ab[k], ACT.Ln, bias=one_col).then_inc(s["ln_done"], 1)

            def weight(nb, k, diagonal):
                act.wait_ge(s["arg_done"], UNITS * nb + k + 1)
                wait("av_done", UNITS * (nb - 1) + k + 1 if not is0(nb) else 0)
                act.activation(zs[k][:], zs[k][:], ACT.Exp).then_inc(s["a_done"], 1)

            def one_pass(I, n, nb, side, inner, end, last):
                run_units(act, stages, nb, inner, None if is0(n) else lambda k: y_out(n - 1, k))
                drain_units(stages, end)

            stages = [(z_abs, 0), (weight, 3), (exp_ln, 0)]

            def y_out(n, k):
                act.wait_ge(s["y_done"], 4 * n + k + 1)
                wait("y_used", 4 * (n - 1) + k + 1 if not is0(n) else 0)
                act.activation(y_sb[:, k, :], M[:], ACT.Copy).then_inc(s["y_read"], 1)
                act.wait_ge(s["y_read"], 4 * n + k + 1)
                ins = act.activation(junk[k][:], y_sb[:, k, :], ACT.Square, accum_out=ssy[:, k:k + 1])
                if k % 2:
                    tt = k // 2
                    ins.then_inc(s["y_sq"], 1)
                    act.wait_ge(s["dve_link"], 2 * n + tt + 1)
                    act.activation(lny[:, tt:tt + 1], sst[:, tt:tt + 1], ACT.Ln, scale=1.0 / D, bias=eps_col)\
                       .then_inc(s["act_pre"], 1)
                    act.wait_ge(s["act_pre"], 2 * n + tt + 1)
                    act.activation(rsy[:, tt:tt + 1], lny[:, tt:tt + 1], ACT.Exp, scale=-0.5).then_inc(s["y_stat"], 1)

            act.wait_ge(s["w_lo"], NY)
            all_passes(act, one_pass)
            for k in range(UNITS):
                y_out(NP2 - 1, k)

        @block.vector
        def _(dve):
            wait = waiter(dve)
            pre = Link(dve, s["dve_pre"], 0)
            dve.wait_ge(s["consts_ready"], 1)
            dve.wait_ge(s["consts_in"], 48)
            dve.wait_ge(s["c_silu"], 1)
            pre.done(dve.tensor_scalar(c_t, c_t, 1.0, None, ALU.add))
            pre.done(dve.reciprocal(c_t, c_t))
            pre.done(dve.tensor_tensor(c_act, c_t, c_col, ALU.mult))
            for kb in range(KB):
                dve.wait_ge(slot_in[kb % NS], 16 * (kb // NS + 1))
                w = stage[:, kb % NS, :]
                if kb == 0:
                    ins = dve.tensor_scalar(acc[:], w, c_act[:, 0:1], None, ALU.mult)
                else:
                    dve.wait_ge(s["mod_acc"], kb)
                    ins = dve.scalar_tensor_tensor(acc[:], w, c_act[:, kb:kb + 1], acc[:], ALU.mult, ALU.add)
                ins.then_inc(s["mod_acc"], 1)
            for n in range(KB, NW):
                dve.wait_ge(s["w_hi"], n - KB + 1)
                r = Y_BLOCKS[n - KB]
                dve.tensor_tensor(wo_lo[0:r, n - KB, :], stage[0:r, n % NS, :], wo_hi[0:r, n - KB, :], ALU.subtract)\
                   .then_inc(s["w_lo"], 1)
            for n in range(2):
                half = slice(n * 512, (n + 1) * 512)
                dve.wait_ge(s["mod_summed"], n + 1)
                pre.done(dve.tensor_tensor(g_row[:, half], g_row[:, half], (M, O)[n][:], ALU.add))
            dve.tensor_tensor(gp_row[:], gp_row[:], g_row[:], ALU.mult).then_inc(s["row_done"], 1)
            dve.wait_ge(s["row_done"], 1)
            dve.wait_ge(s["w_lo"], NY)

            def heads2(v):
                return v.rearrange("p (h t) -> p h t", h=2)

            def z_copy(nb, k, diagonal):
                dve.wait_ge(s["abs_done"], UNITS * nb + k + 1)
                wait("av_done", UNITS * (nb - 1) + k + 1 if not is0(nb) else 0)
                if diagonal:
                    ins = dve.tensor_tensor(heads2(zs[k][:]), heads2(Z[k][:]),
                                            cap[:, k // 2:k // 2 + 1, :].broadcast_to([P, 2, T2]), ALU.min)
                else:
                    ins = dve.tensor_copy(zs[k][:], Z[k][:])
                ins.then_inc(s["z_read"], 1)

            def softplus(nb, k, diagonal):
                dve.wait_ge(s["ln_done"], UNITS * nb + k + 1)
                dve.wait_ge(s["z_read"], UNITS * nb + k + 1)
                wait("lo_done", UNITS * (nb - 1) + k + 1 if not is0(nb) else 0)
                ins = dve.scalar_tensor_tensor(sp_[k], zs[k][:], 0.0, ab[k], ALU.max, ALU.add)
                if diagonal:
                    ins.then_inc(s["masked"], 1)
                    dve.wait_ge(s["masked"], UNITS * passes[0] + k + 1)
                    ins = dve.tensor_tensor(heads2(sp_[k]), heads2(sp_[k]),
                                            keep[:, k // 2:k // 2 + 1, :].broadcast_to([P, 2, T2]), ALU.mult)
                ins.then_inc(s["sp_done"], 1)

            def low(nb, k, diagonal):
                dve.wait_ge(s["hi_done"], UNITS * nb + k + 1)
                dve.tensor_tensor(lo[k][:], sp_[k], hi[k][:], ALU.subtract).then_inc(s["lo_done"], 1)

            def exponent(nb, k, diagonal):
                dve.wait_ge(s["cs_done"], UNITS * nb + k + 1)
                dve.tensor_tensor(zs[k][:], zs[k][:], C[k % 2][:], ALU.subtract).then_inc(s["arg_done"], 1)

            def one_pass(I, n, nb, side, inner, end, last):
                passes[0] = n
                run_units(dve, stages, nb, inner, None if is0(n) else lambda k: y_scale(n - 1, k))
                drain_units(stages, end)
                dve.wait_ge(s["av_done"], UNITS * end)
                dve.wait_ge(q_in[side], 64 * n + 128 - 64 * side)
                wait("ys_lo_done", n)
                dve.tensor_tensor(ys, O[:], sz_sb[side][:].rearrange("p b t -> p (b t)"), ALU.mult)\
                   .then_inc(s["ys_done"], 1)
                dve.wait_ge(s["ys_hi_done"], n + 1)
                dve.tensor_tensor(ys_lo[:].rearrange("p b t -> p (b t)"), ys, ys_hi[:].rearrange("p b t -> p (b t)"),
                                  ALU.subtract).then_inc(s["ys_lo_done"], 1)

            passes = [0]
            stages = [(exponent, 2), (z_copy, 0), (low, 1), (softplus, 0)]

            def y_scale(n, k):
                if k % 2 == 0:
                    return
                tt = k // 2
                dve.wait_ge(s["y_sq"], 2 * n + tt + 1)
                dve.tensor_tensor(sst[:, tt:tt + 1], ssy[:, 2 * tt:2 * tt + 1], ssy[:, 2 * tt + 1:2 * tt + 2],
                                  ALU.add).then_inc(s["dve_link"], 1)
                dve.wait_ge(s["x_in"], 32 * (n + 1))
                dve.wait_ge(s["y_stat"], 2 * n + tt + 1)
                for h in range(2):
                    half = slice(h * 512, (h + 1) * 512)
                    yt = y_sb[:, 2 * tt + h, :]
                    dve.scalar_tensor_tensor(yt, yt, rsy[:, tt:tt + 1], gp_row[:, half], ALU.mult, ALU.mult)\
                       .then_inc(s["y_scaled"], 1)
                    dve.wait_ge(s["y_scaled"], 4 * n + 2 * tt + h + 1)
                    dve.tensor_tensor(xr[:, tt, half], xr[:, tt, half], yt, ALU.add).then_inc(s["y_used"], 1)

            all_passes(dve, one_pass)
            for k in range(UNITS):
                y_scale(NP2 - 1, k)

        @block.tensor
        def _(pe):
            wait = waiter(pe)
            pe.wait_ge(s["consts_ready"], 1)
            pe.wait_ge(s["mod_acc"], KB)
            for n, bank in enumerate((M, O)):
                pe.matmul(bank[:], ones[:], acc[:, n * 512:(n + 1) * 512], start=True, stop=True)\
                  .then_inc(s["mod_summed"], 1)
            pe.wait_ge(s["row_done"], 1)

            def scores(nb, k, diagonal):
                g = k % 2
                ps = slice(g * SD, (g + 1) * SD)
                pe.wait_ge(s["k_staged"], 2 * nb + k // 2 + 1)
                wait("z_read", UNITS * (nb - 1) + k + 1 if not is0(nb) else 0)
                wait("abs_done", UNITS * (nb - 1) + k + 1 if not is0(nb) else 0)
                for b in range(2):
                    ins = pe.matmul(Z[k][:, b * T2:(b + 1) * T2], k_st[k // 2][ps, b, :], side_q[0][ps, b, :],
                                    start=True, stop=True)
                ins.then_inc(s["z_done"], 1)

            def sums(nb, k, diagonal):
                g = k % 2
                pe.wait_ge(s["lo_done"], UNITS * nb + k + 1)
                start = diagonal and k < 2
                if not start:
                    pk = (k - 2) % UNITS
                    pe.wait_ge(s["arg_done"], UNITS * nb + k - 1)
                    pe.matmul(C[g][:], unt[:], hi[pk][:], start=False, stop=False, skip_group_check=True)
                    pe.matmul(C[g][:], unt[:], lo[pk][:], start=False, stop=False, skip_group_check=True)
                else:
                    wait("arg_done", UNITS * nb)
                pe.matmul(C[g][:], tri[:], hi[k][:], start=start, stop=False, skip_group_check=True)
                pe.matmul(C[g][:], tri[:], lo[k][:], start=False, stop=True, skip_group_check=True)\
                  .then_inc(s["cs_done"], 1)

            def values(nb, k, diagonal):
                g = k % 2
                pe.wait_ge(s["v_staged"], 2 * nb + k // 2 + 1)
                pe.wait_ge(s["a_done"], UNITS * nb + k + 1)
                for b in range(2):
                    h = 2 * b + g
                    ins = pe.matmul(O[g * SD:(g + 1) * SD, b * T2:(b + 1) * T2], v_st[k // 2][:, h * SD:(h + 1) * SD],
                                    zs[k][:, b * T2:(b + 1) * T2], start=False, stop=True,
                                    skip_group_check=True)
                ins.then_inc(s["av_done"], 1)

            side_q = [None]
            stages = [(scores, 0), (sums, 2), (values, 4)]

            def one_pass(I, n, nb, side, inner, end, last):
                side_q[0] = q_sb[side]
                pe.wait_ge(q_in[side], 64 * n + 128 - 64 * side)
                wait("ys_done", n)
                pe.matmul(O[:], zero[:], hi[0][:], start=True, stop=True, skip_group_check=True)
                run_units(pe, stages, nb, inner, None if is0(n) else lambda k: y_products(n - 1, 1 - side, k))
                drain_units(stages, end)

            def y_products(n, side, k):
                pe.wait_ge(s["ys_lo_done"], n + 1)
                wait("y_read", 4 * n + k)
                tt, h = k // 2, k % 2
                ts = slice(tt * T, (tt + 1) * T)
                cs = slice(h * 512, (h + 1) * 512)
                for b in range(NY):
                    r = Y_BLOCKS[b]
                    if b < MH:
                        y_hi, y_lo = (ym_sb[side][0:MD, tt, v, b, :] for v in range(2))
                    elif b < MH + AW // P:
                        y_hi, y_lo = (ya_sb[side][:, tt, v, b - MH, :] for v in range(2))
                    else:
                        y_hi, y_lo = (v[:, b - MH - AW // P, ts] for v in (ys_hi, ys_lo))
                    pe.matmul(M[:], y_hi, wo_hi[0:r, b, cs], start=(b == 0), stop=False)
                    pe.matmul(M[:], y_hi, wo_lo[0:r, b, cs], start=False, stop=False)
                    ins = pe.matmul(M[:], y_lo, wo_hi[0:r, b, cs], start=False, stop=(b == NY - 1))
                ins.then_inc(s["y_done"], 1)

            pe.wait_ge(s["w_lo"], NY)
            all_passes(pe, one_pass)
            for k in range(UNITS):
                y_products(NP2 - 1, 1, k)


def build(nc, a, out):
    def dram(name, shape, dt=F32):
        return nc.dram_tensor(name, shape, dt, kind="Internal").ap()

    x1 = dram("x1", [S, D])
    ym_d, ya_d = dram("ym_d", [NT * MD, 2 * MH * T], BF16), dram("ya_d", [NT * P, 2 * AG * T], BF16)
    sqk_d, sv_d, sz_d = dram("sqk_d", [S, 2 * SW]), dram("sv_d", [S, SW]), dram("sz_d", [S, SW])
    gla_phase(nc, a["x"], a["c_cols"], a["ada_w"], a["ada_b"], a["ada_b_cols"], a["norm_g_cols"], a["gla_w_in"],
              a["gla_w_alpha"], a["gla_b_alpha_cols"], a["gla_norm_g"], a["gla_w_out"], a["final_g"], x1)
    mix_phase(nc, x1, a["c_2_cols"], a["w_mod_2"], a["b_mod_2_cols"], a["g_pre_2_cols"], a["w_in_2"],
              a["m_conv_w_2_cols"], a["m_conv_b_2_cols"], a["m_wq_2"][0].rearrange("h d e -> d h e"),
              a["m_wk_2"][0].rearrange("h d e -> d h e"), a["m_b_i_2_cols"], a["m_b_f_2_cols"], a["m_norm_g_2_cols"],
              a["m_skip_2_cols"], a["a_sinks_2"][0], ym_d, ya_d, sqk_d, sv_d, sz_d)
    stick_phase(nc, x1, a["c_2_cols"], a["w_mod_2"], a["b_mod_2"], a["g_post_2"], a["w_out_2"][0], ym_d, ya_d, sqk_d,
                sv_d, sz_d, out[0])


_INS = ['x', 'ada_w', 'ada_b', 'gla_w_in', 'gla_w_alpha', 'gla_norm_g', 'gla_w_out', 'final_g',
        'w_mod_2', 'b_mod_2', 'g_post_2', 'm_wq_2', 'm_wk_2', 'a_sinks_2', 'w_out_2']
_COLS = [('c', 0, D, P), ('ada_b', 0, 2 * D, P), ('norm_g', 0, D, P), ('gla_b_alpha', 0, GH * GDK, P),
         ('c_2', 0, D, P), ('b_mod_2', 0, 2 * D, P), ('g_pre_2', 0, D, P), ('m_conv_w_2', 0, TAPS * MW, MD),
         ('m_conv_b_2', 0, MW, MD), ('m_norm_g_2', 0, MW, MD), ('m_skip_2', 0, MW, MD), ('m_b_i_2', 0, MH, MH),
         ('m_b_f_2', 0, MH, MH)]
_OUTS = [((1, S, D), 'float32')]


def _w_in_2_columns():
    import numpy as _np
    order = [("u", MW), ("mv", MW), ("i", MH), ("f", MH), ("mz", MW), ("aq", AW), ("ak", AKV * AD), ("av", AKV * AD),
             ("az", AW), ("sq", SW), ("sk", SW), ("sv", SW), ("sz", SW)]
    at, lies = 0, {}
    for n, w in order:
        lies[n] = _np.arange(at, at + w)
        at += w
    lies["aq"] = lies["aq"].reshape(AKV, AG, AD).transpose(1, 0, 2).reshape(-1)
    return _np.concatenate([lies[n] for n, _ in PARTS])


def kernel(**inputs):
    import numpy as _np
    import concourse.bacc as _bacc
    from concourse import mybir as _mybir
    from concourse.bass_utils import run_bass_kernel_spmd as _run

    nc = _bacc.Bacc("TRN2", target_bir_lowering=False, num_devices=1)
    arrays, args = {}, {}

    def give(name, a):
        a = _np.ascontiguousarray(a)
        arrays[f"in_{name}_dram"] = a
        args[name] = nc.dram_tensor(f"in_{name}_dram", a.shape, _mybir.dt.from_np(a.dtype), kind="ExternalInput").ap()

    for name in _INS:
        give(name, inputs[name])
    for name, lo, hi, width in _COLS:
        give(name + "_cols", _np.asarray(inputs[name]).reshape(-1)[lo:hi].reshape(-1, width).T)
    give("w_in_2", _np.asarray(inputs["w_in_2"])[0][:, _w_in_2_columns()])
    outs = nc.dram_tensor("out_0_dram", _OUTS[0][0], F32, kind="ExternalOutput").ap()
    build(nc, args, outs)
    r = _run(nc, [arrays], core_ids=[0])
    return r.results[0]["out_0_dram"]
```

```python
from contextlib import ExitStack

import concourse.bass as bass
from concourse import mybir

ALU = mybir.AluOpType
ACT = mybir.ActivationFunctionType
AX = mybir.AxisListType
F32 = mybir.dt.float32
BF16 = mybir.dt.bfloat16
U32 = mybir.dt.uint32

P = 128
S = 2048
D = 1024
T = 128
NT = S // T
KB = D // P
EPS = 1e-6

GH = 4
GDK = 128
GDV = 256
GR = 16
CH = 64
NC = T // CH
TAU = 16.0
Q0, K0, V0, A0, R0 = 0, GH * GDK, 2 * GH * GDK, 2 * GH * GDK + GH * GDV, 2 * GH * GDK + GH * GDV + GR
GIN = R0 + GH * GDV


class Link:

    def __init__(self, eng, sem, base):
        self.eng, self.sem, self.base, self.n = eng, sem, base, 0

    def done(self, ins):
        self.n += 1
        ins.then_inc(self.sem, 1)
        self.eng.wait_ge(self.sem, self.base + self.n)


def phase_semaphores(nc, ctx, prefix):
    held = []

    def sem(name):
        held.append(nc.alloc_semaphore(prefix + name))
        return held[-1]

    def give_back():
        nc.clear_and_free_semaphores(held)
        nc.all_engine_barrier()

    ctx.callback(give_back)
    return sem


def gla_phase(nc, x, c, ada_w, ada_b, ada_b_cols, norm_g, w_in, w_alpha, b_alpha, norm_h, w_out, final_g, x1):
    with ExitStack() as ctx:
        def sb(name, shape, dt=F32):
            return ctx.enter_context(nc.sbuf_tensor("g_" + name, shape, dt))

        sem = phase_semaphores(nc, ctx, "g_")

        wi_hi, wi_lo = sb("wi_hi", [P, KB, GIN], BF16), sb("wi_lo", [P, KB, GIN], BF16)
        wo_hl = sb("wo_hl", [P, 2, KB, D], BF16)
        wo_hi, wo_lo = wo_hl[:, 0], wo_hl[:, 1]
        acc = wo_hl[:].rearrange("p a k d -> p (a k d)").bitcast(F32)[:, 0:3 * D]
        NS = 4
        stage = sb("stage", [P, NS, GIN])
        arena = stage[:].rearrange("p s n -> p (s n)")
        used = [0]

        def carve(n):
            at = used[0]
            used[0] += n
            assert used[0] <= NS * GIN
            return arena[:, at:at + n]

        def carve3(a, b):
            return carve(a * b).rearrange("p (a b) -> p a b", a=a)

        qT, kT = carve(512), carve(512)
        v_sb = carve(D)
        r_sb, sg = carve(D), carve(D)
        lg, tmp = carve(512), carve(512)
        e_q, e_k, e_l, e_b = carve(512), carve(512), carve(512), carve(512)
        am = carve(512)
        st = [carve3(GH, GDV) for _ in range(NC)]
        og_hi = carve(512).bitcast(BF16)
        klT = carve(512)
        og_lo = klT.bitcast(BF16)
        xo = carve(D)
        xs = sb("xs", [P, 2, D])
        xn = sb("xn", [P, D])
        h_hi, h_lo = sb("h_hi", [P, KB, T], BF16), sb("h_lo", [P, KB, T], BF16)
        gate_row, fin_row, nh_row = sb("gate_row", [P, D]), sb("fin_row", [P, D]), sb("nh_row", [P, GDV])
        ident = sb("ident", [P, P])
        ones = sb("ones", [P, P])
        scan_keep = sb("scan_keep", [P, 512], BF16)
        causal = sb("causal", [P, 512], mybir.dt.uint8)
        causal_f = sb("causal_f", [P, 128])
        wal = sb("wal", [GR, 512])
        glr = sb("glr", [GR, T])
        cols = sb("cols", [P, 96])
        c_col, c_t, c_act = cols[:, 0:8], cols[:, 8:16], cols[:, 16:24]
        ng_col, ab_col, h_scale, h_shift = cols[:, 24:32], cols[:, 32:48], cols[:, 48:56], cols[:, 56:64]
        bal_col, eps_col, one_col = cols[:, 64:68], cols[:, 68:69], cols[:, 69:70]
        ssx, lnx, rsx = cols[:, 70:71], cols[:, 71:72], cols[:, 72:73]
        ssy, lny, rsy = cols[:, 73:74], cols[:, 74:75], cols[:, 75:76]
        sso, lno, rso = cols[:, 76:80], cols[:, 80:84], cols[:, 84:88]
        dec = sb("dec", [P, GH * NC])

        banks = [ctx.enter_context(nc.psum_tensor(f"g_bank{b}", [P, 512], F32)) for b in range(8)]
        G0, G1, TR, A, O0, O1, KV0, KV1 = banks
        O, KV = [O0, O1], [KV0, KV1]

        names = ("c_in consts_in wo_hi wo_lo mod_summed mod_out consts_ready c_silu w_hi w_lo mod_acc "
                 "x_stat xn_done xT_done hf_done h_hi_done h_lo_done glr_done glr_copied q_done q_copied k_done k_copied "
                 "alpha_done gate_in gate_act lg_done exp_q_done exp_k_done exp_l_done exp_b_done scores_in "
                 "v_done v_copied a_done am_done kl_turned klT_copied r_done r_used kv_done state_done o_done "
                 "o_stat og_done ogT_done og_hi_done og_lo_done y_done y_used x2_done y_stat x1_done x1_out "
                 "silu_ln silu_arg silu_exp r_gained act_link dve_link act_pre dve_pre pool_pre").split()
        s = {n: sem(n) for n in names}
        slot_in = [sem(f"slot_in{n}") for n in range(NS)]
        wo_in = [sem(f"wo_in{n}") for n in range(2)]
        x_in = [sem(f"x_in{n}") for n in range(2)]
        block = ctx.enter_context(nc.Block())

        NW = 2 * KB

        @block.sync
        def _(sp):
            def wait(name, v):
                if not (isinstance(v, int) and v <= 0):
                    sp.wait_ge(s[name], v)

            sp.dma_start(c_col, c).then_inc(s["c_in"], 16)
            small = [(ng_col, norm_g), (ab_col, ada_b_cols), (bal_col, b_alpha),
                     (wal[:], w_alpha[0]), (gate_row[:], ada_b[0, 2 * D:3 * D].partition_broadcast(P)),
                     (fin_row[:], final_g.partition_broadcast(P)), (nh_row[:], norm_h[0].partition_broadcast(P))]
            assert len(small) == 7
            for n in range(NW):
                w = (ada_w[0], w_in[0])[n // KB]
                width = w.shape[1]
                kb = n % KB
                if n >= NS:
                    m = n - NS
                    if m < KB:
                        sp.wait_ge(s["mod_acc"], m + 1)
                    else:
                        sp.wait_ge(s["w_lo"], m - KB + 1)
                sp.dma_start(stage[:, n % NS, 0:width], w[kb * P:(kb + 1) * P, :]).then_inc(slot_in[n % NS], 16)
                if n == KB:
                    sp.dma_start(xs[:, 0, :], x[0, 0:T, :]).then_inc(x_in[0], 16)
                    for dst, src in small:
                        sp.dma_start(dst, src).then_inc(s["consts_in"], 16)

            def tile(i, par, more=True):
                if more:
                    wait("x2_done", 2 * i)
                    sp.dma_start(xs[:, 1 - par, :], x[0, bass.ds((i + 1) * T, T), :]).then_inc(x_in[1 - par], 16)
                store(i)

            def store(i):
                if isinstance(i, int) and i == 0:
                    return
                wait("x1_done", i)
                sp.dma_start(x1[bass.ds((i - 1) * T, T), :], xo).then_inc(s["x1_out"], 16)

            tile(0, 0)
            sp.wait_ge(s["w_lo"], KB)
            for n in range(2 * KB):
                kb, half = n // 2, slice((n % 2) * 512, (n % 2 + 1) * 512)
                wait("wo_lo", n - 1)
                sp.dma_start(xo[:, half], w_out[0, kb * P:(kb + 1) * P, half]).then_inc(wo_in[n % 2], 16)
            with sp.Fori(0, (NT - 2) // 2) as j:
                tile(2 * j + 1, 1)
                tile(2 * j + 2, 0)
            tile(NT - 1, 1, more=False)
            store(NT)
            sp.wait_ge(s["x1_out"], 16 * NT)

        @block.gpsimd
        def _(pool):
            pool.memset(ones[:], 1.0).then_inc(s["pool_pre"], 1)
            pool.memset(ident[:], 0.0).then_inc(s["pool_pre"], 1)
            pool.memset(scan_keep[:], 1.0).then_inc(s["pool_pre"], 1)
            pool.memset(causal_f[:], 1.0).then_inc(s["pool_pre"], 1)
            pool.memset(eps_col, EPS).then_inc(s["pool_pre"], 1)
            pool.memset(one_col, 1.0).then_inc(s["pool_pre"], 1)
            pool.wait_ge(s["pool_pre"], 6)
            pool.affine_select(out=ident[:], in_=ident[:], compare_op=ALU.not_equal, fill=1.0, base=0,
                               pattern=[[-1, P]], channel_multiplier=1).then_inc(s["pool_pre"], 1)
            pool.memset(scan_keep[:].rearrange("p (c t) -> p c t", t=CH)[:, :, 0:1], 0.0).then_inc(s["pool_pre"], 1)
            pool.affine_select(out=causal_f[:], in_=causal_f[:], compare_op=ALU.is_ge, fill=0.0, base=0,
                               pattern=[[1, T]], channel_multiplier=-1).then_inc(s["pool_pre"], 1)
            pool.wait_ge(s["pool_pre"], 9)
            pool.memset(causal_f[0:CH, CH:T], 0.0).then_inc(s["pool_pre"], 1)
            pool.wait_ge(s["pool_pre"], 10)
            for h in range(GH):
                ins = pool.tensor_copy(causal[:, h * T:(h + 1) * T], causal_f[:])
            ins.then_inc(s["consts_ready"], 1)

            def tile(i):
                pool.wait_ge(s["silu_arg"], i + 1)
                pool.tensor_tensor(r_sb.rearrange("p (h e) -> p h e", h=GH), r_sb.rearrange("p (h e) -> p h e", h=GH),
                                   nh_row[:].unsqueeze(1).broadcast_to([P, GH, GDV]), ALU.mult).then_inc(s["r_gained"], 1)

            pool.wait_ge(s["mod_summed"], 1)
            for n in range(2 * KB):
                kb, half = n // 2, slice((n % 2) * 512, (n % 2 + 1) * 512)
                pool.wait_ge(wo_in[n % 2], 16 * (kb + 1))
                pool.tensor_tensor(wo_hi[:, kb, half], xo[:, half], ones[:, 0:1].broadcast_to([P, 512]), ALU.mult)\
                    .then_inc(s["wo_hi"], 1)
                pool.wait_ge(s["wo_hi"], n + 1)
                pool.tensor_tensor(wo_lo[:, kb, half], xo[:, half], wo_hi[:, kb, half], ALU.subtract)\
                    .then_inc(s["wo_lo"], 1)

            tile(0)
            with pool.Fori(1, NT) as i:
                tile(i)

        @block.scalar
        def _(act):
            def wait(name, v):
                if not (isinstance(v, int) and v <= 0):
                    act.wait_ge(s[name], v)

            pre = Link(act, s["act_pre"], 0)
            act.preload_act_table_set("natural_log_exp_and_others")
            act.wait_ge(s["consts_ready"], 1)
            act.wait_ge(s["c_in"], 16)
            act.activation(c_t, c_col, ACT.Exp, scale=-1.0).then_inc(s["c_silu"], 1)
            def x_stats(i, par, half, link, squares=r_sb):
                act.wait_ge(x_in[par], 16 * (half + 1))
                link.done(act.activation(squares, xs[:, par, :], ACT.Square, accum_out=ssx))
                link.done(act.activation(lnx, ssx, ACT.Ln, scale=1.0 / D, bias=eps_col))
                wait("xn_done", i)
                act.activation(rsx, lnx, ACT.Exp, scale=-0.5).then_inc(s["x_stat"], 1)

            def h_high(i):
                act.wait_ge(s["hf_done"], 2 * (i + 1))
                wait("r_done", 2 * i)
                act.activation(h_hi[:].rearrange("p k t -> p (k t)"), xn[:], ACT.Copy).then_inc(s["h_hi_done"], 1)

            def y_tail(i, link):
                act.wait_ge(s["x2_done"], 2 * (i + 1))
                link.done(act.activation(r_sb, xo, ACT.Square, accum_out=ssy))
                link.done(act.activation(lny, ssy, ACT.Ln, scale=1.0 / D, bias=eps_col))
                wait("x1_done", i)
                act.activation(rsy, lny, ACT.Exp, scale=-0.5).then_inc(s["y_stat"], 1)

            def og_high(i):
                for n, bank in enumerate((TR, G1)):
                    act.wait_ge(s["ogT_done"], 2 * i + n + 1)
                    wait("y_done", 2 * i)
                    act.activation(og_hi[:, n * 512:(n + 1) * 512], bank[:], ACT.Copy).then_inc(s["og_hi_done"], 1)

            ACT_LINKS = 9

            def tile(i, par, half, first=False, last=False):
                link = Link(act, s["act_link"], 0 if first else ACT_LINKS * i - 2)
                act.wait_ge(s["glr_done"], i + 1)
                wait("alpha_done", i)
                act.activation(glr[:], A[0:GR, 0:T], ACT.Copy).then_inc(s["glr_copied"], 1)
                act.wait_ge(s["q_done"], i + 1)
                wait("scores_in", 4 * i)
                act.activation(qT, G0[:], ACT.Copy).then_inc(s["q_copied"], 1)
                act.wait_ge(s["gate_in"], i + 1)
                link.done(act.activation(tmp, lg, ACT.Abs))
                link.done(act.activation(tmp, tmp, ACT.Exp, scale=-1.0))
                act.activation(tmp, tmp, ACT.Ln, bias=one_col).then_inc(s["gate_act"], 1)
                act.wait_ge(s["k_done"], i + 1)
                act.activation(kT, G0[:], ACT.Copy).then_inc(s["k_copied"], 1)
                if not first:
                    og_high(i - 1)
                act.wait_ge(s["lg_done"], i + 1)
                wait("a_done", i)
                act.activation(e_q, tmp, ACT.Exp, scale=1.0 / TAU).then_inc(s["exp_q_done"], 1)
                act.activation(e_k, tmp, ACT.Exp, scale=-1.0 / TAU).then_inc(s["exp_k_done"], 1)
                act.activation(e_l, e_l, ACT.Exp, scale=1.0 / TAU).then_inc(s["exp_l_done"], 1)
                wait("o_done", i)
                act.activation(e_b, lg, ACT.Exp, scale=1.0 / TAU).then_inc(s["exp_b_done"], 1)
                for n, bank in enumerate((G0, G1)):
                    act.wait_ge(s["v_done"], 2 * i + n + 1)
                    act.activation(v_sb[:, n * 512:(n + 1) * 512], bank[:], ACT.Copy).then_inc(s["v_copied"], 1)
                if not first:
                    y_tail(i - 1, link)
                if not last:
                    x_stats(i + 1, 1 - par, half + par, link)
                act.wait_ge(s["kl_turned"], i + 1)
                act.activation(klT, TR[:], ACT.Copy).then_inc(s["klT_copied"], 1)
                for n, bank in enumerate((G0, G1)):
                    act.wait_ge(s["r_done"], 2 * i + n + 1)
                    wait("ogT_done", 2 * i)
                    cs = slice(n * 512, (n + 1) * 512)
                    act.activation(r_sb[:, cs], bank[:], ACT.Copy)
                    act.activation(sg[:, cs], bank[:], ACT.Abs).then_inc(s["r_used"], 1)
                if not last:
                    h_high(i + 1)
                act.wait_ge(s["r_used"], 2 * (i + 1))
                link.done(act.activation(sg, sg, ACT.Exp, scale=-1.0))
                act.activation(sg, sg, ACT.Ln, bias=one_col).then_inc(s["silu_ln"], 1)
                act.wait_ge(s["o_done"], i + 1)
                for h in range(GH):
                    o_h = O[h // 2][:, (h % 2) * GDV:(h % 2 + 1) * GDV]
                    ins = act.activation((qT, kT)[h // 2][:, (h % 2) * GDV:(h % 2 + 1) * GDV], o_h, ACT.Square, accum_out=sso[:, h:h + 1])
                link.done(ins)
                link.done(act.activation(lno, sso, ACT.Ln, scale=1.0 / GDV, bias=eps_col))
                act.activation(rso, lno, ACT.Exp, scale=-0.5).then_inc(s["o_stat"], 1)
                act.wait_ge(s["silu_arg"], i + 1)
                act.activation(sg, sg, ACT.Exp).then_inc(s["silu_exp"], 1)

            for kb in range(KB):
                act.wait_ge(slot_in[(KB + kb) % NS], 16 * ((KB + kb) // NS + 1))
                act.activation(wi_hi[:, kb, :], stage[:, (KB + kb) % NS, :], ACT.Copy).then_inc(s["w_hi"], 1)
                if kb == 1:
                    x_stats(0, 0, 0, pre, xn[:])
                if kb == 4:
                    h_high(0)
            act.wait_ge(s["w_lo"], KB)
            tile(0, 0, 0, first=True)
            with act.Fori(0, (NT - 2) // 2) as j:
                tile(2 * j + 1, 1, j)
                tile(2 * j + 2, 0, j + 1)
            tile(NT - 1, 1, NT // 2 - 1, last=True)
            og_high(NT - 1)
            y_tail(NT - 1, Link(act, s["act_link"], ACT_LINKS * NT - 4))

        @block.vector
        def _(dve):
            def wait(name, v):
                if not (isinstance(v, int) and v <= 0):
                    dve.wait_ge(s[name], v)

            pre = Link(dve, s["dve_pre"], 0)
            dve.wait_ge(s["consts_ready"], 1)
            dve.wait_ge(s["c_in"], 16)
            dve.wait_ge(s["c_silu"], 1)
            pre.done(dve.tensor_scalar(c_t, c_t, 1.0, None, ALU.add))
            pre.done(dve.reciprocal(c_t, c_t))
            pre.done(dve.tensor_tensor(c_act, c_t, c_col, ALU.mult))
            for kb in range(KB):
                dve.wait_ge(slot_in[kb % NS], 16 * (kb // NS + 1))
                w = stage[:, kb % NS, 0:3 * D]
                if kb == 0:
                    ins = dve.tensor_scalar(acc, w, c_act[:, 0:1], None, ALU.mult)
                else:
                    dve.wait_ge(s["mod_acc"], kb)
                    ins = dve.scalar_tensor_tensor(acc, w, c_act[:, kb:kb + 1], acc, ALU.mult, ALU.add)
                ins.then_inc(s["mod_acc"], 1)

            def x_norm(i, par):
                dve.wait_ge(s["x_stat"], i + 1)
                wait("h_lo_done", i)
                wait("h_hi_done", i)
                dve.tensor_scalar(xn[:], xs[:, par, :], rsx, None, ALU.mult).then_inc(s["xn_done"], 1)

            def h_make(i):
                for n, bank in enumerate((TR, G0)):
                    dve.wait_ge(s["xT_done"], 2 * i + n + 1)
                    for m in range(4):
                        kb = 4 * n + m
                        ins = dve.tensor_scalar(xn[:, kb * T:(kb + 1) * T], bank[:, m * T:(m + 1) * T],
                                                h_scale[:, kb:kb + 1], h_shift[:, kb:kb + 1], ALU.mult, ALU.add)
                    ins.then_inc(s["hf_done"], 1)

            def h_low(i):
                dve.wait_ge(s["h_hi_done"], i + 1)
                dve.wait_ge(s["hf_done"], 2 * (i + 1))
                dve.tensor_tensor(h_lo[:].rearrange("p k t -> p (k t)"), xn[:],
                                  h_hi[:].rearrange("p k t -> p (k t)"), ALU.subtract).then_inc(s["h_lo_done"], 1)

            def og_low(i):
                for n, bank in enumerate((TR, G1)):
                    half = slice(n * 512, (n + 1) * 512)
                    dve.wait_ge(s["og_hi_done"], 2 * i + n + 1)
                    dve.tensor_tensor(og_lo[:, half], bank[:], og_hi[:, half], ALU.subtract)\
                       .then_inc(s["og_lo_done"], 1)

            def y_add(i, par, link):
                wait("x1_out", 16 * i)
                for n, bank in enumerate((G1, TR)):
                    half = slice(n * 512, (n + 1) * 512)
                    dve.wait_ge(s["y_done"], 2 * i + n + 1)
                    dve.tensor_tensor(xo[:, half], bank[:], gate_row[:, half], ALU.mult).then_inc(s["y_used"], 1)
                    dve.wait_ge(s["y_used"], 2 * i + n + 1)
                    dve.tensor_tensor(xo[:, half], xo[:, half], xs[:, par, half], ALU.add).then_inc(s["x2_done"], 1)

            def y_norm(i):
                dve.wait_ge(s["y_stat"], i + 1)
                dve.scalar_tensor_tensor(xo, xo, rsy, fin_row[:], ALU.mult, ALU.mult).then_inc(s["x1_done"], 1)

            DVE_LINKS = 4

            def tile(i, par, first=False, last=False):
                link = Link(dve, s["dve_link"], DVE_LINKS * i)
                dve.wait_ge(s["alpha_done"], i + 1)
                wait("exp_b_done", i)
                dve.tensor_tensor(lg.rearrange("p (h t) -> p h t", h=GH), A[:].rearrange("p (h t) -> p h t", h=GH),
                                  bal_col.unsqueeze(2).broadcast_to([P, GH, T]), ALU.add).then_inc(s["gate_in"], 1)
                dve.wait_ge(s["gate_act"], i + 1)
                link.done(dve.scalar_tensor_tensor(tmp, lg, 0.0, tmp, ALU.min, ALU.subtract))
                link.done(dve.tensor_tensor_scan(lg, scan_keep[:], tmp, 0.0, ALU.mult, ALU.add))
                b3 = lg.rearrange("p (c t) -> p c t", t=CH)
                mid = b3[:, :, CH // 2:CH // 2 + 1].broadcast_to([P, GH * NC, CH])
                end = b3[:, :, CH - 1:CH].broadcast_to([P, GH * NC, CH])
                wait("kl_turned", i)
                dve.tensor_tensor(tmp.rearrange("p (c t) -> p c t", t=CH), b3, mid, ALU.subtract)
                dve.tensor_tensor(e_l.rearrange("p (c t) -> p c t", t=CH), end, b3, ALU.subtract)\
                   .then_inc(s["lg_done"], 1)
                if not first:
                    og_low(i - 1)
                qs = GDK ** -0.5
                dve.wait_ge(s["q_copied"], i + 1)
                dve.wait_ge(s["exp_q_done"], i + 1)
                dve.scalar_tensor_tensor(e_q, qT, qs, e_q, ALU.mult, ALU.mult).then_inc(s["scores_in"], 1)
                dve.wait_ge(s["k_copied"], i + 1)
                dve.wait_ge(s["exp_k_done"], i + 1)
                dve.tensor_tensor(e_k, kT, e_k, ALU.mult).then_inc(s["scores_in"], 1)
                dve.wait_ge(s["exp_l_done"], i + 1)
                dve.tensor_tensor(e_l, kT, e_l, ALU.mult).then_inc(s["scores_in"], 1)
                dve.wait_ge(s["exp_b_done"], i + 1)
                link.done(dve.tensor_copy(dec[:].unsqueeze(2), e_b.rearrange("p (c t) -> p c t", t=CH)[:, :, CH - 1:CH]))
                dve.scalar_tensor_tensor(e_b, qT, qs, e_b, ALU.mult, ALU.mult).then_inc(s["scores_in"], 1)
                if not first:
                    y_add(i - 1, 1 - par, link)
                if not last:
                    x_norm(i + 1, 1 - par)
                dve.wait_ge(s["a_done"], i + 1)
                dve.memset(c_t[:, 0:1], 0.0)
                dve.copy_predicated(am, causal[:], A[:]).then_inc(s["am_done"], 1)
                for ch in range(NC):
                    if ch == 1 and not last:
                        h_make(i + 1)
                        h_low(i + 1)
                    dve.wait_ge(s["kv_done"], NC * i + ch + 1)
                    old, new = st[ch], st[(ch + 1) % NC]
                    for h in range(GH):
                        ins = dve.scalar_tensor_tensor(new[:, h, :], old[:, h, :], dec[:, NC * h + ch:NC * h + ch + 1],
                                                       KV[h // 2][:, (h % 2) * GDV:(h % 2 + 1) * GDV],
                                                       ALU.mult, ALU.add)
                    ins.then_inc(s["state_done"], 1)
                    dve.wait_ge(s["state_done"], NC * i + ch + 1)
                dve.wait_ge(s["silu_ln"], i + 1)
                dve.scalar_tensor_tensor(sg, r_sb, 0.0, sg, ALU.min, ALU.subtract).then_inc(s["silu_arg"], 1)
                if not first:
                    y_norm(i - 1)
                dve.wait_ge(s["silu_exp"], i + 1)
                dve.wait_ge(s["r_gained"], i + 1)
                link.done(dve.tensor_tensor(sg, sg, r_sb, ALU.mult))
                dve.wait_ge(s["o_stat"], i + 1)
                for h in range(GH):
                    part = sg[:, h * GDV:(h + 1) * GDV]
                    ins = dve.scalar_tensor_tensor(part, O[h // 2][:, (h % 2) * GDV:(h % 2 + 1) * GDV],
                                                   rso[:, h:h + 1], part, ALU.mult, ALU.mult)
                ins.then_inc(s["og_done"], 1)
                assert link.n == DVE_LINKS, link.n

            def low(kb):
                dve.wait_ge(s["w_hi"], kb + 1)
                dve.tensor_tensor(wi_lo[:, kb, :], stage[:, (KB + kb) % NS, :], wi_hi[:, kb, :],
                                  ALU.subtract).then_inc(s["w_lo"], 1)

            def modulation():
                dve.wait_ge(s["consts_in"], 16 * 7)
                dve.wait_ge(s["mod_summed"], 1)
                pre.done(dve.tensor_tensor(ab_col, ab_col, G0[:, 0:16], ALU.add))
                pre.done(dve.scalar_tensor_tensor(h_scale, ab_col[:, 8:16], 1.0, ng_col, ALU.add, ALU.mult))
                pre.done(dve.tensor_copy(h_shift, ab_col[:, 0:8]))
                for n, bank in enumerate((KV0, KV1)):
                    half = slice(n * 512, (n + 1) * 512)
                    pre.done(dve.tensor_tensor(gate_row[:, half], gate_row[:, half], bank[:], ALU.add))
                dve.memset(c_t, 0.0).then_inc(s["mod_out"], 1)

            for kb in range(KB):
                low(kb)
                if kb == 1:
                    modulation()
                if kb == 2:
                    x_norm(0, 0)
                if kb == 3:
                    h_make(0)
                if kb == 5:
                    h_low(0)
            dve.wait_ge(s["w_lo"], KB)
            pre.done(dve.memset(am, 0.0))
            pre.done(dve.memset(st[0], 0.0))
            tile(0, 0, first=True)
            with dve.Fori(0, (NT - 2) // 2) as j:
                tile(2 * j + 1, 1)
                tile(2 * j + 2, 0)
            tile(NT - 1, 1, last=True)
            og_low(NT - 1)
            y_add(NT - 1, 1, None)
            y_norm(NT - 1)

        @block.tensor
        def _(pe):
            def wait(name, v):
                if not (isinstance(v, int) and v <= 0):
                    pe.wait_ge(s[name], v)

            def mm3(out, parts, name):
                n = len(parts)
                for k, (l_hi, l_lo, r_hi, r_lo) in enumerate(parts):
                    pe.matmul(out, l_hi, r_hi, start=(k == 0), stop=False)
                    pe.matmul(out, l_hi, r_lo, start=False, stop=False)
                    ins = pe.matmul(out, l_lo, r_hi, start=False, stop=(k == n - 1))
                if name:
                    ins.then_inc(s[name], 1)

            def by_feature(out, c0, width, name):
                cs = slice(c0, c0 + width)
                mm3(out, [(wi_hi[:, kb, cs], wi_lo[:, kb, cs], h_hi[:, kb, :], h_lo[:, kb, :]) for kb in range(KB)], name)

            def by_token(out, c0, name):
                cs = slice(c0, c0 + 512)
                mm3(out, [(h_hi[:, kb, :], h_lo[:, kb, :], wi_hi[:, kb, cs], wi_lo[:, kb, cs]) for kb in range(KB)], name)

            pe.wait_ge(s["consts_ready"], 1)
            pe.wait_ge(s["mod_acc"], KB)
            for m in range(16):
                pe.matmul(G0[:, m:m + 1], acc[:, m * P:(m + 1) * P], ones[:, 0:1], start=(m == 0), stop=(m == 15),
                          skip_group_check=True)
            for n, bank in enumerate((KV0, KV1)):
                ins = pe.matmul(bank[:], ones[:], acc[:, 2 * D + n * 512:2 * D + (n + 1) * 512], start=True, stop=True)
            ins.then_inc(s["mod_summed"], 1)

            def turn_x(i):
                pe.wait_ge(s["xn_done"], i + 1)
                for n, bank in enumerate((TR, G0)):
                    if n == 0:
                        wait("klT_copied", i)
                    else:
                        wait("r_used", 2 * i - 1)
                    for m in range(4):
                        kb = 4 * n + m
                        ins = pe.transpose(bank[:, m * T:(m + 1) * T], xn[:, kb * P:(kb + 1) * P], ident[:])
                    ins.then_inc(s["xT_done"], 1)

            def turn_og(i):
                pe.wait_ge(s["og_done"], i + 1)
                for n, bank in enumerate((TR, G1)):
                    if n == 1:
                        pe.wait_ge(s["r_used"], 2 * (i + 1))
                    for m in range(4):
                        kb = 4 * n + m
                        ins = pe.transpose(bank[:, m * T:(m + 1) * T], sg[:, kb * P:(kb + 1) * P], ident[:])
                    ins.then_inc(s["ogT_done"], 1)

            def y_products(i):
                pe.wait_ge(s["wo_lo"], 2 * KB)
                for n, bank in enumerate((G1, TR)):
                    pe.wait_ge(s["og_lo_done"], 2 * (i + 1))
                    cs = slice(n * 512, (n + 1) * 512)
                    mm3(bank[:], [(og_hi[:, kb * P:(kb + 1) * P], og_lo[:, kb * P:(kb + 1) * P],
                                   wo_hi[:, kb, cs], wo_lo[:, kb, cs]) for kb in range(KB)], "y_done")

            def tile(i, par, first=False, last=False):
                pe.wait_ge(s["h_lo_done"], i + 1)
                wait("am_done", i)
                by_feature(A[0:GR, 0:T], A0, GR, "glr_done")
                pe.wait_ge(s["hf_done"], 2 * (i + 1))
                for h in range(GH):
                    by_feature(G0[:, h * T:(h + 1) * T], Q0 + h * GDK, GDK, "q_done" if h == GH - 1 else None)
                pe.wait_ge(s["glr_copied"], i + 1)
                for h in range(GH):
                    ins = pe.matmul(A[:, h * T:(h + 1) * T], wal[:, h * GDK:(h + 1) * GDK], glr[:], start=True, stop=True)
                ins.then_inc(s["alpha_done"], 1)
                pe.wait_ge(s["q_copied"], i + 1)
                for h in range(GH):
                    by_feature(G0[:, h * T:(h + 1) * T], K0 + h * GDK, GDK, "k_done" if h == GH - 1 else None)
                if not first:
                    turn_og(i - 1)
                pe.wait_ge(s["k_copied"], i + 1)
                by_token(G0[:], V0, "v_done")
                if not first:
                    y_products(i - 1)
                wait("y_used", 2 * i - 1)
                by_token(G1[:], V0 + 512, "v_done")
                pe.wait_ge(s["scores_in"], 4 * (i + 1))
                pe.wait_ge(s["gate_in"], i + 1)
                for h in range(GH):
                    hs = slice(h * T, (h + 1) * T)
                    ins = pe.matmul(A[:, hs], e_k[:, hs], e_q[:, hs], start=True, stop=True)
                ins.then_inc(s["a_done"], 1)
                wait("y_used", 2 * i)
                for h in range(GH):
                    ins = pe.transpose(TR[:, h * T:(h + 1) * T], e_l[:, h * T:(h + 1) * T], ident[:])
                ins.then_inc(s["kl_turned"], 1)
                pe.wait_ge(s["v_copied"], 2 * i + 1)
                by_token(G0[:], R0, "r_done")

                def kv(ch):
                    pe.wait_ge(s["klT_copied"], i + 1)
                    pe.wait_ge(s["v_copied"], 2 * (i + 1))
                    wait("state_done", NC * i + ch)
                    ts = slice(ch * CH, (ch + 1) * CH)
                    for h in range(GH):
                        ins = pe.matmul(KV[h // 2][:, (h % 2) * GDV:(h % 2 + 1) * GDV], klT[ts, h * GDK:(h + 1) * GDK],
                                        v_sb[ts, h * GDV:(h + 1) * GDV], start=True, stop=True)
                    ins.then_inc(s["kv_done"], 1)

                def o_state(ch):
                    if ch == 0:
                        wait("og_done", i)
                    for h in range(GH):
                        ins = pe.matmul(O[h // 2][ch * CH:(ch + 1) * CH, (h % 2) * GDV:(h % 2 + 1) * GDV],
                                        e_b[:, h * T + ch * CH:h * T + (ch + 1) * CH], st[ch][:, h, :],
                                        start=(h % 2 == 0), stop=False, skip_group_check=True)
                kv(0)
                by_token(G1[:], R0 + 512, "r_done")
                if not last:
                    turn_x(i + 1)
                o_state(0)
                kv(1)
                pe.wait_ge(s["state_done"], NC * i + 1)
                o_state(1)
                pe.wait_ge(s["am_done"], i + 1)
                for h in range(GH):
                    ins = pe.matmul(O[h // 2][:, (h % 2) * GDV:(h % 2 + 1) * GDV], am[:, h * T:(h + 1) * T],
                                    v_sb[:, h * GDV:(h + 1) * GDV], start=False, stop=True, skip_group_check=True)
                ins.then_inc(s["o_done"], 1)

            pe.wait_ge(s["mod_out"], 1)
            turn_x(0)
            pe.wait_ge(s["w_lo"], KB)
            tile(0, 0, first=True)
            with pe.Fori(0, (NT - 2) // 2) as j:
                tile(2 * j + 1, 1)
                tile(2 * j + 2, 0)
            tile(NT - 1, 1, last=True)
            turn_og(NT - 1)
            y_products(NT - 1)


MH, MD = 4, 96
MW = MH * MD
TAPS = 4
AH, AKV, AD = 6, 2, 64
AG = AH // AKV
AW = AH * AD
WINDOW = 128
SH, SD = 4, 64
SW = SH * SD
PARTS = [("i", MH), ("f", MH), ("u", MW), ("mz", MW), ("mv", MW), ("av", AKV * AD), ("sv", SW), ("aq", AW),
         ("ak", AKV * AD), ("az", AW), ("sq", SW), ("sk", SW), ("sz", SW)]
C0 = {n: sum(w for _, w in PARTS[:k]) for k, (n, _) in enumerate(PARTS)}
NIN = sum(w for _, w in PARTS)
MASKED = -1e30
SLOPES = [2.0 ** (-8.0 * (h + 1) / AH) for h in range(AH)]


def mix_phase(nc, x1, c, w_mod, b_mod_cols, g_pre, w_in, conv_w, conv_b, wq, wk, b_i, b_f, norm_h, skip, sinks,
              ym_d, ya_d, sq_d, sk_d, sv_d, sz_d):
    with ExitStack() as ctx:
        def sb(name, shape, dt=F32):
            return ctx.enter_context(nc.sbuf_tensor("m_" + name, shape, dt))

        w_hi, w_lo = sb("w_hi", [P, KB, NIN], BF16), sb("w_lo", [P, KB, NIN], BF16)
        NS = 3
        SIZE = 24800
        arena = sb("arena", [P, SIZE])
        stage = arena[:, 0:NS * NIN].rearrange("p (s n) -> p s n", s=NS)
        acc = arena[:, NS * NIN:NS * NIN + 2 * D]
        used = [0]

        def carve(n, dt=F32):
            at = used[0]
            used[0] += n if dt == F32 else n // 2
            assert used[0] <= SIZE, used[0]
            v = arena[:, at:used[0]]
            return v if dt == F32 else v.bitcast(dt)

        def carve3(a, b, dt=F32):
            return carve(a * b, dt).rearrange("p (a b) -> p a b", a=a)

        z_sb, e_sb = [carve(1152) for _ in range(2)], carve(1152)
        u_sb = carve3(MH, T + TAPS - 1)
        cv, ec, cu, skc = (carve3(MH, T) for _ in range(4))
        ct = ec
        va, vw = carve3(MH, MD + 1), carve3(MH, MD + 1)
        qT, kT, k_tok = carve3(MH, T), carve3(MH, T), carve3(MH, MD)
        dx = carve3(MH, T)
        C_st = [carve3(MH, MD + 1) for _ in range(NC)]
        nb, hh = carve3(MH, MD + 1), carve3(MH, MD)
        ym = carve3(MH, T)
        ym_hl = carve(2 * MH * T, BF16).rearrange("p (s h t) -> p s h t", s=2, h=MH)
        aq = carve3(AG, T)
        ak, av = carve3(2, T), carve3(2, AKV * AD)
        sc, pt = carve3(AH, 2 * T), carve3(AH, 2 * T)
        oa, ya = carve3(AH, AD), carve(AG * T)
        ya_hl = carve(2 * AG * T, BF16).rearrange("p (s n) -> p s n", s=2)
        sqk, sv = carve(2 * SW), carve(SW)
        sqk_hl = carve(4 * SW, BF16).rearrange("p (s n) -> p s n", s=2)
        rows = carve(10 * T)[0:MH, :].rearrange("p (n t) -> p n t", n=10)
        li, fr, ft, b_r, g_r, m_r, wi_r, ws_r, nm_r, nM_r = (rows[:, n, :] for n in range(10))
        used[0] = max(used[0], NS * NIN + 2 * D)
        xs = carve3(2, D)
        xn = carve(D)
        h_hi, h_lo = carve3(KB, T, BF16), carve3(KB, T, BF16)
        bias = carve3(AH, 2 * T)
        maskneg = sb("maskneg", [P, T])
        ident, ones = sb("ident", [P, P]), sb("ones", [P, 1])
        keep = sb("keep", [MH, T])
        sel = sb("sel", [MH, MH, P])
        wq_sb, wk_sb = sb("wq", [MD, MH, MD]), sb("wk", [MD, MH, MD])
        cols = sb("cols", [P, 176])
        at = [0]

        def col(n):
            at[0] += n
            assert at[0] <= 176
            return cols[:, at[0] - n:at[0]]

        c_col, c_t, c_act, gp_col, b_col, h_scale = col(8), col(8), col(8), col(8), col(16), col(8)
        eps_col, one_col, ssx, lnx, rsx = col(1), col(1), col(1), col(1), col(1)
        cw_col, cb_col, hn_col, sk_col = col(TAPS * MH), col(MH), col(MH), col(MH)
        bi_col, bf_col, m_0, m_1 = col(1), col(1), col(1), col(1)
        g_col, x_col, carry = col(MH), col(3 * MH), col(2 * MH)
        w_col, s_col, n_col = x_col[:, 0:MH], x_col[:, MH:2 * MH], x_col[:, 2 * MH:3 * MH]
        dn, rd, ssh, lnh, rsh = col(MH), col(MH), col(MH), col(MH), col(MH)
        snk, mx, ngm, es, sm, rs_a = (col(AH) for _ in range(6))

        banks = [ctx.enter_context(nc.psum_tensor(f"m_bank{b}", [P, 512], F32)) for b in range(8)]
        G0, G1, TR, B3, B4, B5, B6, B7 = banks

        names = ("c_in consts_in pool_pre consts_ready c_silu w_hi w_lo mod_acc mod_summed mod_out tiles_free "
                 "x_stat xn_done xT_done hf_done h_hi_done h_lo_done "
                 "gates_done gates_read gate_abs u_done u_copied mz_done mz_read aqk_done aqk_copied tv_done tv_copied "
                 "cols_done neg_max_done cols_exp az_done az_read qk_done qk_copied ktok_copied sqk_done sqk_copied "
                 "qk_scores dx_arg dx_exp dx_done kv_done state_done sz_done sz_read inter_done intra_done "
                 "sv_done sv_copied conv_done conv_link conv_exp cu_done skc_done vw_done num_done h_sq h_done hT_done ym_mid ym_done ym_split "
                 "scores_done hh_done max_done p_done pT_done pT_copied av_done oa_done oT_done ya_done ya_split "
                 "rows_done silu_one silu_rec silu_done sqk_split ym_out ya_out sq_out sk_out sv_out sz_out dve_pre act_pre dve_link act_link "
                 "head_2_scored").split()
        sem = phase_semaphores(nc, ctx, "m_")
        s = {n: sem(n) for n in names}
        slot_in = [sem(f"slot_in{n}") for n in range(NS)]
        x_in = [sem(f"x_in{n}") for n in range(2)]
        block = ctx.enter_context(nc.Block())

        def by_head(bank):
            return bank[0:MD, :].rearrange("p (h t) -> p h t", h=MH)

        def waiter(eng):
            def wait(name, v):
                if not (isinstance(v, int) and v <= 0):
                    eng.wait_ge(s[name], v)
            return wait

        def all_tiles(eng, tile):
            tile(0, 0, 0, True, False)
            with eng.Fori(0, (NT - 2) // 2) as j:
                tile(2 * j + 1, 1, j, False, False)
                tile(2 * j + 2, 0, j + 1, False, False)
            tile(NT - 1, 1, NT // 2 - 1, False, True)

        @block.sync
        def _(sp):
            wait = waiter(sp)
            sp.dma_start(c_col, c).then_inc(s["c_in"], 16)
            small = [(gp_col, g_pre), (b_col, b_mod_cols), (cw_col[0:MD], conv_w), (cb_col[0:MD], conv_b),
                     (hn_col[0:MD], norm_h), (sk_col[0:MD], skip), (bi_col[0:MH], b_i), (bf_col[0:MH], b_f),
                     (wq_sb[:], wq), (wk_sb[:], wk), (snk, sinks.partition_broadcast(P))]
            assert len(small) == 11
            for n in range(2 * KB):
                kb = n % KB
                src = w_mod[0, kb * P:(kb + 1) * P, 0:2 * D] if n < KB else w_in[kb * P:(kb + 1) * P, :]
                if n >= NS:
                    m = n - NS
                    if m < KB:
                        sp.wait_ge(s["mod_acc"], m + 1)
                    else:
                        sp.wait_ge(s["w_lo"], m - KB + 1)
                sp.dma_start(stage[:, n % NS, 0:src.shape[1]], src).then_inc(slot_in[n % NS], 16)
                if n == KB:
                    sp.dma_start(xs[:, 0, :], x1[0:T, :]).then_inc(x_in[0], 16)
                    for dst, src in small:
                        sp.dma_start(dst, src).then_inc(s["consts_in"], 16)

            def store_y(i):
                wait("ym_split", 2 * (i + 1))
                sp.dma_start(ym_d[bass.ds(i * MD, MD), :], ym_hl[0:MD].rearrange("p s h t -> p (s h t)"))\
                  .then_inc(s["ym_out"], 16)
                wait("ya_split", 2 * (i + 1))
                sp.dma_start(ya_d[bass.ds(i * P, P), :], ya_hl.rearrange("p s n -> p (s n)")).then_inc(s["ya_out"], 16)

            def tile(i, par, half, first, last):
                if not last:
                    wait("xn_done", i + 1)
                    sp.dma_start(xs[:, 1 - par, :], x1[bass.ds((i + 1) * T, T), :]).then_inc(x_in[1 - par], 16)
                if not first:
                    store_y(i - 1)
                wait("sqk_split", 2 * (i + 1))
                for g in range(2):
                    ps = slice(g * SD, (g + 1) * SD)
                    for v in range(2):
                        dst = sq_d[bass.ds(i * SD, SD), :].rearrange("r (v b g t) -> r v b g t", v=2, b=2, g=2)
                        sp.dma_start(dst[:, v, :, g, :], sqk_hl[ps, v, 0:SW].rearrange("p (b t) -> p b t", b=2))\
                          .then_inc(s["sq_out"], 16)
                        dst = sk_d[bass.ds(i * P + v * SD, SD), :].rearrange("r (b g t) -> r b g t", b=2, g=2)
                        sp.dma_start(dst[:, :, g, :], sqk_hl[ps, v, SW:2 * SW].rearrange("p (b t) -> p b t", b=2))\
                          .then_inc(s["sk_out"], 16)
                wait("sv_copied", i + 1)
                sp.dma_start(sv_d[bass.ds(i * P, P), :], sv).then_inc(s["sv_out"], 16)
                wait("silu_done", i + 1)
                sp.dma_start(sz_d[bass.ds(i * P, P), :], z_sb[par][:, 896:1152]).then_inc(s["sz_out"], 16)

            all_tiles(sp, tile)
            store_y(NT - 1)
            for n in ("ym_out", "ya_out", "sv_out", "sz_out"):
                sp.wait_ge(s[n], 16 * NT)
            for n in ("sq_out", "sk_out"):
                sp.wait_ge(s[n], 64 * NT)

        @block.gpsimd
        def _(pool):
            wait = waiter(pool)
            n_pre = [0]

            def pre(ins):
                n_pre[0] += 1
                ins.then_inc(s["pool_pre"], 1)
                pool.wait_ge(s["pool_pre"], n_pre[0])

            pre(pool.memset(ones[:], 1.0))
            pre(pool.memset(eps_col, EPS))
            pre(pool.memset(one_col, 1.0))
            pre(pool.memset(ident[:], 0.0))
            pre(pool.affine_select(out=ident[:], in_=ident[:], compare_op=ALU.not_equal, fill=1.0, base=0,
                                   pattern=[[-1, P]], channel_multiplier=1))
            pre(pool.memset(keep[:], 1.0))
            pre(pool.memset(keep[:].rearrange("p (c t) -> p c t", t=CH)[:, :, 0:1], 0.0))
            pre(pool.memset(sel[:], 0.0))
            pre(pool.affine_select(out=sel[:], in_=sel[:], compare_op=ALU.not_equal, fill=1.0, base=0,
                                   pattern=[[-1, MH], [0, P]], channel_multiplier=1))
            pre(pool.memset(maskneg[:], 0.0))
            pre(pool.affine_select(out=maskneg[:], in_=maskneg[:], compare_op=ALU.is_ge, fill=MASKED, base=0,
                                   pattern=[[1, T]], channel_multiplier=-1))
            pre(pool.memset(maskneg[0:CH, CH:T], MASKED))
            pre(pool.iota(bias[:, 0, :], pattern=[[-1, 2 * T]], base=WINDOW, channel_multiplier=1,
                          allow_small_or_imprecise_dtypes=True))
            for n in reversed(range(AH)):
                pre(pool.tensor_scalar(bias[:, n, :], bias[:, 0, :], -SLOPES[n], None, ALU.mult))
            pre(pool.affine_select(out=bias, in_=bias, compare_op=ALU.is_ge, fill=MASKED, base=WINDOW,
                                   pattern=[[0, AH], [-1, 2 * T]], channel_multiplier=1))
            pre(pool.affine_select(out=bias, in_=bias, compare_op=ALU.is_ge, fill=MASKED, base=-1,
                                   pattern=[[0, AH], [1, 2 * T]], channel_multiplier=-1))
            pool.memset(m_0, 0.0).then_inc(s["consts_ready"], 1)
            pool.wait_ge(s["w_lo"], KB)
            pool.wait_ge(s["mod_out"], 1)
            for v in (u_sb, C_st[0], e_sb, z_sb[0], z_sb[1]):
                pool.memset(v, 0.0)
            pool.memset(va[:, :, MD:MD + 1], 1.0).then_inc(s["tiles_free"], 1)
            pool.wait_ge(s["tiles_free"], 1)

            CONV_LINKS = 8

            def tap(n):
                return cw_col[0:MD, n * MH:(n + 1) * MH].unsqueeze(2).broadcast_to([MD, MH, T])

            def wide(v):
                return v[0:MD].unsqueeze(2).broadcast_to([MD, MH, T])

            def wide1(n):
                return ones[0:MD].unsqueeze(2).broadcast_to([MD, MH, n])

            def split_y(i):
                pool.wait_ge(s["ym_done"], i + 1)
                wait("ym_out", 16 * i)
                pool.tensor_tensor(ym_hl[0:MD, 0], ym[0:MD], wide1(T), ALU.mult).then_inc(s["ym_split"], 1)
                pool.wait_ge(s["ym_split"], 2 * i + 1)
                pool.tensor_tensor(ym_hl[0:MD, 1], ym[0:MD], ym_hl[0:MD, 0], ALU.subtract).then_inc(s["ym_split"], 1)
                pool.wait_ge(s["ya_done"], i + 1)
                wait("ya_out", 16 * i)
                pool.tensor_tensor(ya_hl[:, 0], ya, ones[:].broadcast_to([P, AG * T]), ALU.mult).then_inc(s["ya_split"], 1)
                pool.wait_ge(s["ya_split"], 2 * i + 1)
                pool.tensor_tensor(ya_hl[:, 1], ya, ya_hl[:, 0], ALU.subtract).then_inc(s["ya_split"], 1)

            def tile(i, par, half, first, last):
                n = [CONV_LINKS * i]

                def link(ins):
                    n[0] = n[0] + 1
                    ins.then_inc(s["conv_link"], 1)
                    pool.wait_ge(s["conv_link"], n[0])

                pool.wait_ge(s["u_copied"], i + 1)
                link(pool.tensor_tensor(cv[0:MD], u_sb[0:MD, :, 0:T], tap(0), ALU.mult))
                for k in range(1, TAPS):
                    link(pool.tensor_tensor(ct[0:MD], u_sb[0:MD, :, k:k + T], tap(k), ALU.mult))
                    link(pool.tensor_tensor(cv[0:MD], cv[0:MD], ct[0:MD], ALU.add))
                link(pool.tensor_tensor(u_sb[0:MD, :, 0:TAPS - 1], u_sb[0:MD, :, T:T + TAPS - 1],
                                        wide1(TAPS - 1), ALU.mult))
                pool.tensor_tensor(cv[0:MD], cv[0:MD], wide(cb_col), ALU.add).then_inc(s["conv_done"], 1)
                if not first:
                    split_y(i - 1)
                pool.wait_ge(s["cu_done"], i + 1)
                pool.tensor_tensor(skc[0:MD], cu[0:MD], wide(sk_col), ALU.mult).then_inc(s["skc_done"], 1)
                pool.wait_ge(s["sqk_copied"], 2 * (i + 1))
                wait("sq_out", 64 * i)
                wait("sk_out", 64 * i)
                pool.tensor_tensor(sqk_hl[:, 0], sqk, ones[:].broadcast_to([P, 2 * SW]), ALU.mult)\
                    .then_inc(s["sqk_split"], 1)
                pool.wait_ge(s["sqk_split"], 2 * i + 1)
                pool.tensor_tensor(sqk_hl[:, 1], sqk, sqk_hl[:, 0], ALU.subtract).then_inc(s["sqk_split"], 1)
                pool.wait_ge(s["sz_read"], i + 1)
                pool.tensor_tensor(e_sb, e_sb, ones[:].broadcast_to([P, 1152]), ALU.add).then_inc(s["silu_one"], 1)
                pool.wait_ge(s["silu_rec"], i + 1)
                pool.tensor_tensor(z_sb[par], z_sb[par], e_sb, ALU.mult).then_inc(s["silu_done"], 1)

            all_tiles(pool, tile)
            split_y(NT - 1)

        @block.scalar
        def _(act):
            wait = waiter(act)
            pre = Link(act, s["act_pre"], 0)
            act.preload_act_table_set("natural_log_exp_and_others")
            act.wait_ge(s["c_in"], 16)
            act.activation(c_t, c_col, ACT.Exp, scale=-1.0).then_inc(s["c_silu"], 1)
            def x_stats(i, par, half, link):
                act.wait_ge(x_in[par], 16 * (half + 1))
                wait("h_lo_done", i)
                wait("h_hi_done", i)
                link.done(act.activation(xn, xs[:, par, :], ACT.Square, accum_out=ssx))
                link.done(act.activation(lnx, ssx, ACT.Ln, scale=1.0 / D, bias=eps_col))
                act.activation(rsx, lnx, ACT.Exp, scale=-0.5).then_inc(s["x_stat"], 1)

            def h_high(i):
                act.wait_ge(s["hf_done"], 2 * (i + 1))
                wait("sv_done", i)
                act.activation(h_hi.rearrange("p k t -> p (k t)"), xn, ACT.Copy).then_inc(s["h_hi_done"], 1)

            def gate_out(name, bank, n, at, i, par):
                act.wait_ge(s[name + "_done"], i + 1)
                act.activation(z_sb[par][0:n, at[0]:at[1]], bank[0:n, 0:at[1] - at[0]], ACT.Copy)
                act.activation(e_sb[0:n, at[0]:at[1]], bank[0:n, 0:at[1] - at[0]], ACT.Exp, scale=-1.0)\
                   .then_inc(s[name + "_read"], 1)

            ACT_LINKS = 6

            def late(i, par):
                for n, bank in enumerate((B3, B4, B5)):
                    act.wait_ge(s["pT_done"], 3 * i + n + 1)
                    act.activation(pt[:, 2 * n:2 * n + 2, :].rearrange("p h s -> p (h s)"), bank[:], ACT.Copy)\
                       .then_inc(s["pT_copied"], 1)

            def late_first(i, par):
                for n, bank in enumerate((B3, B4, B5)):
                    act.wait_ge(s["pT_done"], n + 1)
                    act.activation(pt[:, 2 * n:2 * n + 2, T:2 * T],
                                   bank[:].rearrange("p (h s) -> p h s", h=2)[:, :, T:2 * T], ACT.Copy)\
                       .then_inc(s["pT_copied"], 1)

            def tile(i, par, half, first, last):
                link = Link(act, s["act_link"], ACT_LINKS * i)
                act.wait_ge(s["u_done"], i + 1)
                wait("conv_done", i)
                act.activation(u_sb[0:MD, :, TAPS - 1:], by_head(G0), ACT.Copy).then_inc(s["u_copied"], 1)
                act.wait_ge(s["gates_read"], i + 1)
                link.done(act.activation(ft, fr, ACT.Abs))
                link.done(act.activation(ft, ft, ACT.Exp, scale=-1.0))
                act.activation(ft, ft, ACT.Ln, bias=one_col[0:MH]).then_inc(s["gate_abs"], 1)
                wait("silu_done", i)
                wait("sz_out", 16 * (i - 1) if not first else 0)
                gate_out("mz", G1, MD, (0, 512), i, par)
                if not first:
                    (late_first if isinstance(i, int) and i == 1 else late)(i - 1, 1 - par)
                act.wait_ge(s["aqk_done"], i + 1)
                wait("scores_done", i)
                act.activation(aq.rearrange("p j t -> p (j t)"), G0[:, 0:AG * T], ACT.Copy, scale=AD ** -0.5)
                act.activation(ak[:, par, :], G0[:, AG * T:AG * T + T], ACT.Copy).then_inc(s["aqk_copied"], 1)
                act.wait_ge(s["conv_done"], i + 1)
                wait("cu_done", i)
                act.activation(ec[0:MD], cv[0:MD], ACT.Exp, scale=-1.0).then_inc(s["conv_exp"], 1)
                act.wait_ge(s["tv_done"], i + 1)
                wait("av_done", i)
                act.activation(va[:, :, 0:MD], G1[:, 0:MW].rearrange("p (h e) -> p h e", h=MH), ACT.Copy)
                act.activation(av[:, par, :], G1[:, MW:MW + AKV * AD], ACT.Copy).then_inc(s["tv_copied"], 1)
                act.wait_ge(s["cols_done"], i + 1)
                wait("num_done", i)
                act.activation(g_col, TR[:, 0:MH], ACT.Copy)
                act.activation(x_col, TR[:, MH:4 * MH], ACT.Exp)
                act.activation(carry[0:MD], TR[0:MD, 4 * MH:6 * MH], ACT.Exp).then_inc(s["cols_exp"], 1)
                act.wait_ge(s["dx_arg"], i + 1)
                act.activation(dx, dx, ACT.Exp).then_inc(s["dx_exp"], 1)
                gate_out("az", G0, P, (512, 896), i, par)
                act.wait_ge(s["qk_done"], i + 1)
                act.activation(qT[0:MD], by_head(B3), ACT.Copy, scale=MD ** -0.5)
                act.activation(kT[0:MD], by_head(B4), ACT.Copy).then_inc(s["qk_copied"], 1)
                act.wait_ge(s["sqk_done"], i + 1)
                wait("sqk_split", 2 * i)
                act.activation(sqk[:, 0:SW], G1[:, 0:SW], ACT.Copy, scale=SD ** -0.5).then_inc(s["sqk_copied"], 1)
                act.activation(sqk[:, SW:2 * SW], G1[:, SW:2 * SW], ACT.Copy).then_inc(s["sqk_copied"], 1)
                if not last:
                    x_stats(i + 1, 1 - par, half + par, link)
                gate_out("sz", G0, P, (896, 1152), i, par)
                act.wait_ge(s["sv_done"], i + 1)
                wait("sv_out", 16 * i)
                act.activation(sv, G1[:, 0:SW], ACT.Copy).then_inc(s["sv_copied"], 1)
                if not last:
                    h_high(i + 1)
                act.wait_ge(s["h_sq"], i + 1)
                for h in range(MH):
                    ins = act.activation(dx[:, h, 0:MD], hh[:, h, :], ACT.Square, accum_out=ssh[:, h:h + 1])
                link.done(ins)
                link.done(act.activation(lnh, ssh, ACT.Ln, scale=1.0 / MD, bias=eps_col))
                act.activation(rsh, lnh, ACT.Exp, scale=-0.5).then_inc(s["h_done"], 1)
                act.wait_ge(s["max_done"], i + 1)
                act.activation(es, es, ACT.Exp)
                for n in range(AH):
                    at = sc[:, n, T if first else 0:2 * T]
                    ins = act.activation(at, at, ACT.Exp, bias=ngm[:, n:n + 1], accum_out=sm[:, n:n + 1])
                ins.then_inc(s["p_done"], 1)

            act.wait_ge(s["consts_ready"], 1)
            for kb in range(KB):
                n = KB + kb
                act.wait_ge(slot_in[n % NS], 16 * (n // NS + 1))
                act.activation(w_hi[:, kb, :], stage[:, n % NS, :], ACT.Copy).then_inc(s["w_hi"], 1)
                if kb == 1:
                    x_stats(0, 0, 0, pre)
                if kb == 4:
                    h_high(0)
            act.wait_ge(s["tiles_free"], 1)
            tile(0, 0, 0, True, False)
            tile(1, 1, 0, False, False)
            with act.Fori(1, (NT - 2) // 2) as j:
                tile(2 * j, 0, j, False, False)
                tile(2 * j + 1, 1, j, False, False)
            tile(NT - 2, 0, NT // 2 - 1, False, False)
            tile(NT - 1, 1, NT // 2 - 1, False, True)
            late(NT - 1, 1)

        @block.vector
        def _(dve):
            wait = waiter(dve)
            pre = Link(dve, s["dve_pre"], 0)
            dve.wait_ge(s["c_in"], 16)
            dve.wait_ge(s["c_silu"], 1)
            pre.done(dve.tensor_scalar(c_t, c_t, 1.0, None, ALU.add))
            pre.done(dve.reciprocal(c_t, c_t))
            pre.done(dve.tensor_tensor(c_act, c_t, c_col, ALU.mult))
            for kb in range(KB):
                dve.wait_ge(slot_in[kb % NS], 16 * (kb // NS + 1))
                w = stage[:, kb % NS, 0:2 * D]
                if kb == 0:
                    ins = dve.tensor_scalar(acc, w, c_act[:, 0:1], None, ALU.mult)
                else:
                    dve.wait_ge(s["mod_acc"], kb)
                    ins = dve.scalar_tensor_tensor(acc, w, c_act[:, kb:kb + 1], acc, ALU.mult, ALU.add)
                ins.then_inc(s["mod_acc"], 1)
            h_shift = b_col[:, 0:8]

            def x_norm(i, par):
                dve.wait_ge(s["x_stat"], i + 1)
                dve.tensor_scalar(xn, xs[:, par, :], rsx, None, ALU.mult).then_inc(s["xn_done"], 1)

            def h_make(i):
                for n, bank in enumerate((TR, G0)):
                    dve.wait_ge(s["xT_done"], 2 * i + n + 1)
                    for m in range(4):
                        kb = 4 * n + m
                        ins = dve.tensor_scalar(xn[:, kb * T:(kb + 1) * T], bank[:, m * T:(m + 1) * T],
                                                h_scale[:, kb:kb + 1], h_shift[:, kb:kb + 1], ALU.mult, ALU.add)
                    ins.then_inc(s["hf_done"], 1)

            def h_low(i):
                dve.wait_ge(s["h_hi_done"], i + 1)
                dve.wait_ge(s["hf_done"], 2 * (i + 1))
                dve.tensor_tensor(h_lo.rearrange("p k t -> p (k t)"), xn, h_hi.rearrange("p k t -> p (k t)"),
                                  ALU.subtract).then_inc(s["h_lo_done"], 1)

            DVE_LINKS = 24

            def heads_out(i, par):
                dve.wait_ge(s["hT_done"], i + 1)
                wait("ym_split", 2 * i)
                for h in range(MH):
                    ins = dve.scalar_tensor_tensor(ym[0:MD, h, :], B7[0:MD, h * T:(h + 1) * T], hn_col[0:MD, h:h + 1],
                                                   skc[0:MD, h, :], ALU.mult, ALU.add)
                ins.then_inc(s["ym_mid"], 1)
                dve.wait_ge(s["ym_mid"], i + 1)
                dve.wait_ge(s["silu_done"], i + 1)
                dve.tensor_tensor(ym[0:MD], ym[0:MD], z_sb[par][0:MD, 0:512].rearrange("p (h t) -> p h t", h=MH),
                                  ALU.mult).then_inc(s["ym_done"], 1)

            def window_norm(i):
                dve.wait_ge(s["av_done"], i + 1)
                dve.tensor_tensor(oa, B6[:, 0:AW].rearrange("p (h e) -> p h e", h=AH),
                                  rs_a.unsqueeze(2).broadcast_to([P, AH, AD]), ALU.mult).then_inc(s["oa_done"], 1)

            def window_out(i, par):
                dve.wait_ge(s["oT_done"], i + 1)
                wait("ya_split", 2 * i)
                dve.tensor_tensor(ya, TR[:, 0:AG * T], z_sb[par][:, 512:896], ALU.mult).then_inc(s["ya_done"], 1)

            def tile(i, par, half, first, last):
                link = Link(dve, s["dve_link"], DVE_LINKS * i)
                dve.wait_ge(s["gates_done"], i + 1)
                dve.tensor_scalar(li, TR[0:MH, 0:T], bi_col[0:MH], None, ALU.add)
                dve.tensor_scalar(fr, TR[0:MH, T:2 * T], bf_col[0:MH], None, ALU.add).then_inc(s["gates_read"], 1)
                dve.wait_ge(s["gate_abs"], i + 1)
                wait("cols_done", i)
                wait("neg_max_done", i)
                link.done(dve.scalar_tensor_tensor(fr, fr, 0.0, ft, ALU.min, ALU.subtract))
                link.done(dve.tensor_tensor_scan(b_r, keep[:], fr, 0.0, ALU.mult, ALU.add))
                link.done(dve.tensor_tensor(g_r, li, b_r, ALU.subtract))
                for ch in range(NC):
                    ts = slice(ch * CH, (ch + 1) * CH)
                    last_t = slice((ch + 1) * CH - 1, (ch + 1) * CH)
                    m_old, m_new = (m_0, m_1) if ch == 0 else (m_1, m_0)
                    link.done(dve.tensor_tensor_scan(m_r[:, ts], g_r[:, ts], g_r[:, ts], m_old[0:MH], ALU.max, ALU.max))
                    link.done(dve.tensor_scalar(wi_r[:, ts], m_r[:, ts], -1.0, m_old[0:MH], ALU.mult, ALU.add))
                    link.done(dve.tensor_scalar(ws_r[:, ts], g_r[:, ts], m_r[:, last_t], None, ALU.subtract))
                    link.done(dve.tensor_tensor(m_new[0:MH], b_r[:, last_t], m_r[:, last_t], ALU.add))
                link.done(dve.scalar_tensor_tensor(nm_r, b_r, -1.0, m_r, ALU.mult, ALU.subtract))
                dve.tensor_scalar(nM_r, m_r, -1.0, None, ALU.mult).then_inc(s["rows_done"], 1)
                if not first:
                    heads_out(i - 1, 1 - par)
                    window_norm(i - 1)
                dve.wait_ge(s["conv_exp"], i + 1)
                wait("skc_done", i)
                wait("qk_done", i)
                link.done(dve.tensor_scalar(ec[0:MD], ec[0:MD], 1.0, None, ALU.add))
                link.done(dve.reciprocal(ec[0:MD], ec[0:MD]))
                dve.tensor_tensor(cu[0:MD], cv[0:MD], ec[0:MD], ALU.mult).then_inc(s["cu_done"], 1)
                dve.wait_ge(s["cols_exp"], i + 1)
                dve.wait_ge(s["neg_max_done"], i + 1)
                wait("h_done", i)
                for h in range(MH):
                    ins = dve.scalar_tensor_tensor(dx[:, h, :], B7[:, h * T:(h + 1) * T], g_col[:, h:h + 1],
                                                   maskneg[:], ALU.add, ALU.min)
                ins.then_inc(s["dx_arg"], 1)
                if not first:
                    window_out(i - 1, 1 - par)
                dve.wait_ge(s["tv_copied"], i + 1)
                wait("kv_done", NC * i)
                dve.tensor_tensor(vw, va, s_col.unsqueeze(2).broadcast_to([P, MH, MD + 1]), ALU.mult)\
                   .then_inc(s["vw_done"], 1)
                dve.wait_ge(s["qk_done"], i + 1)
                dve.tensor_copy(k_tok, B5[:, 0:MW].rearrange("p (h e) -> p h e", h=MH)).then_inc(s["ktok_copied"], 1)
                dve.wait_ge(s["dx_exp"], i + 1)
                dve.wait_ge(s["qk_scores"], i + 1)
                dve.tensor_tensor(dx, B6[:].rearrange("p (h t) -> p h t", h=MH), dx, ALU.mult)\
                   .then_inc(s["dx_done"], 1)
                for ch, bank in enumerate((B3, B5)):
                    dve.wait_ge(s["kv_done"], NC * i + ch + 1)
                    old, new = C_st[ch], C_st[(ch + 1) % NC]
                    for h in range(MH):
                        ins = dve.scalar_tensor_tensor(new[0:MD, h, :], old[0:MD, h, :],
                                                       carry[0:MD, NC * h + ch:NC * h + ch + 1],
                                                       bank[0:MD, h * (MD + 1):(h + 1) * (MD + 1)], ALU.mult, ALU.add)
                    ins.then_inc(s["state_done"], 1)
                    dve.wait_ge(s["state_done"], NC * i + ch + 1)
                    if ch == 0 and not last:
                        x_norm(i + 1, 1 - par)
                if not last:
                    h_make(i + 1)
                    h_low(i + 1)
                dve.wait_ge(s["inter_done"], i + 1)
                wait("hT_done", i)
                link.done(dve.tensor_tensor(nb, B4[:, 0:MH * (MD + 1)].rearrange("p (h e) -> p h e", h=MH),
                                            w_col.unsqueeze(2).broadcast_to([P, MH, MD + 1]), ALU.mult))
                dve.wait_ge(s["intra_done"], i + 1)
                link.done(dve.tensor_tensor(nb, nb, B7[:, 0:MH * (MD + 1)].rearrange("p (h e) -> p h e", h=MH), ALU.add))
                den = nb[:, :, MD:MD + 1].rearrange("p h o -> p (h o)")
                link.done(dve.scalar_tensor_tensor(dn, den, -1.0, den, ALU.mult, ALU.max))
                dve.tensor_tensor(dn, dn, n_col, ALU.max).then_inc(s["num_done"], 1)
                dve.wait_ge(s["num_done"], i + 1)
                link.done(dve.reciprocal(rd, dn))
                dve.tensor_tensor(hh, nb[:, :, 0:MD], rd.unsqueeze(2).broadcast_to([P, MH, MD]), ALU.mult)\
                   .then_inc(s["h_sq"], 1)
                wait("pT_done", 3 * i)
                k0 = T if first else 0
                for n, bank in enumerate((B3, B5, B6)):
                    dve.wait_ge(s["scores_done"], i + 1)
                    ins = dve.tensor_tensor(sc[:, 2 * n:2 * n + 2, k0:2 * T],
                                            bank[:].rearrange("p (h s) -> p h s", h=2)[:, :, k0:2 * T],
                                            bias[:, 2 * n:2 * n + 2, k0:2 * T], ALU.add)
                link.done(ins)
                link.done(dve.tensor_reduce(mx, sc[:, :, k0:2 * T], AX.X, ALU.max))
                link.done(dve.tensor_tensor(mx, mx, snk, ALU.max))
                link.done(dve.tensor_tensor(es, snk, mx, ALU.subtract))
                dve.tensor_scalar(ngm, mx, -1.0, None, ALU.mult).then_inc(s["max_done"], 1)
                dve.wait_ge(s["h_done"], i + 1)
                dve.tensor_tensor(hh, hh, rsh.unsqueeze(2).broadcast_to([P, MH, MD]), ALU.mult)\
                   .then_inc(s["hh_done"], 1)
                dve.wait_ge(s["sz_read"], i + 1)
                dve.wait_ge(s["silu_one"], i + 1)
                dve.reciprocal(e_sb, e_sb).then_inc(s["silu_rec"], 1)
                dve.wait_ge(s["p_done"], i + 1)
                link.done(dve.tensor_tensor(sm, sm, es, ALU.add))
                link.done(dve.reciprocal(rs_a, sm))
                assert link.n == DVE_LINKS, link.n

            dve.wait_ge(s["consts_ready"], 1)
            for kb in range(KB):
                dve.wait_ge(s["w_hi"], kb + 1)
                dve.tensor_tensor(w_lo[:, kb, :], stage[:, (KB + kb) % NS, :], w_hi[:, kb, :], ALU.subtract)\
                   .then_inc(s["w_lo"], 1)
                if kb == 1:
                    dve.wait_ge(s["consts_in"], 16 * 11)
                    dve.wait_ge(s["mod_summed"], 1)
                    pre.done(dve.tensor_tensor(b_col, b_col, G0[:, 0:16], ALU.add))
                    dve.scalar_tensor_tensor(h_scale, b_col[:, 8:16], 1.0, gp_col, ALU.add, ALU.mult)\
                       .then_inc(s["mod_out"], 1)
                    dve.wait_ge(s["mod_out"], 1)
                if kb == 2:
                    x_norm(0, 0)
                if kb == 3:
                    h_make(0)
                if kb == 5:
                    h_low(0)
            dve.wait_ge(s["tiles_free"], 1)
            all_tiles(dve, tile)
            heads_out(NT - 1, 1)
            window_norm(NT - 1)
            window_out(NT - 1, 1)

        @block.tensor
        def _(pe):
            wait = waiter(pe)

            def mm3(out, parts, name):
                n = len(parts)
                for k, (l_hi, l_lo, r_hi, r_lo) in enumerate(parts):
                    pe.matmul(out, l_hi, r_hi, start=(k == 0), stop=False)
                    pe.matmul(out, l_hi, r_lo, start=False, stop=False)
                    ins = pe.matmul(out, l_lo, r_hi, start=False, stop=(k == n - 1))
                if name:
                    ins.then_inc(s[name], 1)

            def by_feature(bank, blocks, name):
                for n, (c0, width) in enumerate(blocks):
                    cs = slice(c0, c0 + width)
                    mm3(bank[0:width, n * T:(n + 1) * T],
                        [(w_hi[:, kb, cs], w_lo[:, kb, cs], h_hi[:, kb, :], h_lo[:, kb, :]) for kb in range(KB)],
                        name if n == len(blocks) - 1 else None)

            def by_token(bank, c0, width, name):
                cs = slice(c0, c0 + width)
                mm3(bank[:, 0:width], [(h_hi[:, kb, :], h_lo[:, kb, :], w_hi[:, kb, cs], w_lo[:, kb, cs])
                                       for kb in range(KB)], name)

            pe.wait_ge(s["consts_ready"], 1)
            pe.wait_ge(s["mod_acc"], KB)
            for m in range(16):
                ins = pe.matmul(G0[:, m:m + 1], acc[:, m * P:(m + 1) * P], ones[:, 0:1], start=(m == 0), stop=(m == 15),
                                skip_group_check=True)
            ins.then_inc(s["mod_summed"], 1)
            pe.wait_ge(s["mod_out"], 1)

            def turn_x(i):
                pe.wait_ge(s["xn_done"], i + 1)
                for n, bank in enumerate((TR, G0)):
                    if n == 0:
                        wait("ya_done", i - 1)
                        wait("cols_exp", i)
                    else:
                        wait("sz_read", i)
                    for m in range(4):
                        kb = 4 * n + m
                        ins = pe.transpose(bank[:, m * T:(m + 1) * T], xn[:, kb * P:(kb + 1) * P], ident[:])
                    ins.then_inc(s["xT_done"], 1)

            def turn_p(i, first):
                pe.wait_ge(s["p_done"], i + 1)
                for n, bank in enumerate((B3, B4, B5)):
                    for k in range(4):
                        head, half = 2 * n + k // 2, k % 2
                        if first and half == 0:
                            continue
                        ins = pe.transpose(bank[:, k * T:(k + 1) * T], sc[:, head, half * T:(half + 1) * T], ident[:])
                    ins.then_inc(s["pT_done"], 1)

            def p_times_v(i, par, first):
                pe.wait_ge(s["pT_copied"], 3 * (i + 1))
                for n in range(AH):
                    g = n // AG
                    for half in range(1 if first else 0, 2):
                        slot = par if half else 1 - par
                        ins = pe.matmul(B6[:, n * AD:(n + 1) * AD], pt[:, n, half * T:(half + 1) * T],
                                        av[:, slot, g * AD:(g + 1) * AD], start=(first or half == 0), stop=(half == 1))
                ins.then_inc(s["av_done"], 1)

            def turn_h(i):
                pe.wait_ge(s["hh_done"], i + 1)
                for h in range(MH):
                    ins = pe.transpose(B7[0:MD, h * T:(h + 1) * T], hh[:, h, :], ident[:])
                ins.then_inc(s["hT_done"], 1)

            def turn_o(i):
                pe.wait_ge(s["oa_done"], i + 1)
                flat = oa.rearrange("p h e -> p (h e)")
                for j in range(AG):
                    ins = pe.transpose(TR[:, j * T:(j + 1) * T], flat[:, j * P:(j + 1) * P], ident[:])
                ins.then_inc(s["oT_done"], 1)

            def tile(i, par, half, first, last, second=False):
                pe.wait_ge(s["h_lo_done"], i + 1)
                for n, name in enumerate(("i", "f")):
                    cs = slice(C0[name], C0[name] + MH)
                    mm3(TR[0:MH, n * T:(n + 1) * T], [(w_hi[:, kb, cs], w_lo[:, kb, cs], h_hi[:, kb, :], h_lo[:, kb, :])
                                                      for kb in range(KB)], "gates_done" if n else None)
                pe.wait_ge(s["hf_done"], 2 * (i + 1))
                by_feature(G0, [(C0["u"] + h * MD, MD) for h in range(MH)], "u_done")
                wait("sv_copied", i)
                by_feature(G1, [(C0["mz"] + h * MD, MD) for h in range(MH)], "mz_done")
                if not first:
                    turn_p(i - 1, second)
                pe.wait_ge(s["u_copied"], i + 1)
                by_feature(G0, [(C0["aq"] + n * P, P) for n in range(AG + 1)], "aqk_done")
                if not first:
                    p_times_v(i - 1, 1 - par, second)
                    turn_h(i - 1)
                pe.wait_ge(s["mz_read"], i + 1)
                by_token(G1, C0["mv"], MW + AKV * AD, "tv_done")
                pe.wait_ge(s["rows_done"], i + 1)
                for h in range(MH):
                    pe.matmul(TR[0:MD, 4 * MH + NC * h:4 * MH + NC * (h + 1)], sel[:, h, 0:MD],
                              wi_r[:, CH - 1:T:CH], start=True, stop=True)
                for n, row in enumerate((g_r, wi_r, ws_r, nm_r)):
                    ins = pe.transpose(TR[:, n * MH:(n + 1) * MH], row, ident[0:MH, 0:MH])
                ins.then_inc(s["cols_done"], 1)
                wait("ym_mid", i)
                for h in range(MH):
                    ins = pe.matmul(B7[:, h * T:(h + 1) * T], sel[:, h, :], nM_r, start=True, stop=True)
                ins.then_inc(s["neg_max_done"], 1)
                pe.wait_ge(s["aqk_copied"], i + 1)
                by_feature(G0, [(C0["az"] + n * P, P) for n in range(AG)], "az_done")
                if not first:
                    pe.wait_ge(s["cols_exp"], i + 1)
                    turn_o(i - 1)
                pe.wait_ge(s["cu_done"], i + 1)
                for h in range(MH):
                    hs = slice(h * T, (h + 1) * T)
                    pe.matmul(B3[0:MD, hs], wq_sb[:, h, :], cu[0:MD, h, :], start=True, stop=True)
                    pe.matmul(B4[0:MD, hs], wk_sb[:, h, :], cu[0:MD, h, :], start=True, stop=True)
                    ins = pe.matmul(B5[:, h * MD:(h + 1) * MD], cu[0:MD, h, :], wk_sb[:, h, :], start=True, stop=True)
                ins.then_inc(s["qk_done"], 1)
                pe.wait_ge(s["tv_copied"], i + 1)
                by_feature(G1, [(C0["sq"] + n * P, P) for n in range(4)], "sqk_done")
                pe.wait_ge(s["qk_copied"], i + 1)
                wait("oa_done", i)
                for h in range(MH):
                    ins = pe.matmul(B6[:, h * T:(h + 1) * T], kT[0:MD, h, :], qT[0:MD, h, :], start=True, stop=True)
                ins.then_inc(s["qk_scores"], 1)

                def kv(ch, bank):
                    pe.wait_ge(s["ktok_copied"], i + 1)
                    pe.wait_ge(s["vw_done"], i + 1)
                    ts = slice(ch * CH, (ch + 1) * CH)
                    for h in range(MH):
                        ins = pe.matmul(bank[0:MD, h * (MD + 1):(h + 1) * (MD + 1)], k_tok[ts, h, :], vw[ts, h, :],
                                        start=True, stop=True)
                    ins.then_inc(s["kv_done"], 1)

                def inter(ch):
                    for h in range(MH):
                        ins = pe.matmul(B4[ch * CH:(ch + 1) * CH, h * (MD + 1):(h + 1) * (MD + 1)],
                                        qT[0:MD, h, ch * CH:(ch + 1) * CH], C_st[ch][0:MD, h, :], start=True, stop=True)
                    return ins

                kv(0, B3)
                pe.wait_ge(s["az_read"], i + 1)
                by_feature(G0, [(C0["sz"] + n * P, P) for n in range(2)], "sz_done")
                inter(0)
                kv(1, B5)
                if not last:
                    turn_x(i + 1)
                pe.wait_ge(s["sqk_copied"], 2 * (i + 1))
                by_token(G1, C0["sv"], SW, "sv_done")
                pe.wait_ge(s["state_done"], NC * i + 1)
                inter(1).then_inc(s["inter_done"], 1)
                pe.wait_ge(s["dx_done"], i + 1)
                for h in range(MH):
                    ins = pe.matmul(B7[:, h * (MD + 1):(h + 1) * (MD + 1)], dx[:, h, :], va[:, h, :],
                                    start=True, stop=True)
                ins.then_inc(s["intra_done"], 1)
                pe.wait_ge(s["state_done"], NC * (i + 1))
                for head in (0, 1, 2, 4, 5, 3):
                    if head == 3:
                        pe.wait_ge(s["head_2_scored"], i + 1)
                    for half in range(1 if first else 0, 2):
                        slot = par if half else 1 - par
                        g, j = head // AG, head % AG
                        ps = slice(g * AD, (g + 1) * AD)
                        at = (head % 2) * 2 * T + half * T
                        ins = pe.matmul((B3, B5, B6)[head // 2][:, at:at + T], aq[ps, j, :], ak[ps, slot, :],
                                        start=True, stop=True)
                    if head == 2:
                        ins.then_inc(s["head_2_scored"], 1)
                ins.then_inc(s["scores_done"], 1)

            turn_x(0)
            pe.wait_ge(s["w_lo"], KB)
            tile(0, 0, 0, True, False)
            tile(1, 1, 0, False, False, True)
            with pe.Fori(1, (NT - 2) // 2) as j:
                tile(2 * j, 0, j, False, False)
                tile(2 * j + 1, 1, j, False, False)
            tile(NT - 2, 0, NT // 2 - 1, False, False)
            tile(NT - 1, 1, NT // 2 - 1, False, True)
            turn_p(NT - 1, False)
            p_times_v(NT - 1, 1, False)
            turn_h(NT - 1)
            turn_o(NT - 1)


Y_BLOCKS = [MD] * MH + [P] * (AW // P) + [P] * (SW // P)
NY = len(Y_BLOCKS)
T2 = 2 * T
NP2 = S // T2
UNITS = 4


def stick_phase(nc, x1, c, w_mod, b_mod, g_post, w_out, ym_d, ya_d, sq_d, sk_d, sv_d, sz_d, out):
    with ExitStack() as ctx:
        def sb(name, shape, dt=F32):
            return ctx.enter_context(nc.sbuf_tensor("s_" + name, shape, dt))

        wo_hi, wo_lo = sb("wo_hi", [P, NY, D], BF16), sb("wo_lo", [P, NY, D], BF16)
        NS = 6
        stage = sb("stage", [P, NS, D])
        acc = sb("acc", [P, D])
        k_c = sb("k_c", [P, NT, SH * T], BF16)
        v_c = sb("v_c", [P, NT, SW])
        ab = [sb(f"ab{n}", [P, 512])[:] for n in range(UNITS)]
        sp_ = [sb(f"sp{n}", [P, 512])[:] for n in range(UNITS)]
        zs = [sb(f"zs{n}", [P, 512]) for n in range(UNITS)]
        hi = [sb(f"hi{n}", [P, 512], BF16) for n in range(UNITS)]
        lo = [sb(f"lo{n}", [P, 512], BF16) for n in range(UNITS)]
        q_sb = [sb(f"q{n}", [P, 2, SH, T2], BF16) for n in range(2)]
        o_sb = sb("o_sb", [P, 512])
        ident = sb("ident", [P, P])
        sz_sb = [sb(f"sz{n}", [P, 2, T2]) for n in range(2)]
        ym_sb = [sb(f"ym{n}", [P, 2, 2, MH, T], BF16) for n in range(2)]
        ya_sb = [sb(f"ya{n}", [P, 2, 2, AW // P, T], BF16) for n in range(2)]
        ys, ys_hi, ys_lo = acc[:, 0:512], sb("ys_hi", [P, 2, T2], BF16), sb("ys_lo", [P, 2, T2], BF16)
        xr = sb("xr", [P, 2, D])
        y_sb = sb("y_sb", [P, UNITS, 512])
        junk = [sb(f"junk{n}", [P, 512], BF16) for n in range(UNITS)]
        zero, nothing = sb("zero", [P, P], BF16), sb("nothing", [P, 512], BF16)
        gp_row, g_row = sb("gp_row", [P, D]), sb("g_row", [P, D])
        ones = sb("ones", [P, P])
        tri, unt = sb("tri", [P, P], BF16), sb("unt", [P, P], BF16)
        keep = sb("keep", [P, 2, T2])
        cap = sb("cap", [P, 2, T2])
        cols = sb("cols", [P, 64])
        c_col, c_t, c_act = cols[:, 0:8], cols[:, 8:16], cols[:, 16:24]
        eps_col, one_col = cols[:, 24:25], cols[:, 25:26]
        ssy, sst, lny, rsy = cols[:, 26:30], cols[:, 30:32], cols[:, 32:34], cols[:, 34:36]

        banks = [ctx.enter_context(nc.psum_tensor(f"s_bank{b}", [P, 512], F32)) for b in range(8)]
        Z, C, O, M = banks[0:4], banks[4:6], banks[6], banks[7]

        names = ("c_in consts_in kv_rest pool_pre consts_ready c_silu w_hi w_lo mod_acc mod_summed row_done kv_in x_in "
                 "z_done z_read abs_done ln_done sp_done hi_done lo_done cs_done arg_done a_done av_done "
                 "ys_done ys_hi_done ys_lo_done y_done y_sq y_stat y_used x_out act_pre dve_pre act_link dve_link "
                 "o_read o_turned masked y_scaled y_read").split()
        sem = phase_semaphores(nc, ctx, "s_")
        s = {n: sem(n) for n in names}
        slot_in = [sem(f"slot_in{n}") for n in range(NS)]
        q_in = [sem(f"q_in{side}") for side in range(2)]
        block = ctx.enter_context(nc.Block())
        NW = KB + NY

        def waiter(eng):
            def wait(name, v):
                if not (isinstance(v, int) and v <= 0):
                    eng.wait_ge(s[name], v)
            return wait

        def is0(v):
            return isinstance(v, int) and v == 0

        def all_passes(eng, one_pass, after_first=None):
            def round_(m):
                last = m * -1 + NP2
                one_pass(m, 2 * m, (NP2 + 1) * m, 0, m, (NP2 + 2) * m + 1, last)
                if is0(m) and after_first:
                    after_first()
                late = m * -1 + (NP2 - 1)
                one_pass(late, 2 * m + 1, (NP2 + 2) * m + 1, 1, late, (NP2 + 1) * m + NP2 + 1, m)
            round_(0)
            round_(1)
            with eng.Fori(2, NP2 // 2) as m:
                round_(m)

        def run_units(eng, stages, I, nb, inner, beside=None):
            def body(nb, diagonal, pair, step=None):
                for k in range(UNITS):
                    for stage_, lag in stages:
                        if k >= lag:
                            stage_(nb, k - lag, diagonal, pair)
                        elif not diagonal:
                            stage_(nb - 1, k - lag + UNITS, False, pair + 1)
                    if step is not None and beside:
                        beside(step + k)

            body(nb, True, I, 0)
            if not is0(inner):
                body(nb + 1, False, I - 1, UNITS)
                if not (isinstance(inner, int) and inner == 1):
                    with eng.Fori(1, inner) as r:
                        body(nb + 1 + r, False, nc.s_assert_within(
                            r * -1 + (I - 1), 0, NP2 - 2, skip_runtime_bounds_check_because="a pair before the queries"))

        def drain_units(stages, end):
            for k in range(UNITS, UNITS + max(lag for _, lag in stages)):
                for stage_, lag in stages:
                    if k - lag < UNITS:
                        stage_(end - 1, k - lag, False, 0)

        @block.sync
        def _(sp):
            wait = waiter(sp)
            sp.dma_start(c_col, c).then_inc(s["c_in"], 16)
            k_blocks, v_blocks = (d.rearrange("(n p) f -> p n f", p=P) for d in (sk_d, sv_d))
            sp.dma_start(k_c[:, 0:2], k_blocks[:, 0:2]).then_inc(s["kv_in"], 16)
            sp.dma_start(v_c[:, 0:2], v_blocks[:, 0:2]).then_inc(s["kv_in"], 16)

            def weights():
                small = [(g_row[:], b_mod[0, 2 * D:3 * D].partition_broadcast(P)),
                         (gp_row[:], g_post[0].partition_broadcast(P))]
                row = 0
                for n in range(NW):
                    if n == NS:
                        sp.dma_start(k_c[:, 2:NT], k_blocks[:, 2:NT]).then_inc(s["kv_rest"], 16)
                        sp.dma_start(v_c[:, 2:NT], v_blocks[:, 2:NT]).then_inc(s["kv_rest"], 16)
                        for dst, src in small:
                            sp.dma_start(dst, src).then_inc(s["consts_in"], 16)
                    if n < KB:
                        src = w_mod[0, n * P:(n + 1) * P, 2 * D:3 * D]
                    else:
                        src = w_out[row:row + Y_BLOCKS[n - KB], :]
                        row += Y_BLOCKS[n - KB]
                    if n >= NS:
                        m = n - NS
                        if m < KB:
                            sp.wait_ge(s["mod_acc"], m + 1)
                        else:
                            sp.wait_ge(s["w_lo"], m - KB + 1)
                    sp.dma_start(stage[0:src.shape[0], n % NS, :], src).then_inc(slot_in[n % NS], 16)

            def one_pass(I, n, nb, side, inner, end, last):
                wait("y_done", 4 * (n - 1))
                for tt in range(2):
                    ts = slice(tt * T, (tt + 1) * T)
                    rows = bass.ds((2 * I + tt) * P, P)
                    for half in range(2):
                        sp.dma_start(q_sb[side][half * SD:(half + 1) * SD, :, :, ts].rearrange("p v h t -> p (v h) t"),
                                     sq_d[bass.ds((2 * I + tt) * SD, SD), :].rearrange("r (n t) -> r n t", t=T))\
                          .then_inc(q_in[side], 16)
                    sp.dma_start(sz_sb[side][:, :, ts], sz_d[rows, :].rearrange("p (b t) -> p b t", b=2))\
                      .then_inc(q_in[side], 16)
                    sp.dma_start(ym_sb[side][0:MD, tt].rearrange("p s h t -> p (s h t)"),
                                 ym_d[bass.ds((2 * I + tt) * MD, MD), :]).then_inc(q_in[side], 16)
                    sp.dma_start(ya_sb[side][:, tt].rearrange("p s h t -> p (s h t)"), ya_d[rows, :])\
                      .then_inc(q_in[side], 16)
                if not (isinstance(n, int) and n < 2):
                    store(I - 1 if side == 0 else I + 1, n - 2)
                if not is0(n):
                    load_x(last)

            def load_x(I):
                for tt in range(2):
                    sp.dma_start(xr[:, tt, :], x1[bass.ds((2 * I + tt) * T, T), :]).then_inc(s["x_in"], 16)

            def store(I, n):
                for tt in range(2):
                    sp.wait_ge(s["y_used"], 4 * n + 2 * (tt + 1))
                    sp.dma_start(out[bass.ds((2 * I + tt) * T, T), :], xr[:, tt, :]).then_inc(s["x_out"], 16)
                sp.wait_ge(s["x_out"], 32 * (n + 1))

            all_passes(sp, one_pass, weights)
            store(NP2 // 2 - 1, NP2 - 2)
            load_x(NP2 // 2)
            store(NP2 // 2, NP2 - 1)

        @block.gpsimd
        def _(pool):
            wait = waiter(pool)
            n_pre = [0]

            def pre(ins):
                n_pre[0] += 1
                ins.then_inc(s["pool_pre"], 1)
                pool.wait_ge(s["pool_pre"], n_pre[0])

            pre(pool.memset(ones[:], 1.0))
            pre(pool.memset(eps_col, EPS))
            pre(pool.memset(one_col, 1.0))
            for m, op, b in ((tri, ALU.is_ge, 0), (unt, ALU.is_gt, 0)):
                pre(pool.memset(m[:], 1.0))
                sign = 1 if m is tri else -1
                pre(pool.affine_select(out=m[:], in_=m[:], compare_op=op, fill=0.0, base=b, pattern=[[-sign, P]],
                                       channel_multiplier=sign))
            pre(pool.memset(zero[:], 0.0))
            pre(pool.memset(ident[:], 0.0))
            pre(pool.affine_select(out=ident[:], in_=ident[:], compare_op=ALU.not_equal, fill=1.0, base=0,
                                   pattern=[[-1, P]], channel_multiplier=1))
            pre(pool.memset(nothing[:], 0.0))
            for n in range(2):
                pre(pool.memset(keep[:, n], 1.0))
                pre(pool.affine_select(out=keep[:, n], in_=keep[:, n], compare_op=ALU.is_gt, fill=0.0,
                                       base=-T * (1 - n), pattern=[[1, T2]], channel_multiplier=-1))
                pre(pool.tensor_scalar(cap[:, n], keep[:, n], 0.5, -2.0 * MASKED, ALU.subtract, ALU.mult))
            pool.memset(cols[:, 42:43], 0.0).then_inc(s["consts_ready"], 1)

            def high(nb, k):
                pool.wait_ge(s["sp_done"], UNITS * nb + k + 1)
                wait("cs_done", UNITS * nb + k - 1 if not is0(nb) else 0)
                pool.tensor_tensor(hi[k][:], sp_[k], one_col.broadcast_to([P, 512]), ALU.mult).then_inc(s["hi_done"], 1)

            def one_pass(I, n, nb, side, inner, end, last):
                for k in range(UNITS):
                    high(nb, k)
                if not is0(inner):
                    with pool.Fori(0, inner) as r:
                        for k in range(UNITS):
                            high(nb + 1 + r, k)

            all_passes(pool, one_pass)

        @block.scalar
        def _(act):
            wait = waiter(act)
            act.preload_act_table_set("natural_log_exp_and_others")
            act.wait_ge(s["c_in"], 16)
            act.activation(c_t, c_col, ACT.Exp, scale=-1.0).then_inc(s["c_silu"], 1)
            act.wait_ge(s["consts_ready"], 1)

            def weights():
                for n in range(KB, NW):
                    act.wait_ge(slot_in[n % NS], 16 * (n // NS + 1))
                    r = Y_BLOCKS[n - KB]
                    act.activation(wo_hi[0:r, n - KB, :], stage[0:r, n % NS, :], ACT.Copy).then_inc(s["w_hi"], 1)

            def z_abs(nb, k, diagonal, pair):
                act.wait_ge(s["z_done"], UNITS * nb + k + 1)
                wait("sp_done", UNITS * (nb - 1) + k + 1 if not is0(nb) else 0)
                act.activation(ab[k], Z[k][:], ACT.Abs).then_inc(s["abs_done"], 1)

            def exp_ln(nb, k, diagonal, pair):
                act.wait_ge(s["abs_done"], UNITS * nb + k + 1)
                act.activation(ab[k], ab[k], ACT.Exp, scale=-1.0).then_inc(s["act_link"], 1)
                act.wait_ge(s["act_link"], UNITS * nb + k + 1)
                act.activation(ab[k], ab[k], ACT.Ln, bias=one_col).then_inc(s["ln_done"], 1)

            def weight(nb, k, diagonal, pair):
                act.wait_ge(s["arg_done"], UNITS * nb + k + 1)
                wait("av_done", UNITS * (nb - 1) + k + 1 if not is0(nb) else 0)
                act.activation(zs[k][:], zs[k][:], ACT.Exp).then_inc(s["a_done"], 1)

            def one_pass(I, n, nb, side, inner, end, last):
                if not is0(n):
                    ys_high(n - 1)
                run_units(act, stages, I, nb, inner, None if is0(n) else lambda step: y_out(n - 1, step // 2) if step % 2 else None)
                drain_units(stages, end)

            stages = [(z_abs, 0), (exp_ln, 0), (weight, 3)]

            def ys_high(n):
                act.wait_ge(s["ys_done"], n + 1)
                act.activation(ys_hi[:].rearrange("p b t -> p (b t)"), ys, ACT.Copy).then_inc(s["ys_hi_done"], 1)

            def y_out(n, k):
                act.wait_ge(s["y_done"], 4 * n + k + 1)
                wait("y_used", 4 * (n - 1) + k + 1 if not is0(n) else 0)
                act.activation(y_sb[:, k, :], M[:], ACT.Copy).then_inc(s["y_read"], 1)
                act.wait_ge(s["y_read"], 4 * n + k + 1)
                act.activation(junk[k][:], y_sb[:, k, :], ACT.Square, accum_out=ssy[:, k:k + 1]).then_inc(s["y_sq"], 1)
                act.wait_ge(s["y_sq"], 4 * n + k + 1)
                tt = k // 2
                if k % 2 == 0:
                    act.activation(sst[:, tt:tt + 1], ssy[:, k:k + 1], ACT.Identity, scale=1.0 / D, bias=eps_col)\
                       .then_inc(s["act_pre"], 1)
                else:
                    act.wait_ge(s["act_pre"], 4 * n + k)
                    act.activation(lny[:, tt:tt + 1], ssy[:, k:k + 1], ACT.Ln, scale=1.0 / D, bias=sst[:, tt:tt + 1])\
                       .then_inc(s["act_pre"], 1)
                    act.wait_ge(s["act_pre"], 4 * n + k + 1)
                    act.activation(rsy[:, tt:tt + 1], lny[:, tt:tt + 1], ACT.Exp, scale=-0.5).then_inc(s["y_stat"], 1)

            all_passes(act, one_pass, weights)
            ys_high(NP2 - 1)
            for k in range(UNITS):
                y_out(NP2 - 1, k)

        @block.vector
        def _(dve):
            wait = waiter(dve)
            pre = Link(dve, s["dve_pre"], 0)
            dve.wait_ge(s["c_in"], 16)
            dve.wait_ge(s["c_silu"], 1)
            pre.done(dve.tensor_scalar(c_t, c_t, 1.0, None, ALU.add))
            pre.done(dve.reciprocal(c_t, c_t))
            pre.done(dve.tensor_tensor(c_act, c_t, c_col, ALU.mult))
            dve.wait_ge(s["consts_ready"], 1)

            def weights():
                for kb in range(KB):
                    dve.wait_ge(slot_in[kb % NS], 16 * (kb // NS + 1))
                    w = stage[:, kb % NS, :]
                    if kb == 0:
                        ins = dve.tensor_scalar(acc[:], w, c_act[:, 0:1], None, ALU.mult)
                    else:
                        dve.wait_ge(s["mod_acc"], kb)
                        ins = dve.scalar_tensor_tensor(acc[:], w, c_act[:, kb:kb + 1], acc[:], ALU.mult, ALU.add)
                    ins.then_inc(s["mod_acc"], 1)
                for n in range(KB, NW):
                    dve.wait_ge(s["w_hi"], n - KB + 1)
                    r = Y_BLOCKS[n - KB]
                    dve.tensor_tensor(wo_lo[0:r, n - KB, :], stage[0:r, n % NS, :], wo_hi[0:r, n - KB, :], ALU.subtract)\
                       .then_inc(s["w_lo"], 1)
                dve.wait_ge(s["consts_in"], 32)
                for n in range(2):
                    half = slice(n * 512, (n + 1) * 512)
                    dve.wait_ge(s["mod_summed"], n + 1)
                    pre.done(dve.tensor_tensor(g_row[:, half], g_row[:, half], Z[n][:], ALU.add))
                dve.tensor_tensor(gp_row[:], gp_row[:], g_row[:], ALU.mult).then_inc(s["row_done"], 1)
                dve.wait_ge(s["row_done"], 1)

            def heads2(v):
                return v.rearrange("p (h t) -> p h t", h=2)

            def z_copy(nb, k, diagonal, pair):
                dve.wait_ge(s["abs_done"], UNITS * nb + k + 1)
                wait("av_done", UNITS * (nb - 1) + k + 1 if not is0(nb) else 0)
                if diagonal:
                    ins = dve.tensor_tensor(heads2(zs[k][:]), heads2(Z[k][:]),
                                            cap[:, k // 2:k // 2 + 1, :].broadcast_to([P, 2, T2]), ALU.min)
                else:
                    ins = dve.tensor_copy(zs[k][:], Z[k][:])
                ins.then_inc(s["z_read"], 1)

            def softplus(nb, k, diagonal, pair):
                dve.wait_ge(s["ln_done"], UNITS * nb + k + 1)
                dve.wait_ge(s["z_read"], UNITS * nb + k + 1)
                wait("lo_done", UNITS * (nb - 1) + k + 1 if not is0(nb) else 0)
                ins = dve.scalar_tensor_tensor(sp_[k], zs[k][:], 0.0, ab[k], ALU.max, ALU.add)
                if diagonal:
                    ins.then_inc(s["masked"], 1)
                    dve.wait_ge(s["masked"], UNITS * passes[0] + k + 1)
                    ins = dve.tensor_tensor(heads2(sp_[k]), heads2(sp_[k]),
                                            keep[:, k // 2:k // 2 + 1, :].broadcast_to([P, 2, T2]), ALU.mult)
                ins.then_inc(s["sp_done"], 1)

            def low(nb, k, diagonal, pair):
                dve.wait_ge(s["hi_done"], UNITS * nb + k + 1)
                dve.tensor_tensor(lo[k][:], sp_[k], hi[k][:], ALU.subtract).then_inc(s["lo_done"], 1)

            def exponent(nb, k, diagonal, pair):
                dve.wait_ge(s["cs_done"], UNITS * nb + k + 1)
                dve.tensor_tensor(zs[k][:], zs[k][:], C[k % 2][:], ALU.subtract).then_inc(s["arg_done"], 1)

            def one_pass(I, n, nb, side, inner, end, last):
                passes[0] = n
                if not is0(n):
                    gate(n - 1, 1 - side)
                if not (isinstance(n, int) and n < 2):
                    y_scale(n - 2, 1)
                run_units(dve, stages, I, nb, inner, None if is0(n) else lambda k: between(n - 1, k))
                drain_units(stages, end)
                dve.wait_ge(s["av_done"], UNITS * end)
                wait("o_turned", n)
                dve.tensor_copy(o_sb[:], O[:]).then_inc(s["o_read"], 1)

            def between(n, step):
                if step == UNITS + 1:
                    y_scale(n, 0)

            def gate(n, side):
                dve.wait_ge(s["o_turned"], n + 1)
                dve.wait_ge(q_in[side], 80 * n + 160 - 80 * side)
                wait("ys_lo_done", n)
                wait("y_done", 4 * n)
                dve.tensor_tensor(ys, O[:], sz_sb[side][:].rearrange("p b t -> p (b t)"), ALU.mult)\
                   .then_inc(s["ys_done"], 1)
                dve.wait_ge(s["ys_hi_done"], n + 1)
                dve.tensor_tensor(ys_lo[:].rearrange("p b t -> p (b t)"), ys, ys_hi[:].rearrange("p b t -> p (b t)"),
                                  ALU.subtract).then_inc(s["ys_lo_done"], 1)

            passes = [0]
            stages = [(exponent, 3), (z_copy, 0), (low, 1), (softplus, 0)]

            def y_scale(n, tt):
                dve.wait_ge(s["x_in"], 32 * (n + 1))
                dve.wait_ge(s["y_stat"], 2 * n + tt + 1)
                for h in range(2):
                    half = slice(h * 512, (h + 1) * 512)
                    yt = y_sb[:, 2 * tt + h, :]
                    dve.scalar_tensor_tensor(yt, yt, rsy[:, tt:tt + 1], gp_row[:, half], ALU.mult, ALU.mult)\
                       .then_inc(s["y_scaled"], 1)
                    dve.wait_ge(s["y_scaled"], 4 * n + 2 * tt + h + 1)
                    dve.tensor_tensor(xr[:, tt, half], xr[:, tt, half], yt, ALU.add).then_inc(s["y_used"], 1)

            all_passes(dve, one_pass, weights)
            gate(NP2 - 1, 1)
            y_scale(NP2 - 2, 1)
            for tt in range(2):
                y_scale(NP2 - 1, tt)

        @block.tensor
        def _(pe):
            wait = waiter(pe)
            pe.wait_ge(s["consts_ready"], 1)
            pe.wait_ge(s["kv_in"], 32)

            def weights():
                pe.wait_ge(s["mod_acc"], KB)
                pe.wait_ge(s["z_read"], UNITS)
                pe.wait_ge(s["abs_done"], UNITS)
                for n in range(2):
                    pe.matmul(Z[n][:], ones[:], acc[:, n * 512:(n + 1) * 512], start=True, stop=True)\
                      .then_inc(s["mod_summed"], 1)
                pe.wait_ge(s["row_done"], 1)
                pe.wait_ge(s["w_lo"], NY)
                pe.wait_ge(s["kv_rest"], 32)

            def scores(nb, k, diagonal, pair):
                g = k % 2
                wait("z_read", UNITS * (nb - 1) + k + 1 if not is0(nb) else 0)
                wait("abs_done", UNITS * (nb - 1) + k + 1 if not is0(nb) else 0)
                for b in range(2):
                    h = 2 * b + g
                    keys = k_c[:, bass.ds(2 * pair + (1 - k // 2), 1), h * T:(h + 1) * T].rearrange("p o t -> p (o t)")
                    for v in range(2):
                        ins = pe.matmul(Z[k][:, b * T2:(b + 1) * T2], keys, side_q[0][:, v, h, :],
                                        start=(v == 0), stop=(v == 1))
                ins.then_inc(s["z_done"], 1)

            def sums(nb, k, diagonal, pair):
                g = k % 2
                pe.wait_ge(s["lo_done"], UNITS * nb + k + 1)
                start = diagonal and k < 2
                if not start:
                    pk = (k - 2) % UNITS
                    pe.wait_ge(s["arg_done"], UNITS * nb + k - 1)
                    pe.matmul(C[g][:], unt[:], hi[pk][:], start=False, stop=False, skip_group_check=True)
                    pe.matmul(C[g][:], unt[:], lo[pk][:], start=False, stop=False, skip_group_check=True)
                else:
                    wait("arg_done", UNITS * nb)
                pe.matmul(C[g][:], tri[:], hi[k][:], start=start, stop=False, skip_group_check=True)
                pe.matmul(C[g][:], tri[:], lo[k][:], start=False, stop=True, skip_group_check=True)\
                  .then_inc(s["cs_done"], 1)

            def values(nb, k, diagonal, pair):
                g = k % 2
                pe.wait_ge(s["a_done"], UNITS * nb + k + 1)
                for b in range(2):
                    h = 2 * b + g
                    v_h = v_c[:, bass.ds(2 * pair + (1 - k // 2), 1), h * SD:(h + 1) * SD].rearrange("p o e -> p (o e)")
                    for tt in range(2):
                        at = tt * SW + h * SD
                        ins = pe.matmul(O[:, at:at + SD], zs[k][:, b * T2 + tt * T:b * T2 + (tt + 1) * T], v_h,
                                        start=False, stop=True, skip_group_check=True)
                ins.then_inc(s["av_done"], 1)

            side_q = [None]
            stages = [(scores, 0), (values, 4), (sums, 2)]

            def one_pass(I, n, nb, side, inner, end, last):
                side_q[0] = q_sb[side]
                pe.wait_ge(q_in[side], 80 * n + 160 - 80 * side)
                if not is0(n):
                    turn_o(n - 1)
                run_units(pe, stages, I, nb, inner, lambda k: between(n, side, k))
                drain_units(stages, end)

            def between(n, side, step):
                if not is0(n):
                    y_products(n - 1, 1 - side, step)
                if step == UNITS - 1:
                    pe.matmul(O[:], zero[:], nothing[:], start=True, stop=True, skip_group_check=True)

            def turn_o(n):
                pe.wait_ge(s["o_read"], n + 1)
                for b in range(2):
                    for tt in range(2):
                        ins = pe.transpose(O[:, b * T2 + tt * T:b * T2 + (tt + 1) * T],
                                           o_sb[:, tt * SW + b * P:tt * SW + (b + 1) * P], ident[:])
                ins.then_inc(s["o_turned"], 1)

            def y_products(n, side, step):
                k = step // 2
                if step % 2 == 0:
                    wait("y_read", 4 * n + k)
                tt, h = k // 2, k % 2
                ts = slice(tt * T, (tt + 1) * T)
                cs = slice(h * 512, (h + 1) * 512)
                for b in range(0, 5) if step % 2 == 0 else range(5, NY):
                    if b == MH + AW // P:
                        pe.wait_ge(s["ys_lo_done"], n + 1)
                    r = Y_BLOCKS[b]
                    if b < MH:
                        y_hi, y_lo = (ym_sb[side][0:MD, tt, v, b, :] for v in range(2))
                    elif b < MH + AW // P:
                        y_hi, y_lo = (ya_sb[side][:, tt, v, b - MH, :] for v in range(2))
                    else:
                        y_hi, y_lo = (v[:, b - MH - AW // P, ts] for v in (ys_hi, ys_lo))
                    pe.matmul(M[:], y_hi, wo_hi[0:r, b, cs], start=(b == 0), stop=False)
                    pe.matmul(M[:], y_hi, wo_lo[0:r, b, cs], start=False, stop=False)
                    ins = pe.matmul(M[:], y_lo, wo_hi[0:r, b, cs], start=False, stop=(b == NY - 1))
                if step % 2:
                    ins.then_inc(s["y_done"], 1)

            all_passes(pe, one_pass, weights)
            turn_o(NP2 - 1)
            for step in range(2 * UNITS):
                y_products(NP2 - 1, 1, step)


def build(nc, a, out):
    def dram(name, shape, dt=F32):
        return nc.dram_tensor(name, shape, dt, kind="Internal").ap()

    x1 = dram("x1", [S, D])
    ym_d, ya_d = dram("ym_d", [NT * MD, 2 * MH * T], BF16), dram("ya_d", [NT * P, 2 * AG * T], BF16)
    sq_d, sk_d = dram("sq_d", [NT * SD, 2 * SH * T], BF16), dram("sk_d", [NT * P, SH * T], BF16)
    sv_d, sz_d = dram("sv_d", [S, SW]), dram("sz_d", [S, SW])
    gla_phase(nc, a["x"], a["c_cols"], a["ada_w"], a["ada_b"], a["ada_b_cols"], a["norm_g_cols"], a["gla_w_in"],
              a["gla_w_alpha"], a["gla_b_alpha_cols"], a["gla_norm_g"], a["gla_w_out"], a["final_g"], x1)
    mix_phase(nc, x1, a["c_2_cols"], a["w_mod_2"], a["b_mod_2_cols"], a["g_pre_2_cols"], a["w_in_2"],
              a["m_conv_w_2_cols"], a["m_conv_b_2_cols"], a["m_wq_2"][0].rearrange("h d e -> d h e"),
              a["m_wk_2"][0].rearrange("h d e -> d h e"), a["m_b_i_2_cols"], a["m_b_f_2_cols"], a["m_norm_g_2_cols"],
              a["m_skip_2_cols"], a["a_sinks_2"][0], ym_d, ya_d, sq_d, sk_d, sv_d, sz_d)
    stick_phase(nc, x1, a["c_2_cols"], a["w_mod_2"], a["b_mod_2"], a["g_post_2"], a["w_out_2"][0], ym_d, ya_d, sq_d, sk_d,
                sv_d, sz_d, out[0])


_INS = ['x', 'ada_w', 'ada_b', 'gla_w_in', 'gla_w_alpha', 'gla_norm_g', 'gla_w_out', 'final_g',
        'w_mod_2', 'b_mod_2', 'g_post_2', 'm_wq_2', 'm_wk_2', 'a_sinks_2', 'w_out_2']
_COLS = [('c', 0, D, P), ('ada_b', 0, 2 * D, P), ('norm_g', 0, D, P), ('gla_b_alpha', 0, GH * GDK, P),
         ('c_2', 0, D, P), ('b_mod_2', 0, 2 * D, P), ('g_pre_2', 0, D, P), ('m_conv_w_2', 0, TAPS * MW, MD),
         ('m_conv_b_2', 0, MW, MD), ('m_norm_g_2', 0, MW, MD), ('m_skip_2', 0, MW, MD), ('m_b_i_2', 0, MH, MH),
         ('m_b_f_2', 0, MH, MH)]
_OUTS = [((1, S, D), 'float32')]


def _w_in_2_columns():
    import numpy as _np
    order = [("u", MW), ("mv", MW), ("i", MH), ("f", MH), ("mz", MW), ("aq", AW), ("ak", AKV * AD), ("av", AKV * AD),
             ("az", AW), ("sq", SW), ("sk", SW), ("sv", SW), ("sz", SW)]
    at, lies = 0, {}
    for n, w in order:
        lies[n] = _np.arange(at, at + w)
        at += w
    lies["aq"] = lies["aq"].reshape(AKV, AG, AD).transpose(1, 0, 2).reshape(-1)
    return _np.concatenate([lies[n] for n, _ in PARTS])


def kernel(**inputs):
    import numpy as _np
    import concourse.bacc as _bacc
    from concourse import mybir as _mybir
    from concourse.bass_utils import run_bass_kernel_spmd as _run

    nc = _bacc.Bacc("TRN2", target_bir_lowering=False, num_devices=1)
    arrays, args = {}, {}

    def give(name, a):
        a = _np.ascontiguousarray(a)
        arrays[f"in_{name}_dram"] = a
        args[name] = nc.dram_tensor(f"in_{name}_dram", a.shape, _mybir.dt.from_np(a.dtype), kind="ExternalInput").ap()

    for name in _INS:
        give(name, inputs[name])
    for name, lo, hi, width in _COLS:
        give(name + "_cols", _np.asarray(inputs[name]).reshape(-1)[lo:hi].reshape(-1, width).T)
    give("w_in_2", _np.asarray(inputs["w_in_2"])[0][:, _w_in_2_columns()])
    outs = nc.dram_tensor("out_0_dram", _OUTS[0][0], F32, kind="ExternalOutput").ap()
    build(nc, args, outs)
    r = _run(nc, [arrays], core_ids=[0])
    return r.results[0]["out_0_dram"]
```
